# Optimizing a Trainium2 kernel written in Bass

```python
import math
import jax, jax.numpy as jnp
from jax import lax
import numpy as np

D_MODEL = 1024
BATCH = 1
SEQ = 256
DEPTH = 2

GRID_W = 64
CTX_LEN = 256
BLOCK = 128
ROPE_BASE = 10000.0
EPS = 1e-6
NEG_INF = -1e30

DA_HEADS = 4
DA_DIM = 32
DA_VDIM = 2 * DA_DIM
HY_WIDTH = 256
HY_SHORT = 3
HY_BANDS = 16
HY_EMB = 1 + 2 * HY_BANDS
HY_FF = 64
HY_SHIFT = 0.05
HY_FAST_DECAY = 0.3
HY_SLOW_DECAY = 1.5
HY_TARGET = 1e-2
WA_HEADS = 4
WA_KV_HEADS = 2
WA_GROUP = WA_HEADS // WA_KV_HEADS
WA_DIM = 64
WINDOW = 128
CF_WIDTH = 256
CF_TAPS = 31
N_BRANCH = 4
BRANCH_W = 256
N_GROUPS = 4
EXP_PER_GROUP = 4
N_EXPERTS = N_GROUPS * EXP_PER_GROUP
TOP_K = 2
D_EXPERT = 512
MOE_BLOCK = 256

OFF_A = 0
W_A = 4 * DA_HEADS * DA_DIM + DA_HEADS * DA_VDIM
OFF_B = OFF_A + W_A
W_B = 3 * HY_WIDTH
OFF_C = OFF_B + W_B
W_C = (WA_HEADS + 2 * WA_KV_HEADS) * WA_DIM
OFF_D = OFF_C + W_C
W_D = 2 * CF_WIDTH
OFF_G = OFF_D + W_D
D_IN = OFF_G + N_BRANCH * D_MODEL

kernel_name = 'hybrid_diffusion_trunk'

def rms_norm(x, g):
    xf = x.astype(jnp.float32)
    y = xf * lax.rsqrt(jnp.mean(xf * xf, axis=-1, keepdims=True) + EPS)
    return (y * g.astype(jnp.float32)).astype(x.dtype)

def layer_norm(x, g, b):
    xf = x.astype(jnp.float32)
    xc = xf - jnp.mean(xf, axis=-1, keepdims=True)
    y = xc * lax.rsqrt(jnp.mean(xc * xc, axis=-1, keepdims=True) + EPS)
    return (y * g.astype(jnp.float32) + b.astype(jnp.float32)).astype(x.dtype)

def modulate(x, g, shift, scale):
    return rms_norm(x, g) * (1.0 + scale) + shift

def heads(z, off, n, d):
    return z[..., off:off + n * d].reshape(z.shape[:-1] + (n, d))

def grid_rope(x):
    L, d = x.shape[1], x.shape[-1]
    rows = L // GRID_W
    row = jnp.repeat(jnp.arange(rows, dtype=jnp.float32), GRID_W)
    col = jnp.tile(jnp.arange(GRID_W, dtype=jnp.float32), rows)
    qd = d // 4
    inv = ROPE_BASE ** (-jnp.arange(qd, dtype=jnp.float32) / qd)

    def rot(xa, pos):
        ang = pos[:, None] * inv[None, :]
        cos = jnp.cos(ang)[None, :, None, :]
        sin = jnp.sin(ang)[None, :, None, :]
        x1 = xa[..., :qd].astype(jnp.float32)
        x2 = xa[..., qd:].astype(jnp.float32)
        return jnp.concatenate([x1 * cos - x2 * sin, x2 * cos + x1 * sin], axis=-1)

    out = jnp.concatenate([rot(x[..., :d // 2], row), rot(x[..., d // 2:], col)], axis=-1)
    return out.astype(x.dtype)

def dw_conv(x, w, b):
    taps, ch = w.shape
    y = lax.conv_general_dilated(x, w.astype(x.dtype)[:, None, :], window_strides=(1,),
                                 padding=[(taps // 2, taps // 2)],
                                 dimension_numbers=('NWC', 'WIO', 'NWC'), feature_group_count=ch)
    return y + b.astype(x.dtype)

def da_queries(z, g):
    w = DA_HEADS * DA_DIM
    q1 = rms_norm(heads(z, OFF_A, DA_HEADS, DA_DIM), g)
    q2 = rms_norm(heads(z, OFF_A + w, DA_HEADS, DA_DIM), g)
    return q1, q2

def da_keys_values(z, g):
    w = DA_HEADS * DA_DIM
    k1 = rms_norm(heads(z, OFF_A + 2 * w, DA_HEADS, DA_DIM), g)
    k2 = rms_norm(heads(z, OFF_A + 3 * w, DA_HEADS, DA_DIM), g)
    v = heads(z, OFF_A + 4 * w, DA_HEADS, DA_VDIM)
    return k1, k2, v

def diff_attend(q1, q2, k1, k2, v, lam):
    scale = DA_DIM ** -0.5
    s1 = jnp.einsum('bhqd,bhkd->bhqk', q1, k1).astype(jnp.float32) * scale
    s2 = jnp.einsum('bhqd,bhkd->bhqk', q2, k2).astype(jnp.float32) * scale
    p = jax.nn.softmax(s1, axis=-1) - lam * jax.nn.softmax(s2, axis=-1)
    return jnp.einsum('bhqk,bhkd->bhqd', p.astype(v.dtype), v)

def hyena_filter(L, w1, b1, w2, b2, w3, b3, w4, freq):
    f32 = jnp.float32
    t = jnp.linspace(0.0, 1.0, L, dtype=f32)[:, None]
    w = (2.0 * math.pi / L) * jnp.arange(L, dtype=f32)[:, None]
    bands = jnp.linspace(1e-4, HY_BANDS - 1, HY_BANDS, dtype=f32)[None, :]
    feat = jnp.concatenate([t, jnp.cos(w * bands), jnp.sin(w * bands)], axis=-1)
    fr = freq.astype(f32)
    a = jnp.sin(fr * (feat @ w1.astype(f32) + b1.astype(f32)))
    a = jnp.sin(fr * (a @ w2.astype(f32) + b2.astype(f32)))
    a = jnp.sin(fr * (a @ w3.astype(f32) + b3.astype(f32)))
    coef = a @ w4.astype(f32)
    deltas = jnp.abs(jnp.linspace(math.log(HY_TARGET) / HY_FAST_DECAY,
                                  math.log(HY_TARGET) / HY_SLOW_DECAY, HY_WIDTH, dtype=f32))
    window = jnp.exp(-t * deltas[None, :]) + HY_SHIFT
    hf = coef[:, :HY_WIDTH] * window
    hb = coef[:, HY_WIDTH:] * window
    filt = jnp.concatenate([hf, jnp.zeros((1, HY_WIDTH), f32), hb[:0:-1]], axis=0)
    return filt * lax.rsqrt(jnp.sum(filt * filt, axis=0, keepdims=True) + EPS)

def fft_long_conv(u, filt, bias):
    L = u.shape[1]
    uf = u.astype(jnp.float32)
    spec = jnp.fft.rfft(uf, n=2 * L, axis=1) * jnp.fft.rfft(filt, axis=0)[None]
    y = jnp.fft.irfft(spec, n=2 * L, axis=1)[:, :L]
    return (y + uf * bias.astype(jnp.float32)).astype(u.dtype)

def hyena(zb, conv_w, conv_b, filt, bias):
    u = dw_conv(zb, conv_w, conv_b)
    x0, x1, v = jnp.split(u, 3, axis=-1)
    return x0 * fft_long_conv(v * x1, filt, bias)

def wa_queries(z, g):
    return rms_norm(heads(z, OFF_C, WA_HEADS, WA_DIM), g)

def wa_keys_values(z, g):
    k = rms_norm(heads(z, OFF_C + WA_HEADS * WA_DIM, WA_KV_HEADS, WA_DIM), g)
    v = heads(z, OFF_C + (WA_HEADS + WA_KV_HEADS) * WA_DIM, WA_KV_HEADS, WA_DIM)
    return k, v

def window_gqa_latent(q, k, v, kc, vc, sink):
    B, S = q.shape[:2]
    nb = S // BLOCK
    qb = q.reshape(B, nb, BLOCK, WA_KV_HEADS, WA_GROUP, WA_DIM)

    def band(a):
        ap = jnp.pad(a, ((0, 0), (BLOCK, BLOCK), (0, 0), (0, 0))).reshape(B, nb + 2, BLOCK, WA_KV_HEADS, WA_DIM)
        return jnp.concatenate([ap[:, :-2], ap[:, 1:-1], ap[:, 2:]], axis=2)

    kw, vw = band(k), band(v)
    blk = jnp.arange(nb)[:, None, None]
    qpos = blk * BLOCK + jnp.arange(BLOCK)[None, :, None]
    kpos = (blk - 1) * BLOCK + jnp.arange(3 * BLOCK)[None, None, :]
    valid = (jnp.abs(qpos - kpos) <= WINDOW) & (kpos >= 0) & (kpos < S)
    scale = WA_DIM ** -0.5
    sw = jnp.einsum('bnqhgd,bnkhd->bnhgqk', qb, kw).astype(jnp.float32) * scale
    sw = jnp.where(valid[None, :, None, None], sw, NEG_INF)
    sc = jnp.einsum('bnqhgd,bchd->bnhgqc', qb, kc).astype(jnp.float32) * scale
    snk = jnp.broadcast_to(sink.astype(jnp.float32).reshape(WA_KV_HEADS, WA_GROUP)[None, None, :, :, None, None],
                           sw.shape[:-1] + (1,))
    p = jax.nn.softmax(jnp.concatenate([sw, sc, snk], axis=-1), axis=-1)
    nw = 3 * BLOCK
    nc = kc.shape[1]
    o = (jnp.einsum('bnhgqk,bnkhd->bnqhgd', p[..., :nw].astype(v.dtype), vw)
         + jnp.einsum('bnhgqc,bchd->bnqhgd', p[..., nw:nw + nc].astype(v.dtype), vc))
    return o.reshape(B, S, WA_HEADS * WA_DIM)

def sink_attention_ctx(qc, kc, vc, sink):
    B, C = qc.shape[:2]
    qg = qc.reshape(B, C, WA_KV_HEADS, WA_GROUP, WA_DIM)
    s = jnp.einsum('bqhgd,bkhd->bhgqk', qg, kc).astype(jnp.float32) * (WA_DIM ** -0.5)
    snk = jnp.broadcast_to(sink.astype(jnp.float32).reshape(WA_KV_HEADS, WA_GROUP)[None, :, :, None, None],
                           s.shape[:-1] + (1,))
    p = jax.nn.softmax(jnp.concatenate([s, snk], axis=-1), axis=-1)[..., :C]
    o = jnp.einsum('bhgqk,bkhd->bqhgd', p.astype(vc.dtype), vc)
    return o.reshape(B, C, WA_HEADS * WA_DIM)

def conformer_conv(zd, dw_w, dw_b, ln_g, ln_b):
    a, b = jnp.split(zd, 2, axis=-1)
    u = dw_conv(a * jax.nn.sigmoid(b), dw_w, dw_b)
    return jax.nn.silu(layer_norm(u, ln_g, ln_b))

def token_mixers(h, hc, layer, need_ctx, p):
    B, S, _ = h.shape
    z = h @ p['w_in']
    zc = hc @ p['w_in']
    tr = lambda a: a.transpose(0, 2, 1, 3)
    hf = (p['hf_w1'], p['hf_b1'], p['hf_w2'], p['hf_b2'], p['hf_w3'], p['hf_b3'], p['hf_w4'], p['hf_freq'])

    lam_init = 0.8 - 0.6 * math.exp(-0.3 * layer)
    lv = p['da_lam'].astype(jnp.float32)
    lam = jnp.exp(jnp.sum(lv[0] * lv[1])) - jnp.exp(jnp.sum(lv[2] * lv[3])) + lam_init
    q1, q2 = da_queries(z, p['da_qn'])
    k1, k2, v = da_keys_values(z, p['da_kn'])
    q1, q2, k1, k2 = grid_rope(q1), grid_rope(q2), grid_rope(k1), grid_rope(k2)
    k1c, k2c, vc = da_keys_values(zc, p['da_kn'])
    kk1 = tr(jnp.concatenate([k1, k1c], axis=1))
    kk2 = tr(jnp.concatenate([k2, k2c], axis=1))
    vv = tr(jnp.concatenate([v, vc], axis=1))
    nb = S // BLOCK
    to_blocks = lambda q: q.reshape(B, nb, BLOCK, DA_HEADS, DA_DIM).transpose(1, 0, 3, 2, 4)
    ob = lax.map(lambda qs: diff_attend(qs[0], qs[1], kk1, kk2, vv, lam), (to_blocks(q1), to_blocks(q2)))
    ya = ob.transpose(1, 0, 3, 2, 4).reshape(B, S, DA_HEADS, DA_VDIM)
    ya = (rms_norm(ya, p['da_subln']) * (1.0 - lam_init)).reshape(B, S, BRANCH_W)

    yb = hyena(z[..., OFF_B:OFF_B + W_B], p['hy_conv_w'], p['hy_conv_b'], hyena_filter(S, *hf), p['hy_bias'])

    qw = grid_rope(wa_queries(z, p['wa_qn']))
    kw, vw = wa_keys_values(z, p['wa_kn'])
    kw = grid_rope(kw)
    kwc, vwc = wa_keys_values(zc, p['wa_kn'])
    yc_ = window_gqa_latent(qw, kw, vw, kwc, vwc, p['wa_sink'])

    yd = conformer_conv(z[..., OFF_D:OFF_D + W_D], p['cf_dw_w'], p['cf_dw_b'], p['cf_ln_g'], p['cf_ln_b'])

    def merge(t, ys):
        acc = 0.0
        for bi, yi in enumerate(ys):
            g = jax.nn.sigmoid(t[..., OFF_G + bi * D_MODEL:OFF_G + (bi + 1) * D_MODEL]
                               + p['b_gate'][bi * D_MODEL:(bi + 1) * D_MODEL])
            acc = acc + g * (yi @ p['w_branch'][bi])
        return acc @ p['w_out']

    y = merge(z, (ya, yb, yc_, yd))
    if not need_ctx:
        return y, None

    C = hc.shape[1]
    q1c, q2c = da_queries(zc, p['da_qn'])
    yca = tr(diff_attend(tr(q1c), tr(q2c), tr(k1c), tr(k2c), tr(vc), lam))
    yca = (rms_norm(yca, p['da_subln']) * (1.0 - lam_init)).reshape(B, C, BRANCH_W)
    ycb = hyena(zc[..., OFF_B:OFF_B + W_B], p['hy_conv_w'], p['hy_conv_b'], hyena_filter(C, *hf), p['hy_bias'])
    ycc = sink_attention_ctx(wa_queries(zc, p['wa_qn']), kwc, vwc, p['wa_sink'])
    ycd = conformer_conv(zc[..., OFF_D:OFF_D + W_D], p['cf_dw_w'], p['cf_dw_b'], p['cf_ln_g'], p['cf_ln_b'])
    yc = merge(zc, (yca, ycb, ycc, ycd))
    return y, yc

def hier_moe(h, w_rg, b_rg, w_re, b_re, w1, w3, w2):
    shp = h.shape
    t = h.reshape(-1, D_MODEL)
    T = t.shape[0]
    lg = (t @ w_rg).astype(jnp.float32) + b_rg.astype(jnp.float32)
    pg = jax.nn.softmax(lg, axis=-1)
    gi = jnp.argmax(lg, axis=-1)
    gw = jnp.take_along_axis(pg, gi[:, None], axis=-1)
    le = ((t @ w_re).astype(jnp.float32) + b_re.astype(jnp.float32)).reshape(T, N_GROUPS, EXP_PER_GROUP)
    le = jnp.take_along_axis(le, gi[:, None, None], axis=1)[:, 0]
    top_p, top_i = lax.top_k(jax.nn.softmax(le, axis=-1), TOP_K)
    top_p = top_p / jnp.sum(top_p, axis=-1, keepdims=True) * gw
    e_a = (gi[:, None] * EXP_PER_GROUP + top_i).reshape(-1)
    w_a = top_p.reshape(-1)
    A = T * TOP_K
    tok_a = jnp.arange(A) // TOP_K
    order = jnp.argsort(e_a)
    e_s, tok_s, w_s = e_a[order], tok_a[order], w_a[order]
    counts = jnp.bincount(e_a, length=N_EXPERTS)
    padded = ((counts + MOE_BLOCK - 1) // MOE_BLOCK) * MOE_BLOCK
    pad_end = jnp.cumsum(padded)
    pad_start = pad_end - padded
    seg_start = jnp.cumsum(counts) - counts
    dest = pad_start[e_s] + jnp.arange(A) - seg_start[e_s]
    P = (-(-A // MOE_BLOCK)) * MOE_BLOCK + N_EXPERTS * MOE_BLOCK
    n_blk = P // MOE_BLOCK
    buf_tok = jnp.zeros((P,), jnp.int32).at[dest].set(tok_s.astype(jnp.int32))
    buf_w = jnp.zeros((P,), jnp.float32).at[dest].set(w_s)
    blk_exp = jnp.minimum(jnp.searchsorted(pad_end, jnp.arange(n_blk) * MOE_BLOCK, side='right'), N_EXPERTS - 1)
    xb = t[buf_tok].reshape(n_blk, MOE_BLOCK, D_MODEL)

    def expert_block(args):
        xblk, e = args
        u = jax.nn.silu(xblk @ w1[e]) * (xblk @ w3[e])
        return u @ w2[e]

    yb = lax.map(expert_block, (xb, blk_exp)).reshape(P, D_MODEL)
    y = jax.ops.segment_sum(yb.astype(jnp.float32) * buf_w[:, None], buf_tok, num_segments=T)
    return y.astype(h.dtype).reshape(shp)

def setup_inputs(seed: int = 0) -> dict:
    key = jax.random.key(seed)
    ks = iter(jax.random.split(key, 48))
    f32 = jnp.float32
    D = D_MODEL

    def nrm(shape, scale=1.0):
        return jax.random.normal(next(ks), shape, f32) * scale

    def gain(shape):
        return 1.0 + nrm(shape, 0.02)

    return {
        'x': nrm((BATCH, SEQ, D)),
        'c': nrm((BATCH, D)),
        'ctx': nrm((BATCH, CTX_LEN, D)),
        'c_ctx': nrm((D,)),
        'w_mod': nrm((DEPTH, D, 6 * D), 0.5 * D ** -0.5),
        'b_mod': nrm((DEPTH, 6 * D), 0.02),
        'norm1_g': gain((DEPTH, D)),
        'norm2_g': gain((DEPTH, D)),
        'w_in': nrm((DEPTH, D, D_IN), D ** -0.5),
        'b_gate': nrm((DEPTH, N_BRANCH * D), 0.02),
        'da_qn': gain((DEPTH, DA_DIM)),
        'da_kn': gain((DEPTH, DA_DIM)),
        'da_lam': nrm((DEPTH, 4, DA_DIM), 0.1),
        'da_subln': gain((DEPTH, DA_VDIM)),
        'hy_conv_w': nrm((DEPTH, HY_SHORT, W_B), HY_SHORT ** -0.5),
        'hy_conv_b': nrm((DEPTH, W_B), 0.02),
        'hf_w1': nrm((DEPTH, HY_EMB, HY_FF), HY_EMB ** -0.5),
        'hf_b1': nrm((DEPTH, HY_FF), 0.02),
        'hf_w2': nrm((DEPTH, HY_FF, HY_FF), HY_FF ** -0.5),
        'hf_b2': nrm((DEPTH, HY_FF), 0.02),
        'hf_w3': nrm((DEPTH, HY_FF, HY_FF), HY_FF ** -0.5),
        'hf_b3': nrm((DEPTH, HY_FF), 0.02),
        'hf_w4': nrm((DEPTH, HY_FF, 2 * HY_WIDTH), HY_FF ** -0.5),
        'hf_freq': gain((DEPTH, HY_FF)),
        'hy_bias': nrm((DEPTH, HY_WIDTH)),
        'wa_qn': gain((DEPTH, WA_DIM)),
        'wa_kn': gain((DEPTH, WA_DIM)),
        'wa_sink': nrm((DEPTH, WA_HEADS), 0.5),
        'cf_dw_w': nrm((DEPTH, CF_TAPS, CF_WIDTH), CF_TAPS ** -0.5),
        'cf_dw_b': nrm((DEPTH, CF_WIDTH), 0.02),
        'cf_ln_g': gain((DEPTH, CF_WIDTH)),
        'cf_ln_b': nrm((DEPTH, CF_WIDTH), 0.02),
        'w_branch': nrm((DEPTH, N_BRANCH, BRANCH_W, D), BRANCH_W ** -0.5),
        'w_out': nrm((DEPTH, D, D), D ** -0.5),
        'w_rg': nrm((DEPTH, D, N_GROUPS), D ** -0.5),
        'b_rg': nrm((DEPTH, N_GROUPS), 0.01),
        'w_re': nrm((DEPTH, D, N_EXPERTS), D ** -0.5),
        'b_re': nrm((DEPTH, N_EXPERTS), 0.01),
        'w1': nrm((DEPTH, N_EXPERTS, D, D_EXPERT), D ** -0.5),
        'w3': nrm((DEPTH, N_EXPERTS, D, D_EXPERT), D ** -0.5),
        'w2': nrm((DEPTH, N_EXPERTS, D_EXPERT, D), D_EXPERT ** -0.5),
    }

def reference(x, c, ctx, c_ctx, w_mod, b_mod, norm1_g, norm2_g, w_in, b_gate, da_qn, da_kn, da_lam,
              da_subln, hy_conv_w, hy_conv_b, hf_w1, hf_b1, hf_w2, hf_b2, hf_w3, hf_b3, hf_w4, hf_freq,
              hy_bias, wa_qn, wa_kn, wa_sink, cf_dw_w, cf_dw_b, cf_ln_g, cf_ln_b, w_branch, w_out,
              w_rg, b_rg, w_re, b_re, w1, w3, w2):
    xc = ctx
    sc = jax.nn.silu(c)
    scc = jax.nn.silu(c_ctx)
    for l in range(DEPTH):
        last = l == DEPTH - 1
        mod = (sc @ w_mod[l] + b_mod[l])[:, None, :]
        modc = scc @ w_mod[l] + b_mod[l]
        sh1, s1, g1, sh2, s2, g2 = jnp.split(mod, 6, axis=-1)
        csh1, cs1, cg1, csh2, cs2, cg2 = jnp.split(modc, 6, axis=-1)
        p = dict(w_in=w_in[l], b_gate=b_gate[l], da_qn=da_qn[l], da_kn=da_kn[l], da_lam=da_lam[l],
                 da_subln=da_subln[l], hy_conv_w=hy_conv_w[l], hy_conv_b=hy_conv_b[l],
                 hf_w1=hf_w1[l], hf_b1=hf_b1[l], hf_w2=hf_w2[l], hf_b2=hf_b2[l], hf_w3=hf_w3[l],
                 hf_b3=hf_b3[l], hf_w4=hf_w4[l], hf_freq=hf_freq[l], hy_bias=hy_bias[l],
                 wa_qn=wa_qn[l], wa_kn=wa_kn[l], wa_sink=wa_sink[l], cf_dw_w=cf_dw_w[l],
                 cf_dw_b=cf_dw_b[l], cf_ln_g=cf_ln_g[l], cf_ln_b=cf_ln_b[l], w_branch=w_branch[l],
                 w_out=w_out[l])
        h = modulate(x, norm1_g[l], sh1, s1)
        hc = modulate(xc, norm1_g[l], csh1, cs1)
        y, yc = token_mixers(h, hc, l, not last, p)
        x = x + g1 * y
        if not last:
            xc = xc + cg1 * yc
            hc2 = modulate(xc, norm2_g[l], csh2, cs2)
            xc = xc + cg2 * hier_moe(hc2, w_rg[l], b_rg[l], w_re[l], b_re[l], w1[l], w3[l], w2[l])
        h2 = modulate(x, norm2_g[l], sh2, s2)
        x = x + g2 * hier_moe(h2, w_rg[l], b_rg[l], w_re[l], b_re[l], w1[l], w3[l], w2[l])
    return x


_drawn_inputs = setup_inputs


def setup_inputs(seed=0):
    import zlib

    import numpy as np

    out = dict(_drawn_inputs(seed))
    spreads = {}
    factors = {'norm1_g': 3.382,
     'norm2_g': 4.383,
     'b_gate': 8.0,
     'da_qn': 8.0,
     'da_kn': 8.0,
     'da_subln': 64.0,
     'hy_conv_b': 3.358,
     'hf_b1': 5.008,
     'hf_b2': 5.026,
     'hf_b3': 3.504,
     'hf_freq': 6.358,
     'wa_qn': 21.672,
     'wa_kn': 23.69,
     'wa_sink': 8.0,
     'cf_dw_b': 7.158,
     'cf_ln_g': 37.892,
     'cf_ln_b': 33.665,
     'b_rg': 8.0,
     'b_re': 25.574}
    for name, (base, spread) in spreads.items():
        noise = np.random.default_rng([zlib.crc32(name.encode()), seed]).standard_normal(out[name].shape)
        drawn = base * np.exp(spread * noise) if base else spread * noise
        out[name] = __import__('jax').numpy.asarray(drawn.astype(out[name].dtype))
    for name, factor in factors.items():
        out[name] = (out[name] * factor).astype(out[name].dtype)
    return out
```

```python
import math
from contextlib import ExitStack

import concourse.bass as bass
from concourse import mybir
import numpy as np

ALU = mybir.AluOpType
ACT = mybir.ActivationFunctionType
AX = mybir.AxisListType
F32 = mybir.dt.float32
I32 = mybir.dt.int32

P = 128
D = 1024
KD = D // P
DEPTH = 2
SEQ = 256
TILES = 4
EPS = 1e-6
NEG = -1e30
NE = 16
FE = 512
BRANCHES = (3, 1, 0, 2)
TAPS = 31
PAD = TAPS // 2
BANKS = 8
RING = 3
WCH = 4096

C_N1, C_N2, C_BMOD, C_BGATE = 0, 8, 16, 64
C_HYW, C_HYB, C_HYBIAS = 96, 114, 120
C_CFW, C_CFB, C_LNG, C_LNB = 122, 184, 186, 188
C_HF = 190
NC = 194
R_QN, R_KN, R_WQ, R_WK, R_SUB, R_BR, R_SINK, R_LAM = 0, 32, 64, 128, 192, 256, 276, 280
NR = 408
HF_COLS = 64 * 3 + 512
TWO_PI = 2.0 * math.pi
PI_HI = 6.28125
PI_LO = TWO_PI - PI_HI
MAGIC = 1.5 * 2.0 ** 23
SIN_MAX = 3.1415925


def constants():
    f = np.float64
    L, N = SEQ, 2 * SEQ
    t = np.arange(L, dtype=f)
    k = np.arange(L, dtype=f)
    ang = 2 * np.pi / N * np.outer(t, k)
    alt = (-1.0) ** t
    sin = np.sin(ang)
    sin_nyq = sin.copy()
    sin_nyq[:, 0] = alt
    dft = np.concatenate([np.cos(ang), sin_nyq], 1)
    cos_nyq = np.cos(ang)
    cos_nyq[:, 0] = alt
    sin_zero = sin.copy()
    sin_zero[:, 0] = 0
    ahead = np.concatenate([np.cos(ang), sin_zero, cos_nyq], 1)
    behind = np.concatenate([np.cos(ang), -sin_zero, cos_nyq], 1)
    behind[0, :] = 0
    fdft = np.concatenate([ahead, behind], 0)
    wc = np.full((L, 1), 2.0 / N)
    wc[0] = 1.0 / N
    inv_c = wc * np.cos(ang.T)
    inv_s = 2.0 / N * sin.T
    inv_s[0] = alt / N
    idft = np.concatenate([inv_c, inv_s], 0)
    tl = np.linspace(0.0, 1.0, L, dtype=np.float32)[:, None]
    w = ((2.0 * math.pi / L) * np.arange(L, dtype=np.float32)[:, None]).astype(np.float32)
    bands = np.linspace(1e-4, 15, 16, dtype=np.float32)[None]
    wb = (w * bands).astype(np.float32).astype(f)
    feat = np.concatenate([tl, np.cos(wb), np.sin(wb)], 1)
    featT = np.zeros((P, L))
    featT[:33] = feat.T
    deltas = np.abs(np.linspace(math.log(1e-2) / 0.3, math.log(1e-2) / 1.5, 256, dtype=np.float32))
    win = np.exp(-tl.astype(f) * deltas[None].astype(f)) + 0.05
    win2 = np.concatenate([win, win], 1)
    win2[0, 256:] = 0

    def tiles(a):
        return a.reshape(-1, P, a.shape[1]).transpose(1, 0, 2).reshape(P, -1)

    def rope(d):
        qd = d // 4
        inv = 10000.0 ** (-np.arange(qd, dtype=f) / qd)
        row, col = np.arange(SEQ) // 64, np.arange(SEQ) % 64
        c, s = [], []
        for pos in (row, col):
            a = pos[:, None] * inv[None]
            c += [np.cos(a), np.cos(a)]
            s += [-np.sin(a), np.sin(a)]
        return tiles(np.concatenate(c, 1)), tiles(np.concatenate(s, 1))

    i = np.arange(P)
    mask = np.zeros((P, 2, P))
    mask[:, 0, :] = np.where(i[None] <= i[:, None], 0, NEG)
    mask[:, 1, :] = np.where(i[None] >= i[:, None], 0, NEG)
    sel = np.zeros((P, 2, P))
    for v in range(2):
        sel[np.arange(4) * 32 + v, v, :] = 1
    ca, sa = rope(32)
    cc, sc = rope(64)
    rank = np.tile(np.arange(4, 0, -1.0), (P, 1))
    parts = dict(ident=np.eye(P), mean=np.full((P, P), 1 / 256), dft=tiles(dft), idft=tiles(idft),
                 win=tiles(win2), mask=mask.reshape(P, -1), sel=sel.reshape(P, -1), feat=featT,
                 cosa=ca, sina=sa, cosc=cc, sinc=sc, rank=rank)
    at, off = {}, 0
    for n, a in parts.items():
        at[n] = (off, a.shape[1])
        off += a.shape[1]
    return np.concatenate(list(parts.values()), 1).astype(np.float32), tiles(fdft).astype(np.float32), at


CONST_AT = constants()[2]
NCONST = sum(n for _, n in CONST_AT.values())


def live(l):
    return TILES if l < DEPTH - 1 else 2


def merge(main, side):
    out, n = [], 0
    for i, g in enumerate(main):
        out += g
        upto = (i + 1) * len(side) // len(main)
        for s in side[n:upto]:
            out += s
        n = upto
    return out


def mod_steps(l, chunks):
    out = []
    for c in chunks:
        out += [("T", ("mod", l, c)), ("S", ("modrow", l, c))]
        if c // 2 in (2, 5):
            for v in range(live(l) // 2):
                out += [("T", ("modB", l, c, v)), ("V", ("modgate", l, c, v))]
        else:
            out += [("T", ("modT", l, c)), ("V", ("modcol", l, c))]
    return out


def norm_steps(l, n, tiles):
    out = [("V", ("modfin", l, n))]
    out += [("S", ("sq", l, n, t)) for t in range(tiles)]
    out += [("V", ("rstd", l, n))]
    out += [("S" if t % 2 else "V", ("xn", l, n, t)) for t in range(tiles)]
    for k in range(KD):
        out += [("T", ("hT", l, n, k)), ("V" if k % 2 else "S", ("hTout", l, n, k))]
    return out


def layer_order(l):
    tt = live(l)
    o = [("V", ("pads", l)), ("S", ("lamexp", l)), ("V", ("lam", l))]
    o += mod_steps(l, range(4))
    o += norm_steps(l, 1, TILES)
    for j in (2, 3, 0, 1):
        o += [("T", ("zD", l, j)), ("S" if j >= 2 else "V", ("zDout", l, j))]
    for j in range(6):
        o += [("T", ("zB", l, j)), ("S", ("zBout", l, j)), ("V", ("hyconv", l, j))]
    o += [("V", ("vx", l))]
    for j in range(2):
        o += [("V", ("cfconv", l, j))]
    filt = []
    for n in (1, 2, 3):
        filt += [[("T", ("hf", l, n)), ("V", ("hfarg", l, n)), ("S", ("hfsin", l, n))]]
    for i in range(2):
        filt += [[("T", ("hf4", l, i)), ("V", ("hfwin", l, i)), ("S", ("hfsq", l, i))]]
    filt += [[("T", ("fnorm", l)), ("V", ("fnorms", l))]]
    for m in range(6):
        filt += [[("T", ("fdft", l, m)), ("S", ("fdftout", l, m))]]
    for g in filt:
        o += g
    o += [("T", ("lnmean", l)), ("V", ("xc", l))]
    o += [("S", ("xcsq", l)), ("T", ("lnvar", l)), ("V", ("lnv", l)), ("S", ("lntanh", l)), ("V", ("lnout", l))]
    hy = []
    for i in range(2):
        hy += [[("T", ("vxT", l, i)), ("S", ("vxTout", l, i))]]
    for f in range(4):
        hy += [[("T", ("dft", l, f)), ("S", ("dftout", l, f))]]
    hy[-1] += [("V", ("spec", l))]
    for c in range(2):
        hy += [[("T", ("idft", l, c)), ("V", ("hyout", l, c))]]

    def gate_groups(bi, first):
        out = []
        for j in range(KD):
            out += [[("T", ("gate", l, bi, j)), ("S", ("gtanh", l, bi, j))],
                    [("T", ("br", l, bi, j)), ("V", ("gmul", l, bi, j))]
                    + ([] if first else [("P", ("gadd", l, bi, j))])]
        return out

    o += merge(gate_groups(3, True), hy)
    for t in range(TILES):
        if t < tt:
            o += [("T", ("zAq", l, t)), ("S", ("zAqout", l, t))]
        o += [("T", ("zAk", l, t)), ("S", ("zAkout", l, t)), ("P", ("sqA", l, t)), ("V", ("ssA", l, t))]
    for t in range(TILES):
        o += [("T", ("zC", l, t)), ("S", ("zCout", l, t)), ("P", ("sqC", l, t)), ("V", ("ssC", l, t))]
    prep = []
    o += [("V", ("rsA", l)), ("V", ("rsC", l))]
    for b in "AC":
        for t in range(TILES):
            o += [("V", ("rope" + b, l, t))]
            prep += [[("T", ("qkT" + b, l, t)), ("S", ("qkTout" + b, l, t))]]

    def attention(b):
        units = [(t, h) for t in range(tt) for h in range(4)]
        groups = []
        for i in range(len(units) + 1):
            if i < len(units):
                t, h = units[i]
                ts = [("T", ("s" + b, l, t, h, n)) for n in range(2 if b == "A" else 1)]
                groups += [ts + [("V", ("mx" + b, l, t, h)), ("S", ("ex" + b, l, t, h))]]
            if i:
                t, h = units[i - 1]
                groups[-1] += [("V", ("p" + b, l, t, h))]
                groups += [[("T", ("pT" + b, l, t, h)), ("S", ("pTout" + b, l, t, h))]]
                if h == 3:
                    groups += [[("T", ("y" + b, l, t)), ("V", ("yn" + b, l, t))],
                               [("T", ("yT" + b, l, t)), ("S", ("yTout" + b, l, t))]]
        return groups

    o += merge(gate_groups(1, False), prep + attention("A"))
    o += merge(gate_groups(0, False), attention("C"))
    for g in gate_groups(2, False):
        o += g
    o += mod_steps(l, (4, 5))
    for hf in range(2):
        for t in range(tt):
            o += [("T", ("wo", l, t, hf)), ("V", ("xup", l, t, hf))]
    o += mod_steps(l, (6, 7, 8, 9, 10, 11))
    o += norm_steps(l, 2, tt)
    for t in range(tt):
        o += [("T", ("lg", l, t)), ("V", ("lgout", l, t))]
    o += [("V", ("route1", l)), ("S", ("rexp1", l)), ("V", ("route2", l)), ("S", ("rexp2", l)), ("V", ("route3", l))]
    for e in range(NE):
        for f in range(4):
            o += [("T", ("e1", l, e, f)), ("S", ("etanh", l, e, f)), ("T", ("e3", l, e, f)), ("V", ("eu", l, e, f))]
        for t in range(tt):
            for hf in range(2):
                o += [("T", ("e2", l, e, t, hf)), ("V", ("eacc", l, e, t, hf))]
    for t in range(tt):
        o += [("V", ("xup2", l, t))]
    return o


def chunk_order(l):
    tt = live(l)
    mods = [(("wmod", l, c), ("mod", l, c)) for c in range(12)]
    out = mods[:4]
    out += [(("win", l, 0), ("zD", l, 1)), (("win", l, 1), ("zB", l, 3)), (("win", l, 2), ("zB", l, 5)),
            (("fdft", l), ("fdft", l, 5))]

    def gates(bi):
        return [(("wbr", l, bi), ("br", l, bi, 7)), (("win", l, 6 + 2 * bi), ("gate", l, bi, 3)),
                (("win", l, 7 + 2 * bi), ("gate", l, bi, 7))]
    out += gates(3)
    out += [(("win", l, 3), ("zAq", l, tt - 1)), (("win", l, 4), ("zAk", l, 3)), (("win", l, 5), ("zC", l, 3))]
    out += gates(1) + gates(0) + gates(2)
    out += mods[4:6]
    out += [(("wout", l, hf), ("wo", l, tt - 1, hf)) for hf in range(2)]
    out += mods[6:]
    for e in range(NE):
        out += [(("w1", l, e), ("e1", l, e, 3)), (("w3", l, e), ("e3", l, e, 3)), (("w2", l, e), ("e2", l, e, tt - 1, 1))]
    return out


ORDER = [("S", ("silu", 0))] + [s for l in range(DEPTH) for s in layer_order(l)]
STEPS = {e: [n for x, n in ORDER if x == e] for e in "TVSP"}
COUNT = {e: {n: i + 1 for i, n in enumerate(STEPS[e])} for e in "TVSP"}
CHUNKS = [c for l in range(DEPTH) for c in chunk_order(l)]
CHUNK_AT = {name: i for i, (name, _) in enumerate(CHUNKS)}


def readers(name):
    kind, l, rest = name[0], name[1], name[2:]
    one = {"mod": ("S", "modrow"), "modT": ("V", "modcol"), "modB": ("V", "modgate"),
           "zB": ("S", "zBout"), "hf": ("V", "hfarg"), "hf4": ("V", "hfwin"), "fnorm": ("V", "fnorms"),
           "fdft": ("S", "fdftout"), "lnmean": ("V", "xc"), "lnvar": ("V", "lnv"), "vxT": ("S", "vxTout"),
           "dft": ("S", "dftout"), "idft": ("V", "hyout"), "gate": ("S", "gtanh"), "br": ("V", "gmul"),
           "zAq": ("S", "zAqout"), "zAk": ("S", "zAkout"), "zC": ("S", "zCout"),
           "qkTA": ("S", "qkToutA"), "qkTC": ("S", "qkToutC"), "pTA": ("S", "pToutA"), "pTC": ("S", "pToutC"),
           "yA": ("V", "ynA"), "yC": ("V", "ynC"), "yTA": ("S", "yToutA"), "yTC": ("S", "yToutC"),
           "wo": ("V", "xup"), "lg": ("V", "lgout"), "e3": ("V", "eu"), "e2": ("V", "eacc")}
    if kind in one:
        e, k = one[kind]
        return [(e, (k, l, *rest))]
    if kind == "hT":
        return [("V" if rest[1] % 2 else "S", ("hTout", l, *rest))]
    if kind == "zD":
        return [("S" if rest[0] >= 2 else "V", ("zDout", l, *rest))]
    if kind in ("sA", "sC"):
        return [("S", ("ex" + kind[1], l, *rest[:2]))]
    if kind == "e1":
        return [("V", ("eu", l, *rest))]
    raise KeyError(kind)


def bank_of(name):
    return (COUNT["T"][name] - 1) % BANKS


def check_order():
    at = {s: i for i, s in enumerate(ORDER)}
    for i in range(BANKS, len(STEPS["T"])):
        for s in readers(STEPS["T"][i - BANKS]):
            assert at[s] < at[("T", STEPS["T"][i])], (STEPS["T"][i], s)
    for i in range(RING, len(CHUNKS)):
        assert COUNT["T"][CHUNKS[i - RING][1]] < COUNT["T"][CHUNKS[i][1]], CHUNKS[i]


check_order()


def build_trunk(nc, xin, ccol, const, cols, rows, hfw, wr, bgate_rows, fdft, wmod, win, wbr, wout, w1, w3, w2, out):
    with ExitStack() as ctx:
        def sb(name, shape, dt=F32):
            return ctx.enter_context(nc.sbuf_tensor(name, shape, dt))

        def sem(name):
            return ctx.enter_context(nc.semaphore(name))

        x = sb("x", [P, TILES, D])
        hT = sb("hT", [P, KD, 512])
        con = sb("con", [P, NCONST])
        col = sb("col", [P, DEPTH, NC])
        row = sb("row", [P, NR * DEPTH])
        hw = sb("hw", [64, HF_COLS])
        wrt = sb("wrt", [P, DEPTH, KD, 20])
        bgr = sb("bgr", [8, 512])
        cc = sb("cc", [P, KD * 32])
        ct = sb("ct", [P, KD * 32])
        ring = sb("ring", [P, RING, WCH])
        wide = sb("wide", [P, 4 * D])
        yT = sb("yT", [P, 2, 2, 512])
        gth = sb("gth", [P, 2, 512])
        gtmp = sb("gtmp", [P, 2, 512])
        mr = sb("mr", [P, 2, 512])
        mod = sb("mod", [P, 4, KD, 2])
        modt = sb("modt", [P, 4, 2])
        amp = sb("amp", [P, KD, 2])
        hbg = sb("hbg", [P, 32])
        ss = sb("ss", [P, 4])
        small = sb("small", [P, 3, 64])
        lamt = sb("lamt", [P, 72])
        nlam = sb("nlam", [P, 4])
        mx = sb("mx", [P, 2, 2])
        nm = sb("nm", [P, 2, 2])
        sums = sb("sums", [P, 2, 2])
        esk = sb("esk", [P, 2])
        rr = sb("rr", [P, 2])
        den = sb("den", [P, 4])
        rden = sb("rden", [P, 4])
        fn = sb("fn", [P, 2])
        ssa = sb("ssa", [P, TILES, 16])
        ssc = sb("ssc", [P, TILES, 6])
        rsa = sb("rsa", [P, TILES, 16])
        rsc = sb("rsc", [P, TILES, 6])
        m = sb("m", [P, 9736])
        n_ = sb("n_", [P, 5240])

        def part(t, at, *shape):
            size = int(np.prod(shape))
            ap = t[:, at:at + size]
            if len(shape) == 2:
                return ap.rearrange("p (a b) -> p a b", a=shape[0])
            if len(shape) == 3:
                return ap.rearrange("p (a b c) -> p a b c", a=shape[0], b=shape[1])
            return ap
        zb = part(m, 0, 2, 2, 258)
        hu = part(m, 1032, 6, 2, 256)
        us = part(m, 4104, 4, 512)
        fs = part(m, 6152, 6, 256)
        ysp = part(m, 7688, 4, 512)
        hfarg = part(m, 7688, 256)
        hfk = part(m, 7944, 256)
        hfa = part(m, 8200, 2, 256)
        hf2 = part(m, 8712, 2, 512)
        hf = part(m, 4104, 2, 512)
        ut = part(m, 2056, 2, 512)
        za = part(m, 0, TILES, 768)
        zc = part(m, 3072, TILES, 512)
        qkta = part(m, 5120, 4, 512)
        qktc = part(m, 7168, 3, 512)
        sq = part(m, 8704, 2, 512)
        rt = part(n_, 0, 2, 512)
        gbc = part(m, 0, 2, D)
        u = part(m, 2048, 4, 512)
        eth = part(m, 4096, 2, 512)
        es = part(m, 5120, 512)
        lg = part(m, 5632, TILES, 20)
        rw = part(m, 5760, TILES, 16)
        rtmp = part(m, 5824, 12, 16)
        rt16 = part(m, 6016, TILES, 16)
        ud = part(n_, 0, 2, 2, 286)
        cv = part(n_, 1144, 2, 512)
        thd = part(n_, 2168, 2, 512)
        sqd = part(n_, 3192, 2, 512)
        rsd = part(n_, 4216, 2, 512)
        ee = part(n_, 0, 2, 2, 512)
        pt = part(n_, 2048, 4, 512)
        yn = part(n_, 4096, 256)
        ynq = part(n_, 4352, 256)

        xn = wide[:, :].rearrange("p (t d) -> p t d", t=4)
        acc = wide[:, :].rearrange("p (k n) -> p k n", k=KD)
        ps = ctx.enter_context(nc.psum_tensor("ps", [P, BANKS, 512], F32))

        def c(name, cols_=None):
            at, n = CONST_AT[name]
            return con[:, at:at + n]
        ident = c("ident")
        dft_c = c("dft").rearrange("p (a b) -> p a b", a=2)
        idft_c = c("idft").rearrange("p (a b) -> p a b", a=4)
        win_c = c("win").rearrange("p (a b) -> p a b", a=2)
        mask_c = c("mask").rearrange("p (a b) -> p a b", a=2)
        sel_c = c("sel").rearrange("p (a b) -> p a b", a=2)

        def rowp(l, at, n):
            return row[:, l * NR + at:l * NR + at + n]

        def streams(l):
            return live(l) // 2

        def bank(name):
            return ps[:, bank_of(name), :]

        tensor_done, vector_done, scalar_done, pool_done = (
            sem("tensor_done"), sem("vector_done"), sem("scalar_done"), sem("pool_done"))
        vector_chain = sem("vector_chain")
        params_landed = sem("params_landed")
        x_landed = sem("x_landed")
        hfw_landed = sem("hfw_landed")
        const_landed = sem("const_landed")
        chunk_landed = [sem(f"chunk_landed{i}") for i in range(RING)]
        out_stored = sem("out_stored")
        done_of = {"T": tensor_done, "V": vector_done, "S": scalar_done, "P": pool_done}
        N_PARAMS = 6

        def tensor(*name):
            return COUNT["T"][name]

        def vector(*name):
            return COUNT["V"][name]

        def scalar(*name):
            return COUNT["S"][name]

        def pool(*name):
            return COUNT["P"][name]

        def chunk(name):
            return ring[:, CHUNK_AT[name] % RING, :]

        def chunk3(name, n=KD):
            return chunk(name).rearrange("p (k n) -> p k n", k=n)

        block = ctx.enter_context(nc.Block())

        @block.sync
        def _(sp):
            source = {"wmod": wmod, "win": win, "wbr": wbr, "wout": wout, "w1": w1, "w3": w3, "w2": w2}
            sp.dma_start(cc[:], ccol).then_inc(params_landed, 16)
            for t_, a in ((col[:], cols), (row[:], rows), (wrt[:], wr), (bgr[:], bgate_rows)):
                sp.dma_start(t_, a).then_inc(params_landed, 16)
            sp.dma_start(con[:], const).then_inc(const_landed, 16)
            sp.dma_start(hw[:], hfw[0]).then_inc(hfw_landed, 16)
            sp.dma_start(x[:], xin).then_inc(x_landed, 16)
            for i, (name, _) in enumerate(CHUNKS):
                if i >= RING:
                    sp.wait_ge(tensor_done, tensor(*CHUNKS[i - RING][1]))
                src = fdft if name[0] == "fdft" else source[name[0]][name[1], name[2]]
                width = src.shape[1]
                if name[0] == "win" and name[2] in (2, 3):
                    width = WCH // 2
                sp.dma_start(ring[:, i % RING, 0:width], src[:, 0:width]).then_inc(chunk_landed[i % RING], 16)
                if name == ("wmod", 1, 0):
                    sp.wait_ge(tensor_done, tensor("hf4", 0, 1))
                    sp.dma_start(hw[:], hfw[1]).then_inc(hfw_landed, 16)
            for t in range(2):
                sp.wait_ge(vector_done, vector("xup2", DEPTH - 1, t))
                sp.dma_start(out[t * P:(t + 1) * P, :], x[:, t, :]).then_inc(out_stored, 16)
            sp.wait_ge(out_stored, 32)

        @block.tensor
        def _(pe):
            seen = set()

            def use(name):
                if name not in seen:
                    seen.add(name)
                    i = CHUNK_AT[name]
                    pe.wait_ge(chunk_landed[i % RING], 16 * (i // RING + 1))

            pe.wait_ge(const_landed, 16)
            pe.wait_ge(params_landed, 16 * 5)
            for n, name in enumerate(STEPS["T"]):
                kind, l, rest = name[0], name[1], name[2:]
                W = 128 * live(l)
                b = ps[:, n % BANKS, :]
                if n >= BANKS:
                    for e, r in readers(STEPS["T"][n - BANKS]):
                        pe.wait_ge(done_of[e], COUNT[e][r])
                if kind == "mod":
                    (ch,) = rest
                    use(("wmod", l, ch))
                    if n == 0:
                        pe.wait_ge(vector_done, COUNT["V"][("pads", 0)])
                    w = chunk3(("wmod", l, ch))
                    for k in range(KD):
                        g = 32 * (k % 4)
                        last = pe.matmul(b[g:g + 32, :], cc[:, 32 * k:32 * k + 32], w[:, k, :],
                                         start=(k < 4), stop=(k >= 4), skip_group_check=True)
                    last.then_inc(tensor_done, 1)
                elif kind == "modT":
                    pe.wait_ge(scalar_done, scalar("modrow", l, *rest))
                    for j in range(4):
                        last = pe.transpose(b[:, j * P:(j + 1) * P], mr[:, rest[0] % 2, j * P:(j + 1) * P], ident)
                    last.then_inc(tensor_done, 1)
                elif kind == "modB":
                    ch, v = rest
                    pe.wait_ge(scalar_done, scalar("modrow", l, ch))
                    r = l * 4 + (ch // 6) * 2 + ch % 2
                    pe.matmul(b, sel_c[:, v, :], mr[:, ch % 2, :], start=True, stop=False)
                    last = pe.matmul(b, ident[0:8, r:r + 1].broadcast_to([8, P]), bgr[0:8, :], start=False, stop=True)
                    last.then_inc(tensor_done, 1)
                elif kind == "hT":
                    nn, k = rest
                    T = TILES if nn == 1 else live(l)
                    for t in range(T):
                        if t % 2:
                            pe.wait_ge(scalar_done, scalar("xn", l, nn, t))
                        else:
                            pe.wait_ge(vector_done, vector("xn", l, nn, t))
                    for t in range(T):
                        last = pe.transpose(b[:, t * P:(t + 1) * P], xn[:, t, k * P:(k + 1) * P], ident)
                    last.then_inc(tensor_done, 1)
                elif kind in ("zD", "zB", "gate"):
                    if kind == "gate":
                        bi, j = rest
                        cn = ("win", l, 6 + 2 * bi + j // 4)
                        jj = j % 4
                    elif kind == "zD":
                        cn, jj = ("win", l, 0), rest[0]
                    else:
                        cn, jj = ("win", l, 1 + rest[0] // 4), rest[0] % 4
                    use(cn)
                    cols_ = 256 if cn[2] == 2 else 512
                    w = chunk(cn)[:, 0:KD * cols_].rearrange("p (k n) -> p k n", k=KD)
                    pe.wait_ge(scalar_done, scalar("hTout", l, 1, KD - 2))
                    pe.wait_ge(vector_done, vector("hTout", l, 1, KD - 1))
                    for k in range(KD):
                        last = pe.matmul(b[:, 0:W], w[:, k, jj * P:(jj + 1) * P], hT[:, k, 0:W],
                                         start=(k == 0), stop=(k == KD - 1))
                    last.then_inc(tensor_done, 1)
                elif kind in ("zAq", "zAk", "zC"):
                    (t,) = rest
                    cn = ("win", l, {"zAq": 3, "zAk": 4, "zC": 5}[kind])
                    use(cn)
                    wid = 256 if kind == "zAq" or (kind == "zC" and t >= live(l)) else 512
                    w = chunk(cn)[:, 0:KD * (256 if kind == "zAq" else 512)].rearrange("p (k n) -> p k n", k=KD)
                    for k in range(KD):
                        last = pe.matmul(b[:, 0:wid], hT[:, k, t * P:(t + 1) * P], w[:, k, 0:wid],
                                         start=(k == 0), stop=(k == KD - 1))
                    last.then_inc(tensor_done, 1)
                elif kind == "hf":
                    (i,) = rest
                    pe.wait_ge(hfw_landed, 16 * (l + 1))
                    if i == 1:
                        last = pe.matmul(b[0:64, 0:256], hw[0:33, 0:64], c("feat")[0:33, :], start=True, stop=True)
                    else:
                        pe.wait_ge(scalar_done, scalar("hfsin", l, i - 1))
                        last = pe.matmul(b[0:64, 0:256], hw[0:64, 64 * (i - 1):64 * i], hfa[0:64, (i - 1) % 2, :],
                                         start=True, stop=True)
                    last.then_inc(tensor_done, 1)
                elif kind == "hf4":
                    pe.wait_ge(scalar_done, scalar("hfsin", l, 3))
                    last = pe.matmul(b, hfa[0:64, 1, rest[0] * P:(rest[0] + 1) * P], hw[0:64, 192:704],
                                     start=True, stop=True)
                    last.then_inc(tensor_done, 1)
                elif kind == "fnorm":
                    pe.wait_ge(scalar_done, scalar("hfsq", l, 1))
                    for cch in range(2):
                        for i in range(2):
                            for side in range(2):
                                at = side * 256 + cch * P
                                last = pe.matmul(b[:, cch:cch + 1], hf2[:, i, at:at + P], c("mean")[:, 0:1],
                                                 start=(i + side == 0), stop=(i + side == 2))
                    last.then_inc(tensor_done, 1)
                elif kind == "fdft":
                    (j,) = rest
                    use(("fdft", l))
                    pe.wait_ge(vector_done, vector("hfwin", l, 1))
                    fd = chunk(("fdft", l))
                    for side in range(2):
                        for i in range(2):
                            at = (side * 2 + i) * 768 + j * P
                            last = pe.matmul(b[:, 0:256], fd[:, at:at + P], hf[:, i, side * 256:(side + 1) * 256],
                                             start=(side + i == 0), stop=(side + i == 2))
                    last.then_inc(tensor_done, 1)
                elif kind in ("lnmean", "lnvar"):
                    if kind == "lnmean":
                        pe.wait_ge(vector_done, vector("cfconv", l, 1))
                        src = cv
                    else:
                        pe.wait_ge(scalar_done, scalar("xcsq", l))
                        src = sqd
                    for j in range(2):
                        last = pe.matmul(b[:, 0:W], c("mean"), src[:, j, 0:W], start=(j == 0), stop=(j == 1))
                    last.then_inc(tensor_done, 1)
                elif kind == "vxT":
                    (i,) = rest
                    pe.wait_ge(vector_done, vector("vx", l))
                    for s in range(streams(l)):
                        for cch in range(2):
                            at = s * 256 + cch * P
                            last = pe.transpose(b[:, at:at + P], hu[:, 4 + cch, s, i * P:(i + 1) * P], ident)
                    last.then_inc(tensor_done, 1)
                elif kind == "dft":
                    (f,) = rest
                    pe.wait_ge(scalar_done, scalar("vxTout", l, 1))
                    for i in range(2):
                        last = pe.matmul(b[:, 0:W], dft_c[:, i, f * P:(f + 1) * P], ut[:, i, 0:W],
                                         start=(i == 0), stop=(i == 1))
                    last.then_inc(tensor_done, 1)
                elif kind == "idft":
                    (cch,) = rest
                    pe.wait_ge(vector_done, vector("spec", l))
                    for s in range(streams(l)):
                        for f in range(4):
                            at = s * 256 + cch * P
                            last = pe.matmul(b[:, s * 256:(s + 1) * 256], ysp[:, f, at:at + P], idft_c[:, f, :],
                                             start=(f == 0), stop=(f == 3))
                    last.then_inc(tensor_done, 1)
                elif kind == "br":
                    bi, j = rest
                    use(("wbr", l, bi))
                    if bi == 3:
                        pe.wait_ge(vector_done, vector("lnout", l))
                    elif bi == 1:
                        pe.wait_ge(vector_done, vector("hyout", l, 1))
                    else:
                        pe.wait_ge(scalar_done, scalar("yTout" + ("A" if bi == 0 else "C"), l, live(l) - 1))
                    w = chunk(("wbr", l, bi))[:, 0:2 * D].rearrange("p (k n) -> p k n", k=2)
                    for k in range(2):
                        last = pe.matmul(b[:, 0:W], w[:, k, j * P:(j + 1) * P], yT[:, bi in (1, 2), k, 0:W],
                                         start=(k == 0), stop=(k == 1))
                    last.then_inc(tensor_done, 1)
                elif kind == "qkTA":
                    (t,) = rest
                    pe.wait_ge(vector_done, vector("ropeA", l, t))
                    for j in range(0 if t < live(l) else 2, 4):
                        last = pe.transpose(b[:, j * P:(j + 1) * P], za[:, t, j * P:(j + 1) * P], ident)
                    last.then_inc(tensor_done, 1)
                elif kind == "qkTC":
                    (t,) = rest
                    pe.wait_ge(vector_done, vector("ropeC", l, t))
                    for j in range(3 if t < live(l) else 1):
                        at = 0 if j == 0 else 256 + (j - 1) * P
                        last = pe.transpose(b[:, j * P:(j + 1) * P], zc[:, t, at:at + P], ident)
                    last.then_inc(tensor_done, 1)
                elif kind == "sA":
                    t, h, i = rest
                    pe.wait_ge(scalar_done, scalar("qkToutA", l, TILES - 1))
                    k0 = 0 if t < 2 else 256
                    r = slice(32 * h, 32 * h + 32)
                    last = pe.matmul(b[:, 0:512 - k0], qkta[r, i, t * P:(t + 1) * P], qkta[r, 2 + i, k0:512],
                                     start=True, stop=True)
                    last.then_inc(tensor_done, 1)
                elif kind == "sC":
                    t, h, _ = rest
                    pe.wait_ge(scalar_done, scalar("qkToutC", l, TILES - 1))
                    k0 = 0 if t < 2 else 256
                    r = slice(64 * (h // 2), 64 * (h // 2) + 64)
                    last = pe.matmul(b[:, 0:512 - k0], qktc[r, 1 + h % 2, t * P:(t + 1) * P], qktc[r, 0, k0:512],
                                     start=True, stop=True)
                    last.then_inc(tensor_done, 1)
                elif kind in ("pTA", "pTC"):
                    t, h = rest
                    if kind == "pTA":
                        pe.wait_ge(vector_done, vector("pA", l, t, h))
                    else:
                        pe.wait_ge(scalar_done, scalar("exC", l, t, h))
                    for k in range(4 if t < 2 else 2):
                        last = pe.transpose(b[:, k * P:(k + 1) * P], ee[:, (t * 4 + h) % 2, 0, k * P:(k + 1) * P], ident)
                    last.then_inc(tensor_done, 1)
                elif kind in ("yA", "yC"):
                    (t,) = rest
                    pe.wait_ge(scalar_done, scalar("pTout" + kind[1], l, t, 3))
                    k0, nk = (0, 4) if t < 2 else (2, 2)
                    for h in range(4):
                        for k in range(nk):
                            v = (za[:, k0 + k, 512 + h * 64:576 + h * 64] if kind == "yA"
                                 else zc[:, k0 + k, 128 + (h // 2) * 64:192 + (h // 2) * 64])
                            last = pe.matmul(b[:, h * 64:(h + 1) * 64], pt[:, h, k * P:(k + 1) * P], v,
                                             start=(k == 0), stop=(k == nk - 1))
                    last.then_inc(tensor_done, 1)
                elif kind in ("yTA", "yTC"):
                    (t,) = rest
                    pe.wait_ge(vector_done, vector("yn" + kind[2], l, t))
                    for j in range(2):
                        last = pe.transpose(b[:, j * P:(j + 1) * P], yn[:, j * P:(j + 1) * P], ident)
                    last.then_inc(tensor_done, 1)
                elif kind == "wo":
                    t, half = rest
                    use(("wout", l, half))
                    pe.wait_ge(pool_done, pool("gadd", l, 2, KD - 1))
                    w = chunk3(("wout", l, half))
                    for k in range(KD):
                        last = pe.matmul(b, acc[:, k, t * P:(t + 1) * P], w[:, k, :], start=(k == 0), stop=(k == KD - 1))
                    last.then_inc(tensor_done, 1)
                elif kind == "lg":
                    (t,) = rest
                    pe.wait_ge(scalar_done, scalar("hTout", l, 2, KD - 2))
                    pe.wait_ge(vector_done, vector("hTout", l, 2, KD - 1))
                    for k in range(KD):
                        last = pe.matmul(b[:, 0:20], hT[:, k, t * P:(t + 1) * P], wrt[:, l, k, :],
                                         start=(k == 0), stop=(k == KD - 1))
                    last.then_inc(tensor_done, 1)
                elif kind in ("e1", "e3"):
                    e, f = rest
                    cn = ("w1" if kind == "e1" else "w3", l, e)
                    use(cn)
                    w = chunk3(cn)
                    for k in range(KD):
                        last = pe.matmul(b[:, 0:W], w[:, k, f * P:(f + 1) * P], hT[:, k, 0:W],
                                         start=(k == 0), stop=(k == KD - 1))
                    last.then_inc(tensor_done, 1)
                elif kind == "e2":
                    e, t, half = rest
                    use(("w2", l, e))
                    pe.wait_ge(vector_done, vector("eu", l, e, 3))
                    w = chunk3(("w2", l, e), 4)
                    for f in range(4):
                        last = pe.matmul(b, u[:, f, t * P:(t + 1) * P], w[:, f, half * 512:(half + 1) * 512],
                                         start=(f == 0), stop=(f == 3))
                    last.then_inc(tensor_done, 1)
                else:
                    raise KeyError(kind)

        @block.scalar
        def _(act):
            act.wait_ge(params_landed, 16 * 5)
            for n, name in enumerate(STEPS["S"]):
                kind, l, rest = name[0], name[1], name[2:]
                W = 128 * live(l)
                if n:
                    act.wait_ge(scalar_done, n)
                if kind == "silu":
                    last = act.activation(ct[:], cc[:], ACT.Tanh, scale=0.5)
                    last.then_inc(scalar_done, 1)
                elif kind == "lamexp":
                    act.wait_ge(vector_done, vector("pads", l))
                    last = act.activation(lamt[:, 66:68], lamt[:, 64:66], ACT.Exp)
                    last.then_inc(scalar_done, 1)
                elif kind == "modrow":
                    act.wait_ge(tensor_done, tensor("mod", l, *rest))
                    last = act.activation(mr[:, rest[0] % 2, :], bank(("mod", l, *rest)), ACT.Copy)
                    last.then_inc(scalar_done, 1)
                elif kind == "sq":
                    nn, t = rest
                    if nn == 2:
                        act.wait_ge(tensor_done, tensor("wo", l, live(l) - 1, 1))
                        act.wait_ge(vector_done, vector("xup", l, t, 1))
                    elif l:
                        act.wait_ge(vector_done, vector("xup2", l - 1, live(l - 1) - 1))
                    else:
                        act.wait_ge(x_landed, 16)
                    last = act.activation(xn[:, t, :], x[:, t, :], ACT.Square, accum_out=ss[:, t:t + 1])
                    last.then_inc(scalar_done, 1)
                elif kind == "xn":
                    nn, t = rest
                    act.wait_ge(vector_done, vector("rstd", l, nn))
                    last = act.activation(xn[:, t, :], x[:, t, :], ACT.Copy, scale=small[:, 0, t:t + 1])
                    last.then_inc(scalar_done, 1)
                elif kind == "hTout":
                    nn, k = rest
                    act.wait_ge(tensor_done, tensor("hT", l, *rest))
                    act.wait_ge(vector_done, vector("modfin", l, nn))
                    for s in range(2 if nn == 1 else streams(l)):
                        h = slice(256 * s, 256 * s + 256)
                        last = act.activation(hT[:, k, h], bank(("hT", l, *rest))[:, h], ACT.Identity,
                                              bias=mod[:, 2 * nn - 2, k, s:s + 1], scale=amp[:, k, s:s + 1])
                    last.then_inc(scalar_done, 1)
                elif kind == "zDout":
                    (j,) = rest
                    act.wait_ge(tensor_done, tensor("zD", l, j))
                    last = act.activation(thd[:, j - 2, 0:W], bank(("zD", l, j))[:, 0:W], ACT.Tanh, scale=0.5)
                    last.then_inc(scalar_done, 1)
                elif kind == "zBout":
                    (j,) = rest
                    act.wait_ge(tensor_done, tensor("zB", l, j))
                    act.wait_ge(vector_done, vector(*(("hyconv", l, j - 2) if j >= 2 else ("pads", l))))
                    last = act.activation(zb[:, j % 2, 0:streams(l), 1:257],
                                          bank(("zB", l, j))[:, 0:W].rearrange("p (s n) -> p s n", s=streams(l)),
                                          ACT.Copy)
                    last.then_inc(scalar_done, 1)
                elif kind == "hfsin":
                    (i,) = rest
                    act.wait_ge(vector_done, vector("hfarg", l, i))
                    last = act.activation(hfa[0:64, i % 2, :], hfarg[0:64, :], ACT.Sin)
                    last.then_inc(scalar_done, 1)
                elif kind == "hfsq":
                    (i,) = rest
                    act.wait_ge(vector_done, vector("hfwin", l, i))
                    last = act.activation(hf2[:, i, :], hf[:, i, :], ACT.Square)
                    last.then_inc(scalar_done, 1)
                elif kind == "fdftout":
                    (j,) = rest
                    act.wait_ge(tensor_done, tensor("fdft", l, j))
                    last = act.activation(fs[:, j, :], bank(("fdft", l, j))[:, 0:256], ACT.Copy)
                    last.then_inc(scalar_done, 1)
                elif kind == "xcsq":
                    act.wait_ge(vector_done, vector("xc", l))
                    last = act.activation(sqd[:, :, 0:W], cv[:, :, 0:W], ACT.Square)
                    last.then_inc(scalar_done, 1)
                elif kind == "lntanh":
                    act.wait_ge(vector_done, vector("lnv", l))
                    last = act.activation(thd[:, :, 0:W], cv[:, :, 0:W], ACT.Tanh, scale=0.5)
                    last.then_inc(scalar_done, 1)
                elif kind == "vxTout":
                    (i,) = rest
                    act.wait_ge(tensor_done, tensor("vxT", l, i))
                    last = act.activation(ut[:, i, 0:W], bank(("vxT", l, i))[:, 0:W], ACT.Copy)
                    last.then_inc(scalar_done, 1)
                elif kind == "dftout":
                    (f,) = rest
                    act.wait_ge(tensor_done, tensor("dft", l, f))
                    last = act.activation(us[:, f, 0:W], bank(("dft", l, f))[:, 0:W], ACT.Copy)
                    last.then_inc(scalar_done, 1)
                elif kind == "gtanh":
                    bi, j = rest
                    act.wait_ge(tensor_done, tensor("gate", l, bi, j))
                    i = COUNT["V"][("gmul", l, bi, j)]
                    g = [s for s in STEPS["V"] if s[0] == "gmul"].index(("gmul", l, bi, j))
                    if g >= 2:
                        act.wait_ge(vector_done, vector(*[s for s in STEPS["V"] if s[0] == "gmul"][g - 2]))
                    last = act.activation(gth[:, g % 2, 0:W], bank(("gate", l, bi, j))[:, 0:W], ACT.Tanh,
                                          bias=hbg[:, bi * 8 + j:bi * 8 + j + 1], scale=0.5)
                    last.then_inc(scalar_done, 1)
                elif kind in ("zAqout", "zAkout", "zCout"):
                    (t,) = rest
                    act.wait_ge(vector_done, vector("hyout", l, 1))
                    act.wait_ge(tensor_done, tensor(kind[:-3], l, t))
                    b = bank((kind[:-3], l, t))
                    if kind == "zAqout":
                        last = act.activation(za[:, t, 0:256], b[:, 0:256], ACT.Copy)
                    elif kind == "zAkout":
                        last = act.activation(za[:, t, 256:768], b, ACT.Copy)
                    else:
                        wid = 512 if t < live(l) else 256
                        last = act.activation(zc[:, t, 0:wid], b[:, 0:wid], ACT.Copy)
                    last.then_inc(scalar_done, 1)
                elif kind == "qkToutA":
                    (t,) = rest
                    act.wait_ge(tensor_done, tensor("qkTA", l, t))
                    j0 = 0 if t < live(l) else 2
                    last = act.activation(qkta[:, j0:4, t * P:(t + 1) * P],
                                          bank(("qkTA", l, t))[:, j0 * P:512].rearrange("p (j n) -> p j n", n=P), ACT.Copy)
                    last.then_inc(scalar_done, 1)
                elif kind == "qkToutC":
                    (t,) = rest
                    act.wait_ge(tensor_done, tensor("qkTC", l, t))
                    nj = 3 if t < live(l) else 1
                    last = act.activation(qktc[:, 0:nj, t * P:(t + 1) * P],
                                          bank(("qkTC", l, t))[:, 0:nj * P].rearrange("p (j n) -> p j n", n=P), ACT.Copy)
                    last.then_inc(scalar_done, 1)
                elif kind in ("exA", "exC"):
                    t, h = rest
                    act.wait_ge(vector_done, vector("mx" + kind[-1], l, t, h))
                    i = (t * 4 + h) % 2
                    nk = (4 if t < 2 else 2) * P
                    for q in range(2 if kind == "exA" else 1):
                        last = act.activation(ee[:, i, q, 0:nk], bank(("s" + kind[2], l, t, h, q))[:, 0:nk], ACT.Exp,
                                              bias=nm[:, i, q:q + 1], scale=(32 if kind == "exA" else 64) ** -0.5,
                                              accum_out=sums[:, i, q:q + 1])
                    if kind == "exC":
                        last = act.activation(esk[:, i:i + 1], rowp(l, R_SINK + h, 1), ACT.Exp, bias=nm[:, i, 0:1])
                    last.then_inc(scalar_done, 1)
                elif kind in ("pToutA", "pToutC"):
                    t, h = rest
                    act.wait_ge(tensor_done, tensor("pT" + kind[-1], l, t, h))
                    nk = (4 if t < 2 else 2) * P
                    last = act.activation(pt[:, h, 0:nk], bank(("pT" + kind[-1], l, t, h))[:, 0:nk], ACT.Copy)
                    last.then_inc(scalar_done, 1)
                elif kind in ("yToutA", "yToutC"):
                    (t,) = rest
                    act.wait_ge(tensor_done, tensor("yT" + kind[-1], l, t))
                    last = act.activation(yT[:, kind == "yToutC", :, t * P:(t + 1) * P],
                                          bank(("yT" + kind[-1], l, t))[:, 0:256].rearrange("p (j n) -> p j n", n=P), ACT.Copy)
                    last.then_inc(scalar_done, 1)
                elif kind in ("rexp1", "rexp2"):
                    tt = live(l)
                    act.wait_ge(vector_done, vector("route1" if kind == "rexp1" else "route2", l))
                    if kind == "rexp1":
                        last = act.activation(rtmp[:, 3, 0:4 * tt], rtmp[:, 0, 0:4 * tt], ACT.Exp)
                    else:
                        last = act.activation(rtmp[:, 9, 0:tt], rtmp[:, 8, 0:tt], ACT.Exp)
                    last.then_inc(scalar_done, 1)
                elif kind == "etanh":
                    e, f = rest
                    act.wait_ge(tensor_done, tensor("e1", l, e, f))
                    g = e * 4 + f
                    if g >= 2:
                        act.wait_ge(vector_done, vector("eu", l, (g - 2) // 4, (g - 2) % 4))
                    last = act.activation(eth[:, g % 2, 0:W], bank(("e1", l, e, f))[:, 0:W], ACT.Tanh, scale=0.5)
                    last.then_inc(scalar_done, 1)
                else:
                    raise KeyError(kind)

        @block.gpsimd
        def _(gp):
            gm = [s for s in STEPS["V"] if s[0] == "gmul"]
            for n, name in enumerate(STEPS["P"]):
                kind, l, rest = name[0], name[1], name[2:]
                W = 128 * live(l)
                if n:
                    gp.wait_ge(pool_done, n)
                if kind == "gadd":
                    bi, j = rest
                    gp.wait_ge(vector_done, vector("gmul", l, bi, j))
                    g = gm.index(("gmul", l, bi, j))
                    last = nc.gpsimd.tensor_tensor(acc[:, j, 0:W], acc[:, j, 0:W], gtmp[:, g % 2, 0:W], ALU.add)
                    last.then_inc(pool_done, 1)
                elif kind == "sqA":
                    (t,) = rest
                    gp.wait_ge(scalar_done, scalar("zAkout", l, t))
                    lo = 0 if t < live(l) else 256
                    if t >= 2:
                        gp.wait_ge(vector_done, vector("ssA", l, t - 2))
                    last = nc.gpsimd.tensor_tensor(sq[:, t % 2, lo:512], za[:, t, lo:512], za[:, t, lo:512], ALU.mult)
                    last.then_inc(pool_done, 1)
                elif kind == "sqC":
                    (t,) = rest
                    gp.wait_ge(scalar_done, scalar("zCout", l, t))
                    gp.wait_ge(vector_done, vector(*(("ssC", l, t - 2) if t >= 2 else ("ssA", l, t + 2))))
                    last = nc.gpsimd.tensor_tensor(sq[:, t % 2, 0:128], zc[:, t, 0:128], zc[:, t, 0:128], ALU.mult)
                    if t < live(l):
                        last = nc.gpsimd.tensor_tensor(sq[:, t % 2, 256:512], zc[:, t, 256:512], zc[:, t, 256:512], ALU.mult)
                    last.then_inc(pool_done, 1)

        @block.vector
        def _(v):
            links = [0]

            def link(ins):
                links[0] += 1
                ins.then_inc(vector_chain, 1)
                v.wait_ge(vector_chain, links[0])

            def rsqrt(y, a, t, last=False):
                link(v.tensor_scalar(y.bitcast(I32), a.bitcast(I32), 1, None, ALU.logical_shift_right))
                link(v.tensor_scalar(y.bitcast(I32), y.bitcast(I32), -1.0, float(0x5f3759df), ALU.mult, ALU.add))
                for i in range(3):
                    link(v.scalar_tensor_tensor(out=t, in0=y, scalar=-0.5, in1=y, op0=ALU.mult, op1=ALU.mult))
                    link(v.tensor_tensor(t, t, a, ALU.mult))
                    ins = v.scalar_tensor_tensor(out=y, in0=t, scalar=1.5, in1=y, op0=ALU.add, op1=ALU.mult)
                    if last and i == 2:
                        return ins
                    link(ins)

            def rope(zt, rs, l, t, parts, d, cosn, sinn):
                for k, (lo, hi, g0, gain) in enumerate(parts):
                    G = (hi - lo) // d
                    X = zt[:, t, lo:hi].rearrange("p (g d) -> p g d", d=d)
                    ins = v.tensor_tensor(X, X, rs[:, t, g0:g0 + G].unsqueeze(2).broadcast_to([P, G, d]), ALU.mult)
                    link(ins)
                    ins = v.tensor_tensor(X, X, rowp(l, gain, d).unsqueeze(1).broadcast_to([P, G, d]), ALU.mult)
                    if t >= 2:
                        if k == len(parts) - 1:
                            return ins
                        link(ins)
                        continue
                    link(ins)
                    q = d // 4
                    cs = c(cosn).rearrange("p (t d) -> p t d", t=2)[:, t, :]
                    sn = c(sinn).rearrange("p (t a h q) -> p t a h q", t=2, a=2, h=2)[:, t]
                    R = rt[:, 0, lo:hi].rearrange("p (g d) -> p g d", d=d)
                    link(v.tensor_tensor(R, X, cs.unsqueeze(1).broadcast_to([P, G, d]), ALU.mult))
                    X4 = zt[:, t, lo:hi].rearrange("p (g a h q) -> p g a h q", a=2, h=2, q=q)
                    T4 = rt[:, 1, lo:hi].rearrange("p (g a h q) -> p g a h q", a=2, h=2, q=q)
                    for h in range(2):
                        ins = v.tensor_tensor(T4[:, :, :, h, :], X4[:, :, :, 1 - h, :],
                                              sn[:, :, h, :].unsqueeze(1).broadcast_to([P, G, 2, q]), ALU.mult)
                        link(ins)
                    ins = v.tensor_tensor(zt[:, t, lo:hi], rt[:, 0, lo:hi], rt[:, 1, lo:hi], ALU.add)
                    if k == len(parts) - 1:
                        return ins
                    link(ins)

            def first_max(one_hot, a, top, r, tt):
                A3 = lambda s: s.rearrange("p (t g) -> p t g", g=4)
                link(v.tensor_tensor(A3(r), A3(a), top.unsqueeze(2).broadcast_to([P, tt, 4]), ALU.is_equal))
                link(v.tensor_tensor(A3(r), A3(r), c("rank").unsqueeze(1).broadcast_to([P, tt, 4]), ALU.mult))
                link(v.tensor_reduce(top, A3(r), AX.X, ALU.max))
                link(v.tensor_tensor(A3(one_hot), A3(r), top.unsqueeze(2).broadcast_to([P, tt, 4]), ALU.is_equal))

            gm = [s for s in STEPS["V"] if s[0] == "gmul"]
            v.wait_ge(params_landed, 16 * 5)
            v.wait_ge(const_landed, 16)
            for n, name in enumerate(STEPS["V"]):
                kind, l, rest = name[0], name[1], name[2:]
                tt = live(l)
                W = 128 * tt
                if n:
                    v.wait_ge(vector_done, n)
                if kind == "pads":
                    if l:
                        v.wait_ge(tensor_done, tensor("e2", l - 1, NE - 1, live(l - 1) - 1, 1))
                    else:
                        v.wait_ge(scalar_done, scalar("silu", 0))
                        link(v.scalar_tensor_tensor(out=ct[:], in0=ct[:], scalar=1.0, in1=cc[:], op0=ALU.add, op1=ALU.mult))
                        link(v.tensor_scalar(cc[:], ct[:], 0.5, None, ALU.mult))
                    link(v.memset(m[:, 0:1032], 0.0))
                    link(v.memset(n_[:, 0:1144], 0.0))
                    link(v.tensor_scalar(hbg[:], col[:, l, C_BGATE:C_BGATE + 32], 0.5, None, ALU.mult))
                    lam = rowp(l, R_LAM, 128).rearrange("p (a b n) -> p a b n", a=2, b=2)
                    prod = lamt[:, 0:64].rearrange("p (a n) -> p a n", a=2)
                    link(v.tensor_tensor(prod, lam[:, :, 0, :], lam[:, :, 1, :], ALU.mult))
                    last = v.tensor_reduce(lamt[:, 64:66], prod, AX.X, ALU.add)
                    last.then_inc(vector_done, 1)
                elif kind == "lam":
                    v.wait_ge(scalar_done, scalar("lamexp", l))
                    lam0 = 0.8 - 0.6 * math.exp(-0.3 * l)
                    link(v.tensor_tensor(nlam[:, 0:1], lamt[:, 67:68], lamt[:, 66:67], ALU.subtract))
                    last = v.tensor_scalar(nlam[:, 1:2], nlam[:, 0:1], -lam0, None, ALU.add)
                    last.then_inc(vector_done, 1)
                elif kind == "modcol":
                    (ch,) = rest
                    v.wait_ge(tensor_done, tensor("modT", l, ch))
                    slot = {0: 0, 1: 1, 3: 2, 4: 3}[ch // 2]
                    k0 = (ch % 2) * 4
                    src = bank(("modT", l, ch)).rearrange("p (j g r) -> p j r g", g=4, r=32)[:, :, 0:2, :]
                    link(v.tensor_reduce(modt[:], src, AX.X, ALU.add))
                    bm = col[:, l, C_BMOD + ch * 4:C_BMOD + ch * 4 + 4].unsqueeze(2).broadcast_to([P, 4, 2])
                    last = v.tensor_tensor(mod[:, slot, k0:k0 + 4, :], modt[:], bm, ALU.add)
                    last.then_inc(vector_done, 1)
                elif kind == "modgate":
                    ch, s = rest
                    v.wait_ge(tensor_done, tensor("modB", l, ch, s))
                    last = v.tensor_copy(gbc[:, s, (ch % 2) * 512:(ch % 2 + 1) * 512], bank(("modB", l, ch, s)))
                    last.then_inc(vector_done, 1)
                elif kind == "modfin":
                    (nn,) = rest
                    g = col[:, l, (C_N1, C_N2)[nn - 1]:(C_N1, C_N2)[nn - 1] + KD].unsqueeze(2).broadcast_to([P, KD, 2])
                    last = v.scalar_tensor_tensor(out=amp[:], in0=mod[:, 2 * nn - 1], scalar=1.0, in1=g,
                                                  op0=ALU.add, op1=ALU.mult)
                    last.then_inc(vector_done, 1)
                elif kind == "rstd":
                    (nn,) = rest
                    T = TILES if nn == 1 else tt
                    v.wait_ge(scalar_done, scalar("sq", l, nn, T - 1))
                    link(v.tensor_scalar(small[:, 1, 0:T], ss[:, 0:T], 1.0 / D, EPS, ALU.mult, ALU.add))
                    last = rsqrt(small[:, 0, 0:T], small[:, 1, 0:T], small[:, 2, 0:T], True)
                    last.then_inc(vector_done, 1)
                elif kind == "xn":
                    nn, t = rest
                    last = v.tensor_scalar(xn[:, t, :], x[:, t, :], small[:, 0, t:t + 1], None, ALU.mult)
                    last.then_inc(vector_done, 1)
                elif kind == "hTout":
                    nn, k = rest
                    v.wait_ge(tensor_done, tensor("hT", l, *rest))
                    for s in range(2 if nn == 1 else streams(l)):
                        h = slice(256 * s, 256 * s + 256)
                        last = v.tensor_scalar(hT[:, k, h], bank(("hT", l, *rest))[:, h], amp[:, k, s:s + 1],
                                               mod[:, 2 * nn - 2, k, s:s + 1], ALU.mult, ALU.add)
                    last.then_inc(vector_done, 1)
                elif kind == "zDout":
                    (j,) = rest
                    v.wait_ge(scalar_done, scalar("zDout", l, j + 2))
                    link(v.tensor_scalar(sqd[:, j, 0:W], thd[:, j, 0:W], 0.5, 0.5, ALU.mult, ALU.add))
                    v.wait_ge(tensor_done, tensor("zD", l, j))
                    s3 = lambda a: a[:, 0:W].rearrange("p (s n) -> p s n", n=256)
                    last = v.tensor_tensor(ud[:, j, 0:streams(l), PAD:PAD + 256], s3(sqd[:, j, :]),
                                           s3(bank(("zD", l, j))), ALU.mult)
                    last.then_inc(vector_done, 1)
                elif kind == "hyconv":
                    (j,) = rest
                    v.wait_ge(scalar_done, scalar("zBout", l, j))
                    ns = streams(l)
                    o = hu[:, j, 0:ns, :]
                    w = lambda k: col[:, l, C_HYW + k * 6 + j:C_HYW + k * 6 + j + 1]
                    link(v.tensor_scalar(o, zb[:, j % 2, 0:ns, 0:256], w(0), col[:, l, C_HYB + j:C_HYB + j + 1],
                                         ALU.mult, ALU.add))
                    link(v.scalar_tensor_tensor(out=o, in0=zb[:, j % 2, 0:ns, 1:257], scalar=w(1), in1=o,
                                                op0=ALU.mult, op1=ALU.add))
                    last = v.scalar_tensor_tensor(out=o, in0=zb[:, j % 2, 0:ns, 2:258], scalar=w(2), in1=o,
                                                  op0=ALU.mult, op1=ALU.add)
                    last.then_inc(vector_done, 1)
                elif kind == "vx":
                    ns = streams(l)
                    for j in range(2):
                        last = v.tensor_tensor(hu[:, 4 + j, 0:ns, :], hu[:, 4 + j, 0:ns, :], hu[:, 2 + j, 0:ns, :], ALU.mult)
                    last.then_inc(vector_done, 1)
                elif kind == "cfconv":
                    (j,) = rest
                    ns = streams(l)
                    o = cv[:, j, 0:W].rearrange("p (s n) -> p s n", n=256)
                    w = lambda k: col[:, l, C_CFW + k * 2 + j:C_CFW + k * 2 + j + 1]
                    link(v.tensor_scalar(o, ud[:, j, 0:ns, 0:256], w(0), col[:, l, C_CFB + j:C_CFB + j + 1],
                                         ALU.mult, ALU.add))
                    for k in range(1, TAPS):
                        last = v.scalar_tensor_tensor(out=o, in0=ud[:, j, 0:ns, k:k + 256], scalar=w(k), in1=o,
                                                      op0=ALU.mult, op1=ALU.add)
                        if k < TAPS - 1:
                            link(last)
                    last.then_inc(vector_done, 1)
                elif kind == "hfarg":
                    (i,) = rest
                    v.wait_ge(tensor_done, tensor("hf", l, i))
                    a, kk = hfarg[0:64, :], hfk[0:64, :]
                    link(v.tensor_scalar(a, bank(("hf", l, i))[0:64, 0:256], col[0:64, l, C_HF + i - 1:C_HF + i],
                                         col[0:64, l, C_HF + 3:C_HF + 4], ALU.add, ALU.mult))
                    link(v.tensor_scalar(kk, a, 1.0 / TWO_PI, MAGIC, ALU.mult, ALU.add))
                    link(v.tensor_scalar(kk, kk, MAGIC, None, ALU.subtract))
                    link(v.scalar_tensor_tensor(out=a, in0=kk, scalar=-PI_HI, in1=a, op0=ALU.mult, op1=ALU.add))
                    link(v.scalar_tensor_tensor(out=a, in0=kk, scalar=-PI_LO, in1=a, op0=ALU.mult, op1=ALU.add))
                    last = v.tensor_scalar(a, a, SIN_MAX, -SIN_MAX, ALU.min, ALU.max)
                    last.then_inc(vector_done, 1)
                elif kind == "hfwin":
                    (i,) = rest
                    v.wait_ge(tensor_done, tensor("hf4", l, i))
                    last = v.tensor_tensor(hf[:, i, :], bank(("hf4", l, i)), win_c[:, i, :], ALU.mult)
                    last.then_inc(vector_done, 1)
                elif kind == "fnorms":
                    v.wait_ge(tensor_done, tensor("fnorm", l))
                    link(v.tensor_scalar(small[:, 1, 0:2], bank(("fnorm", l))[:, 0:2], 256.0, EPS, ALU.mult, ALU.add))
                    last = rsqrt(fn[:], small[:, 1, 0:2], small[:, 2, 0:2], True)
                    last.then_inc(vector_done, 1)
                elif kind == "xc":
                    v.wait_ge(tensor_done, tensor("lnmean", l))
                    for j in range(2):
                        last = v.tensor_tensor(cv[:, j, 0:W], cv[:, j, 0:W], bank(("lnmean", l))[:, 0:W], ALU.subtract)
                    last.then_inc(vector_done, 1)
                elif kind == "lnv":
                    v.wait_ge(tensor_done, tensor("lnvar", l))
                    a = sqd[:, 0, 0:W]
                    link(v.tensor_scalar(a, bank(("lnvar", l))[:, 0:W], EPS, None, ALU.add))
                    rsqrt(rsd[:, 0, 0:W], a, rsd[:, 1, 0:W])
                    for j in range(2):
                        link(v.tensor_tensor(cv[:, j, 0:W], cv[:, j, 0:W], rsd[:, 0, 0:W], ALU.mult))
                        last = v.tensor_scalar(cv[:, j, 0:W], cv[:, j, 0:W], col[:, l, C_LNG + j:C_LNG + j + 1],
                                               col[:, l, C_LNB + j:C_LNB + j + 1], ALU.mult, ALU.add)
                    last.then_inc(vector_done, 1)
                elif kind == "lnout":
                    v.wait_ge(scalar_done, scalar("lntanh", l))
                    link(v.tensor_scalar(sqd[:, :, 0:W], thd[:, :, 0:W], 0.5, 0.5, ALU.mult, ALU.add))
                    last = v.tensor_tensor(yT[:, 0, :, 0:W], cv[:, :, 0:W], sqd[:, :, 0:W], ALU.mult)
                    last.then_inc(vector_done, 1)
                elif kind == "spec":
                    v.wait_ge(scalar_done, scalar("dftout", l, 3))
                    v.wait_ge(scalar_done, scalar("fdftout", l, 5))
                    ns = streams(l)
                    S3 = lambda a: a[:, 0:W].rearrange("p (s n) -> p s n", n=256)
                    tmp = hu[:, 2, 0:ns, :]
                    for f in range(2):
                        A, B, C = (fs[:, f + 2 * q, :].unsqueeze(1).broadcast_to([P, ns, 256]) for q in range(3))
                        uc, us_, yc, ys = S3(us[:, f, :]), S3(us[:, 2 + f, :]), S3(ysp[:, f, :]), S3(ysp[:, 2 + f, :])
                        link(v.tensor_tensor(tmp, us_, B, ALU.mult))
                        link(v.tensor_tensor(yc, uc, A, ALU.mult))
                        link(v.tensor_tensor(yc, yc, tmp, ALU.subtract))
                        link(v.tensor_tensor(tmp, uc, B, ALU.mult))
                        link(v.tensor_tensor(ys, us_, C, ALU.mult))
                        last = v.tensor_tensor(ys, ys, tmp, ALU.add)
                        if f == 0:
                            link(last)
                    last.then_inc(vector_done, 1)
                elif kind == "hyout":
                    (j,) = rest
                    v.wait_ge(tensor_done, tensor("idft", l, j))
                    o = yT[:, 1, j, 0:W]
                    S3 = lambda a: a.rearrange("p (s n) -> p s n", n=256)
                    link(v.tensor_scalar(o, bank(("idft", l, j))[:, 0:W], fn[:, j:j + 1], None, ALU.mult))
                    ns = streams(l)
                    link(v.scalar_tensor_tensor(out=S3(o), in0=hu[:, 4 + j, 0:ns, :],
                                                scalar=col[:, l, C_HYBIAS + j:C_HYBIAS + j + 1], in1=S3(o),
                                                op0=ALU.mult, op1=ALU.add))
                    last = v.tensor_tensor(S3(o), S3(o), hu[:, j, 0:ns, :], ALU.mult)
                    last.then_inc(vector_done, 1)
                elif kind == "gmul":
                    bi, j = rest
                    g = gm.index(name)
                    v.wait_ge(scalar_done, scalar("gtanh", l, bi, j))
                    v.wait_ge(tensor_done, tensor("br", l, bi, j))
                    dst = acc[:, j, 0:W] if bi == BRANCHES[0] else gtmp[:, g % 2, 0:W]
                    if g >= 2 and ("gadd", *gm[g - 2][1:]) in COUNT["P"]:
                        v.wait_ge(pool_done, pool("gadd", *gm[g - 2][1:]))
                    last = v.scalar_tensor_tensor(out=dst, in0=gth[:, g % 2, 0:W], scalar=1.0,
                                                  in1=bank(("br", l, bi, j))[:, 0:W], op0=ALU.add, op1=ALU.mult)
                    last.then_inc(vector_done, 1)
                elif kind == "ssA":
                    (t,) = rest
                    v.wait_ge(pool_done, pool("sqA", l, t))
                    lo = 0 if t < tt else 256
                    last = v.tensor_reduce(ssa[:, t, lo // 32:16], sq[:, t % 2, lo:512].rearrange("p (g d) -> p g d", d=32),
                                           AX.X, ALU.add)
                    last.then_inc(vector_done, 1)
                elif kind == "ssC":
                    (t,) = rest
                    v.wait_ge(pool_done, pool("sqC", l, t))
                    last = v.tensor_reduce(ssc[:, t, 0:2], sq[:, t % 2, 0:128].rearrange("p (g d) -> p g d", d=64), AX.X, ALU.add)
                    if t < tt:
                        last = v.tensor_reduce(ssc[:, t, 2:6], sq[:, t % 2, 256:512].rearrange("p (g d) -> p g d", d=64),
                                               AX.X, ALU.add)
                    last.then_inc(vector_done, 1)
                elif kind in ("rsA", "rsC"):
                    s_, r_, k = (ssa, rsa, 64) if kind == "rsA" else (ssc, rsc, 24)
                    f = lambda a: a[:].rearrange("p t g -> p (t g)")
                    link(v.tensor_scalar(small[:, 1, 0:k], f(s_), 1.0 / (32 if kind == "rsA" else 64), EPS, ALU.mult, ALU.add))
                    last = rsqrt(f(r_), small[:, 1, 0:k], small[:, 2, 0:k], True)
                    last.then_inc(vector_done, 1)
                elif kind == "ropeA":
                    (t,) = rest
                    ps_ = ([(0, 256, 0, R_QN)] if t < tt else []) + [(256, 512, 8, R_KN)]
                    last = rope(za, rsa, l, t, ps_, 32, "cosa", "sina")
                    last.then_inc(vector_done, 1)
                elif kind == "ropeC":
                    (t,) = rest
                    ps_ = [(0, 128, 0, R_WK)] + ([(256, 512, 2, R_WQ)] if t < tt else [])
                    last = rope(zc, rsc, l, t, ps_, 64, "cosc", "sinc")
                    last.then_inc(vector_done, 1)
                elif kind == "mxA":
                    t, h = rest
                    i = (t * 4 + h) % 2
                    nk = (4 if t < 2 else 2) * P
                    v.wait_ge(tensor_done, tensor("sA", l, t, h, 1))
                    for q in range(2):
                        link(v.reduce_max(mx[:, i, q:q + 1], bank(("sA", l, t, h, q))[:, 0:nk], AX.X))
                    last = v.tensor_scalar(nm[:, i, :], mx[:, i, :], -(32 ** -0.5), None, ALU.mult)
                    last.then_inc(vector_done, 1)
                elif kind == "mxC":
                    t, h = rest
                    i = (t * 4 + h) % 2
                    nk = (4 if t < 2 else 2) * P
                    v.wait_ge(tensor_done, tensor("sC", l, t, h, 0))
                    b = bank(("sC", l, t, h, 0))
                    if t < 2:
                        other = b[:, (1 - t) * P:(2 - t) * P]
                        link(v.tensor_tensor(other, other, mask_c[:, t, :], ALU.add))
                    link(v.reduce_max(mx[:, i, 0:1], b[:, 0:nk], AX.X))
                    link(v.tensor_scalar(mx[:, i, 1:2], mx[:, i, 0:1], 64 ** -0.5, rowp(l, R_SINK + h, 1), ALU.mult, ALU.max))
                    last = v.tensor_scalar(nm[:, i, 0:1], mx[:, i, 1:2], -1.0, None, ALU.mult)
                    last.then_inc(vector_done, 1)
                elif kind == "pA":
                    t, h = rest
                    i = (t * 4 + h) % 2
                    nk = (4 if t < 2 else 2) * P
                    v.wait_ge(scalar_done, scalar("exA", l, t, h))
                    link(v.reciprocal(rr[:], sums[:, i, :]))
                    link(v.tensor_tensor(nlam[:, 2:3], rr[:, 1:2], nlam[:, 1:2], ALU.mult))
                    link(v.tensor_scalar(ee[:, i, 0, 0:nk], ee[:, i, 0, 0:nk], rr[:, 0:1], None, ALU.mult))
                    last = v.scalar_tensor_tensor(out=ee[:, i, 0, 0:nk], in0=ee[:, i, 1, 0:nk], scalar=nlam[:, 2:3],
                                                  in1=ee[:, i, 0, 0:nk], op0=ALU.mult, op1=ALU.add)
                    last.then_inc(vector_done, 1)
                elif kind == "pC":
                    t, h = rest
                    i = (t * 4 + h) % 2
                    v.wait_ge(scalar_done, scalar("exC", l, t, h))
                    last = v.tensor_tensor(den[:, h:h + 1], sums[:, i, 0:1], esk[:, i:i + 1], ALU.add)
                    last.then_inc(vector_done, 1)
                elif kind == "ynA":
                    (t,) = rest
                    v.wait_ge(tensor_done, tensor("yA", l, t))
                    H = lambda a: a.rearrange("p (h d) -> p h d", h=4)
                    lam0 = 0.8 - 0.6 * math.exp(-0.3 * l)
                    link(v.tensor_copy(yn, bank(("yA", l, t))[:, 0:256]))
                    link(v.tensor_tensor(ynq, yn, yn, ALU.mult))
                    link(v.tensor_reduce(small[:, 1, 0:4], H(ynq), AX.X, ALU.add))
                    link(v.tensor_scalar(small[:, 1, 0:4], small[:, 1, 0:4], 1.0 / 64, EPS, ALU.mult, ALU.add))
                    rsqrt(small[:, 0, 8:12], small[:, 1, 0:4], small[:, 2, 0:4])
                    link(v.tensor_tensor(H(yn), H(yn), small[:, 0, 8:12].unsqueeze(2).broadcast_to([P, 4, 64]), ALU.mult))
                    last = v.scalar_tensor_tensor(out=H(yn), in0=H(yn), scalar=1.0 - lam0,
                                                  in1=rowp(l, R_SUB, 64).unsqueeze(1).broadcast_to([P, 4, 64]),
                                                  op0=ALU.mult, op1=ALU.mult)
                    last.then_inc(vector_done, 1)
                elif kind == "ynC":
                    (t,) = rest
                    v.wait_ge(tensor_done, tensor("yC", l, t))
                    H = lambda a: a.rearrange("p (h d) -> p h d", h=4)
                    link(v.reciprocal(rden[:], den[:]))
                    last = v.tensor_tensor(H(yn), H(bank(("yC", l, t))[:, 0:256]),
                                           rden[:].unsqueeze(2).broadcast_to([P, 4, 64]), ALU.mult)
                    last.then_inc(vector_done, 1)
                elif kind == "xup":
                    t, half = rest
                    v.wait_ge(tensor_done, tensor("wo", l, t, half))
                    xs = x[:, t, half * 512:(half + 1) * 512]
                    link(v.scalar_tensor_tensor(out=gtmp[:, half, :], in0=bank(("wo", l, t, half)), scalar=0.5,
                                                in1=gbc[:, t // 2, half * 512:(half + 1) * 512], op0=ALU.mult, op1=ALU.mult))
                    last = v.tensor_tensor(xs, xs, gtmp[:, half, :], ALU.add)
                    last.then_inc(vector_done, 1)
                elif kind == "lgout":
                    (t,) = rest
                    v.wait_ge(tensor_done, tensor("lg", l, t))
                    last = v.tensor_tensor(lg[:, t, :], bank(("lg", l, t))[:, 0:20], rowp(l, R_BR, 20), ALU.add)
                    last.then_inc(vector_done, 1)
                elif kind == "route1":
                    d0 = rtmp[:, 0, 0:4 * tt].rearrange("p (t g) -> p t g", g=4)
                    link(v.tensor_reduce(rtmp[:, 2, 0:tt], lg[:, 0:tt, 0:4], AX.X, ALU.max))
                    last = v.tensor_tensor(d0, lg[:, 0:tt, 0:4], rtmp[:, 2, 0:tt].unsqueeze(2).broadcast_to([P, tt, 4]),
                                           ALU.subtract)
                    last.then_inc(vector_done, 1)
                elif kind == "route2":
                    d0, oh = rtmp[:, 0, 0:4 * tt], rtmp[:, 1, 0:4 * tt]
                    v.wait_ge(scalar_done, scalar("rexp1", l))
                    T4 = lambda a: a.rearrange("p (t g) -> p t g", g=4)
                    link(v.tensor_reduce(rtmp[:, 2, 0:tt], T4(rtmp[:, 3, 0:4 * tt]), AX.X, ALU.add))
                    link(v.reciprocal(rtmp[:, 4, 0:tt], rtmp[:, 2, 0:tt]))
                    link(v.tensor_reduce(rtmp[:, 2, 0:tt], T4(d0), AX.X, ALU.max))
                    first_max(oh, d0, rtmp[:, 2, 0:tt], rtmp[:, 5, 0:4 * tt], tt)
                    for t in range(tt):
                        link(v.tensor_tensor(rt16[:, t, :].rearrange("p (g j) -> p g j", j=4),
                                             lg[:, t, 4:20].rearrange("p (g j) -> p g j", j=4),
                                             oh[:, 4 * t:4 * t + 4].unsqueeze(2).broadcast_to([P, 4, 4]), ALU.mult))
                    le = rtmp[:, 6, 0:4 * tt]
                    link(v.tensor_reduce(T4(le), rt16[:, 0:tt, :].rearrange("p t (g j) -> p t j g", j=4), AX.X, ALU.add))
                    link(v.tensor_reduce(rtmp[:, 2, 0:tt], T4(le), AX.X, ALU.max))
                    link(v.tensor_copy(rtmp[:, 2, 4:4 + tt], rtmp[:, 2, 0:tt]))
                    first_max(rtmp[:, 7, 0:4 * tt], le, rtmp[:, 2, 0:tt], rtmp[:, 5, 0:4 * tt], tt)
                    link(v.tensor_tensor(T4(le), T4(le), rtmp[:, 2, 4:4 + tt].unsqueeze(2).broadcast_to([P, tt, 4]),
                                         ALU.subtract))
                    link(v.scalar_tensor_tensor(out=le, in0=rtmp[:, 7, 0:4 * tt], scalar=NEG, in1=le,
                                                op0=ALU.mult, op1=ALU.add))
                    link(v.tensor_reduce(rtmp[:, 8, 0:tt], T4(le), AX.X, ALU.max))
                    link(v.tensor_copy(rtmp[:, 2, 0:tt], rtmp[:, 8, 0:tt]))
                    first_max(rtmp[:, 10, 0:4 * tt], le, rtmp[:, 2, 0:tt], rtmp[:, 5, 0:4 * tt], tt)
                    last = v.tensor_copy(rtmp[:, 11, 0:tt], rtmp[:, 8, 0:tt])
                    last.then_inc(vector_done, 1)
                elif kind == "route3":
                    v.wait_ge(scalar_done, scalar("rexp2", l))
                    T4 = lambda a: a.rearrange("p (t g) -> p t g", g=4)
                    p1, p2 = rtmp[:, 11, 0:tt], rtmp[:, 11, 4:4 + tt]
                    link(v.tensor_scalar(p1, rtmp[:, 9, 0:tt], 1.0, None, ALU.add))
                    link(v.reciprocal(p2, p1))
                    link(v.scalar_tensor_tensor(out=p1, in0=p2, scalar=0.5, in1=rtmp[:, 4, 0:tt], op0=ALU.mult, op1=ALU.mult))
                    link(v.tensor_tensor(p2, p1, rtmp[:, 9, 0:tt], ALU.mult))
                    a, b_ = rtmp[:, 7, 0:4 * tt], rtmp[:, 10, 0:4 * tt]
                    link(v.tensor_tensor(T4(a), T4(a), p1.unsqueeze(2).broadcast_to([P, tt, 4]), ALU.mult))
                    link(v.tensor_tensor(T4(b_), T4(b_), p2.unsqueeze(2).broadcast_to([P, tt, 4]), ALU.mult))
                    link(v.tensor_tensor(a, a, b_, ALU.add))
                    for t in range(tt):
                        last = v.tensor_tensor(rw[:, t, :].rearrange("p (g j) -> p g j", j=4),
                                               rtmp[:, 1, 4 * t:4 * t + 4].unsqueeze(2).broadcast_to([P, 4, 4]),
                                               a[:, 4 * t:4 * t + 4].unsqueeze(1).broadcast_to([P, 4, 4]), ALU.mult)
                    last.then_inc(vector_done, 1)
                elif kind == "eu":
                    e, f = rest
                    v.wait_ge(scalar_done, scalar("etanh", l, e, f))
                    link(v.scalar_tensor_tensor(out=es[:, 0:W], in0=eth[:, (e * 4 + f) % 2, 0:W], scalar=1.0,
                                                in1=bank(("e1", l, e, f))[:, 0:W], op0=ALU.add, op1=ALU.mult))
                    v.wait_ge(tensor_done, tensor("e3", l, e, f))
                    last = v.tensor_tensor(u[:, f, 0:W], es[:, 0:W], bank(("e3", l, e, f))[:, 0:W], ALU.mult)
                    last.then_inc(vector_done, 1)
                elif kind == "eacc":
                    e, t, half = rest
                    v.wait_ge(tensor_done, tensor("e2", l, e, t, half))
                    b = bank(("e2", l, e, t, half))
                    o = xn[:, t, half * 512:(half + 1) * 512]
                    w = rw[:, t, e:e + 1]
                    if e == 0:
                        last = v.tensor_scalar(o, b, w, None, ALU.mult)
                    else:
                        last = v.scalar_tensor_tensor(out=o, in0=b, scalar=w, in1=o, op0=ALU.mult, op1=ALU.add)
                    last.then_inc(vector_done, 1)
                elif kind == "xup2":
                    (t,) = rest
                    link(v.tensor_tensor(xn[:, t, :], xn[:, t, :], gbc[:, t // 2, :], ALU.mult))
                    last = v.tensor_tensor(x[:, t, :], x[:, t, :], xn[:, t, :], ALU.add)
                    last.then_inc(vector_done, 1)
                else:
                    raise KeyError(kind)


def kernel(**inputs):
    import numpy as _np
    import concourse.bacc as _bacc
    from concourse import mybir as _mybir
    from concourse.bass_utils import run_bass_kernel_spmd as _run

    I = {k: _np.asarray(v) for k, v in inputs.items()}

    def tiles(a):
        n = a.shape[0] // P
        return a.reshape(n, P, a.shape[1]).transpose(1, 0, 2).reshape(P, -1)

    def chan(v):
        return v.reshape(-1, P).T

    arrays = {}
    tok = _np.concatenate([I["x"][0], I["ctx"][0]], 0)
    arrays["xin"] = tok.reshape(TILES, P, D).transpose(1, 0, 2)
    cc = _np.zeros((P, KD, 32), _np.float32)
    cc[:, :, 0] = chan(I["c"][0])
    cc[:, :, 1] = chan(I["c_ctx"])
    arrays["ccol"] = cc.reshape(P, -1)
    const, fd, _ = constants()
    arrays["const"] = const
    cols = _np.zeros((P, DEPTH, NC), _np.float32)
    rows = _np.zeros((DEPTH, NR), _np.float32)
    hfw = _np.zeros((DEPTH, 64, HF_COLS), _np.float32)
    wr = _np.zeros((P, DEPTH, KD, 20), _np.float32)
    bgr = _np.zeros((8, 512), _np.float32)
    winc = _np.zeros((DEPTH, 14, P, WCH), _np.float32)
    wmod = _np.zeros((DEPTH, 12, P, WCH), _np.float32)
    wbr = _np.zeros((DEPTH, 4, P, 2 * D), _np.float32)
    wout = _np.zeros((DEPTH, 2, P, WCH), _np.float32)
    for l in range(DEPTH):
        q = cols[:, l]
        q[:, C_N1:C_N1 + 8] = chan(I["norm1_g"][l])
        q[:, C_N2:C_N2 + 8] = chan(I["norm2_g"][l])
        q[:, C_BMOD:C_BMOD + 48] = chan(I["b_mod"][l])
        q[:, C_BGATE:C_BGATE + 32] = chan(I["b_gate"][l])
        for k in range(3):
            q[:, C_HYW + 6 * k:C_HYW + 6 * k + 6] = chan(I["hy_conv_w"][l, k])
        q[:, C_HYB:C_HYB + 6] = chan(I["hy_conv_b"][l])
        q[:, C_HYBIAS:C_HYBIAS + 2] = chan(I["hy_bias"][l])
        for k in range(TAPS):
            q[:, C_CFW + 2 * k:C_CFW + 2 * k + 2] = chan(I["cf_dw_w"][l, k])
        q[:, C_CFB:C_CFB + 2] = chan(I["cf_dw_b"][l])
        q[:, C_LNG:C_LNG + 2] = chan(I["cf_ln_g"][l])
        q[:, C_LNB:C_LNB + 2] = chan(I["cf_ln_b"][l])
        for k, nme in enumerate(("hf_b1", "hf_b2", "hf_b3", "hf_freq")):
            q[0:64, C_HF + k] = I[nme][l]
        rows[l, R_QN:R_QN + 32] = I["da_qn"][l]
        rows[l, R_KN:R_KN + 32] = I["da_kn"][l]
        rows[l, R_WQ:R_WQ + 64] = I["wa_qn"][l]
        rows[l, R_WK:R_WK + 64] = I["wa_kn"][l]
        rows[l, R_SUB:R_SUB + 64] = I["da_subln"][l]
        rows[l, R_BR:R_BR + 4] = I["b_rg"][l]
        rows[l, R_BR + 4:R_BR + 20] = I["b_re"][l]
        rows[l, R_SINK:R_SINK + 4] = I["wa_sink"][l]
        rows[l, R_LAM:R_LAM + 128] = I["da_lam"][l].reshape(-1)
        hfw[l, 0:33, 0:64] = I["hf_w1"][l]
        hfw[l, :, 64:128] = I["hf_w2"][l]
        hfw[l, :, 128:192] = I["hf_w3"][l]
        hfw[l, :, 192:704] = I["hf_w4"][l]
        wr[:, l] = _np.concatenate([I["w_rg"][l], I["w_re"][l]], 1).reshape(KD, P, 20).transpose(1, 0, 2)
        for g in range(2):
            for half in range(2):
                at = (2 + 3 * g) * D + half * 512
                bgr[l * 4 + g * 2 + half] = I["b_mod"][l, at:at + 512]
        w = I["w_in"][l]
        wb, wc, wd, wg = w[:, 768:1536], w[:, 1536:2048], w[:, 2048:2560], w[:, 2560:]
        heads = [wc[:, 64 * h:64 * h + 64] for h in (0, 2, 1, 3)]
        wc = _np.concatenate([wc[:, 256:512]] + heads, 1)
        for i, piece in enumerate((wd, wb[:, 0:512], wb[:, 512:768], w[:, 0:256], w[:, 256:768], wc)):
            winc[l, i, :, 0:KD * piece.shape[1]] = tiles(piece)
        for i in range(8):
            winc[l, 6 + i] = tiles(wg[:, i * 512:(i + 1) * 512])
        for i in range(12):
            wmod[l, i] = tiles(I["w_mod"][l][:, i * 512:(i + 1) * 512])
        for i in range(4):
            wbr[l, i] = tiles(I["w_branch"][l, i])
        for i in range(2):
            wout[l, i] = tiles(I["w_out"][l][:, i * 512:(i + 1) * 512])
    arrays["cols"], arrays["hfw"] = cols, hfw
    arrays["rows"] = _np.broadcast_to(rows.reshape(1, -1), (P, DEPTH * NR))
    arrays["wr"], arrays["bgate_rows"], arrays["fdft"] = wr, bgr, fd
    arrays["wmod"], arrays["win"], arrays["wbr"], arrays["wout"] = wmod, winc, wbr, wout
    for nme in ("w1", "w3"):
        arrays[nme] = I[nme].reshape(DEPTH, NE, KD, P, FE).transpose(0, 1, 3, 2, 4).reshape(DEPTH, NE, P, WCH)
    arrays["w2"] = I["w2"].reshape(DEPTH, NE, 4, P, D).transpose(0, 1, 3, 2, 4).reshape(DEPTH, NE, P, WCH)
    arrays = {k: _np.ascontiguousarray(a) for k, a in arrays.items()}

    nc = _bacc.Bacc("TRN2", target_bir_lowering=False, num_devices=1)
    args = {k: nc.dram_tensor(k, a.shape, _mybir.dt.from_np(a.dtype), kind="ExternalInput").ap()
            for k, a in arrays.items()}
    args["out"] = nc.dram_tensor("out", (SEQ, D), F32, kind="ExternalOutput").ap()
    build_trunk(nc, **args)
    r = _run(nc, [arrays], core_ids=[0])
    return r.results[0]["out"].reshape(1, SEQ, D)
```

```python
import math
from contextlib import ExitStack

import concourse.bass as bass
from concourse import mybir
import numpy as np

ALU = mybir.AluOpType
ACT = mybir.ActivationFunctionType
AX = mybir.AxisListType
F32 = mybir.dt.float32
I32 = mybir.dt.int32
U32 = mybir.dt.uint32

P = 128
D = 1024
KD = D // P
DEPTH = 2
SEQ = 256
TILES = 4
EPS = 1e-6
NEG = -1e30
NE = 16
FE = 512
BRANCHES = (3, 1, 0, 2)
TAPS = 31
PAD = TAPS // 2
BANKS = 8
RING = 3
WCH = 4096

C_N1, C_N2, C_BMOD, C_BGATE = 0, 8, 16, 64
C_HYW, C_HYB, C_HYBIAS = 96, 114, 120
C_CFW, C_CFB, C_LNG, C_LNB = 122, 184, 186, 188
C_HF = 190
NC = 194
R_QN, R_KN, R_WQ, R_WK, R_SUB, R_BR, R_SINK, R_LAM = 0, 32, 64, 128, 192, 256, 276, 280
NR = 408
HF_COLS = 64 * 3 + 512
TWO_PI = 2.0 * math.pi
PI_HI = 6.28125
PI_LO = TWO_PI - PI_HI
MAGIC = 1.5 * 2.0 ** 23
SIN_MAX = 3.1415925


def constants():
    f = np.float64
    L, N = SEQ, 2 * SEQ
    t = np.arange(L, dtype=f)
    k = np.arange(L, dtype=f)
    ang = 2 * np.pi / N * np.outer(t, k)
    alt = (-1.0) ** t
    sin = np.sin(ang)
    sin_nyq = sin.copy()
    sin_nyq[:, 0] = alt
    dft = np.concatenate([np.cos(ang), sin_nyq], 1)
    cos_nyq = np.cos(ang)
    cos_nyq[:, 0] = alt
    sin_zero = sin.copy()
    sin_zero[:, 0] = 0
    ahead = np.concatenate([np.cos(ang), sin_zero, cos_nyq], 1)
    behind = np.concatenate([np.cos(ang), -sin_zero, cos_nyq], 1)
    behind[0, :] = 0
    fdft = np.concatenate([ahead, behind], 0)
    wc = np.full((L, 1), 2.0 / N)
    wc[0] = 1.0 / N
    inv_c = wc * np.cos(ang.T)
    inv_s = 2.0 / N * sin.T
    inv_s[0] = alt / N
    idft = np.concatenate([inv_c, inv_s], 0)
    tl = np.linspace(0.0, 1.0, L, dtype=np.float32)[:, None]
    w = ((2.0 * math.pi / L) * np.arange(L, dtype=np.float32)[:, None]).astype(np.float32)
    bands = np.linspace(1e-4, 15, 16, dtype=np.float32)[None]
    wb = (w * bands).astype(np.float32).astype(f)
    feat = np.concatenate([tl, np.cos(wb), np.sin(wb)], 1)
    featT = np.zeros((P, L))
    featT[:33] = feat.T
    deltas = np.abs(np.linspace(math.log(1e-2) / 0.3, math.log(1e-2) / 1.5, 256, dtype=np.float32))
    win = np.exp(-tl.astype(f) * deltas[None].astype(f)) + 0.05
    win2 = np.concatenate([win, win], 1)
    win2[0, 256:] = 0

    def tiles(a):
        return a.reshape(-1, P, a.shape[1]).transpose(1, 0, 2).reshape(P, -1)

    def rope(d):
        qd = d // 4
        inv = 10000.0 ** (-np.arange(qd, dtype=f) / qd)
        row, col = np.arange(SEQ) // 64, np.arange(SEQ) % 64
        c, s = [], []
        for pos in (row, col):
            a = pos[:, None] * inv[None]
            c += [np.cos(a), np.cos(a)]
            s += [-np.sin(a), np.sin(a)]
        return tiles(np.concatenate(c, 1)), tiles(np.concatenate(s, 1))

    i = np.arange(P)
    mask = np.zeros((P, 2, P))
    mask[:, 0, :] = np.where(i[None] <= i[:, None], 0, NEG)
    mask[:, 1, :] = np.where(i[None] >= i[:, None], 0, NEG)
    ca, sa = rope(32)
    cc, sc = rope(64)
    rank = np.tile(np.arange(4, 0, -1.0), (P, 1))
    before = (i[:, None] < i[None]) / 256.0
    expert = np.tile(np.arange(NE, dtype=f), (P, 1))
    token = i[:, None] + P * np.arange(TILES)[None]
    parts = dict(ident=np.eye(P), mean=np.full((P, P), 1 / 256), dft=tiles(dft), idft=tiles(idft),
                 win=tiles(win2), mask=mask.reshape(P, -1), feat=featT,
                 cosa=ca, sina=sa, cosc=cc, sinc=sc, rank=rank, before=before, expert=expert, token=token)
    at, off = {}, 0
    for n, a in parts.items():
        at[n] = (off, a.shape[1])
        off += a.shape[1]
    return np.concatenate(list(parts.values()), 1).astype(np.float32), tiles(fdft).astype(np.float32), at


CONST_AT = constants()[2]
NCONST = sum(n for _, n in CONST_AT.values())


def live(l):
    return TILES if l < DEPTH - 1 else 2


def spread(main, side):
    out, n = [], 0
    for i, g in enumerate(main):
        upto = (i + 1) * len(side) // len(main)
        out += [g] + side[n:upto]
        n = upto
    return out


def merge(main, side):
    return [s for g in spread(main, side) for s in g]


def mod_steps(l, chunks):
    out = []
    for c in chunks:
        out += [("T", ("mod", l, c)), ("S", ("modrow", l, c))]
        out += [("T", ("modT", l, c)), ("V", ("modcol", l, c))]
    return out


def gate_steps(l, chunks):
    return [s for c in chunks for v in range(live(l) // 2)
            for s in (("T", ("modB", l, c, v)), ("V", ("modgate", l, c, v)))]


def filter_groups(l):
    net = [[("T", ("hf", l, n)), ("V", ("hfarg", l, n)), ("S", ("hfsin", l, n))] for n in (1, 2, 3)]
    net += [[("T", ("hf4", l, i)), ("V", ("hfwin", l, i)), ("S", ("hfsq", l, i))] for i in range(2)]
    spectrum = [[("T", ("fnorm", l)), ("V", ("fnorms", l))]]
    spectrum += [[("T", ("fdft", l, m)), ("S", ("fdftout", l, m))] for m in range(6)]
    return net, spectrum


def norm_steps(l, n, tiles):
    out = [("S", ("sq", l, n, t)) for t in tiles]
    out += [("V", ("rstd", l, n, tiles[0], tiles[-1] + 1))]
    out += [("S" if t % 2 else "V", ("xn", l, n, t)) for t in tiles]
    return out


def normed_with(l, n, t):
    last = live(l) - 1
    return (0, TILES) if n == 1 else (last, last + 1) if t == last else (0, last)


def modulated_steps(l, n):
    out = [("V", ("modfin", l, n))]
    for k in range(KD):
        out += [("T", ("hT", l, n, k)), ("V" if k % 2 else "S", ("hTout", l, n, k))]
    return out


def layer_order(l):
    tt = live(l)
    mods = [mod_steps(l, [c]) for c in range(4, 12)]
    pads = [("V", ("pads", l)), ("S", ("lamexp", l)), ("V", ("lam", l))]
    if l == 0:
        net, spectrum = filter_groups(l)
        o = pads + merge(net, [mod_steps(l, [c]) for c in (0, 1)]) + norm_steps(l, 1, range(TILES))
        o += merge(spectrum, [mod_steps(l, [c]) for c in (2, 3)]) + modulated_steps(l, 1)
    else:
        o = norm_steps(l, 1, range(TILES)) + mods[0] + mods[1] + modulated_steps(l, 1) + pads
        mods[:2] = [], []
    for j in (2, 3, 0, 1):
        o += [("T", ("zD", l, j)), ("S" if j >= 2 else "V", ("zDout", l, j))]
    zb = [[("T", ("zB", l, j)), ("S", ("zBout", l, j))] for j in range(6)]
    o += [("V", ("cfconv", l, 0, 0))] + zb[0] + zb[1]
    o += [("V", ("hyconv", l, 0)), ("V", ("hyconv", l, 1)), ("V", ("cfconv", l, 0, 1))] + zb[2] + zb[3]
    o += mods[0] + [("V", ("hyconv", l, 2)), ("V", ("hyconv", l, 3)), ("V", ("cfconv", l, 1, 0))] + mods[1] + zb[4] + zb[5]
    o += mods[2] + [("V", ("hyconv", l, 4)), ("V", ("hyconv", l, 5)), ("V", ("vx", l)), ("V", ("cfconv", l, 1, 1))]
    o += mods[3] + mods[4]
    for i in range(2):
        o += [("T", ("vxT", l, i)), ("S", ("vxTout", l, i))]
    o += mods[5]
    o += [("T", ("lnmean", l)), ("V", ("xc", l)), ("S", ("xcsq", l)), ("T", ("dft", l, 0)), ("S", ("dftout", l, 0))]
    o += mods[6] + [("T", ("lnvar", l))] + mods[7][:2] + [("V", ("lnv", l)), ("S", ("lntanh", l))] + mods[7][2:3]
    o += [("T", ("dft", l, 1)), ("S", ("dftout", l, 1))] + mods[7][3:] + [("V", ("lnout", l))]
    hy = []
    for f in range(2, 4):
        hy += [[("T", ("dft", l, f)), ("S", ("dftout", l, f))]]
    hy[-1] += [("V", ("spec", l))]
    for c in range(2):
        hy += [[("T", ("idft", l, c)), ("V", ("hyout", l, c))]]

    def gate_groups(bi, first):
        out = []
        for j in range(KD):
            out += [[("T", ("gate", l, bi, j)), ("S", ("gtanh", l, bi, j))],
                    [("T", ("br", l, bi, j)), ("V", ("gmul", l, bi, j))]
                    + ([] if first else [("P", ("gadd", l, bi, j))])]
        return out

    conformer = gate_groups(3, True)
    o += merge(conformer[:KD], hy)
    for t in range(TILES):
        if t < tt:
            o += [("T", ("zAq", l, t)), ("S", ("zAqout", l, t))]
        o += [("T", ("zAk", l, t)), ("S", ("zAkout", l, t)), ("P", ("sqA", l, t)), ("V", ("ssA", l, t))]
    o += [("V", ("rsA", l))]
    projections = [[("T", ("zC", l, t)), ("S", ("zCout", l, t)), ("P", ("sqC", l, t)), ("V", ("ssC", l, t))]
                   for t in range(TILES)]

    def prepared(b):
        groups = [[("V", ("rope" + b, l, t))] for t in range(TILES)]
        turns = [[("T", ("qkT" + b, l, t)), ("S", ("qkTout" + b, l, t))] for t in range(TILES)]
        return groups[:2] + [g for t in range(TILES - 2) for g in (groups[t + 2], turns[t])] + turns[-2:]

    def attention(b):
        units = [(t, h) for t in range(tt) for h in range(4)]
        groups, turn = [], []
        for i in range(len(units) + 1):
            if i < len(units):
                t, h = units[i]
                groups += [[("T", ("s" + b, l, t, h, n)) for n in range(2 if b == "A" else 1)]]
            if i:
                groups[-1] += [("V", ("p" + b, l, *units[i - 1]))]
            if i < len(units):
                groups[-1] += [("V", ("mx" + b, l, t, h)), ("S", ("ex" + b, l, t, h))]
            if i:
                t, h = units[i - 1]
                groups += turn
                turn = []
                groups += [[("T", ("pT" + b, l, t, h)), ("S", ("pTout" + b, l, t, h))]]
                if h == 3 and b == "C":
                    groups += [[("T", ("yC", l, t)), ("S", ("yToutC", l, t))]]
                elif h == 3:
                    groups += [[("T", ("y" + b, l, t)), ("V", ("yn" + b, l, t))]]
                    turn = [[("T", ("yT" + b, l, t)), ("S", ("yTout" + b, l, t))]]
        return groups + turn

    ahead = []
    for c in range(4 if l + 1 < DEPTH else 0):
        steps = mod_steps(l + 1, [c])
        ahead += [steps[:2], steps[2:]]
    o += merge(conformer[KD:] + projections + spread(gate_groups(1, False), ahead),
               prepared("A") + attention("A") + [[("V", ("rsC", l))]] + prepared("C"))
    o += merge(gate_groups(0, False), attention("C"))
    net, spectrum = filter_groups(l + 1) if l + 1 < DEPTH else ([], [])
    o += merge(gate_groups(2, False), net)
    o += gate_steps(l, (4, 5))
    for t in range(tt):
        for hf in range(2):
            o += [("T", ("wo", l, t, hf))]
            if t == tt - 1 and hf == 1:
                o += [("S", ("sq", l, 2, u)) for u in range(t)] + [("V", ("rstd", l, 2, 0, t))]
            o += [("V", ("xup", l, t, hf))]
    o += [("S" if t % 2 else "V", ("xn", l, 2, t)) for t in range(tt - 1)]
    o += norm_steps(l, 2, [tt - 1]) + modulated_steps(l, 2)
    o += [("T", ("lg", l)), ("S", ("lgrow", l)), ("T", ("lgT", l)), ("V", ("lgout", l))]
    o += [("V", ("route1", l)), ("S", ("rexp1", l)), ("V", ("route2", l)), ("S", ("rexp2", l)), ("V", ("route3", l))]
    for t in range(tt):
        for hf in range(2):
            o += [("T", ("hb", l, t, hf)), ("S", ("hbout", l, t, hf))]
        o += [("S", ("hstore", l, t))]
    o += [("T", ("rank", l)), ("V", ("slots", l)), ("P", ("list", l))]
    o += gate_steps(l, (10, 11))
    for g in spectrum:
        o += g
    o += [("T", ("experts", l)), ("S", ("experts", l)), ("V", ("experts", l)), ("P", ("experts", l))]
    for t in range(tt):
        o += [("S", ("weigh", l, t)), ("V", ("xup2", l, t))]
    return o


def chunks_of(name):
    kind, l, rest = name[0], name[1], name[2:]
    if kind == "mod":
        return [("wmod", l, rest[0])]
    if kind == "fdft":
        return [("fdft", l)]
    if kind in ("zD", "zAq", "zAk", "zC"):
        return [("win", l, {"zD": 0, "zAq": 3, "zAk": 4, "zC": 5}[kind])]
    if kind == "zB":
        return [("win", l, 1 + rest[0] // 4)]
    if kind == "gate":
        return [("win", l, 6 + 2 * rest[0] + rest[1] // 4)]
    if kind == "br":
        return [("wbr", l, rest[0])]
    if kind == "wo":
        return [("wout", l, rest[1])]
    if kind == "experts":
        return [("w1", l), ("w3", l), ("w2", l)]
    return []


ORDER = [("S", ("silu", 0))] + [s for l in range(DEPTH) for s in layer_order(l)]
STEPS = {e: [n for x, n in ORDER if x == e] for e in "TVSP"}
COUNT = {e: {n: i + 1 for i, n in enumerate(STEPS[e])} for e in "TVSP"}


def plan_ring():
    last = {c: n for n in STEPS["T"] for c in chunks_of(n)}
    chunks = list(dict.fromkeys(c for n in STEPS["T"] for c in chunks_of(n)))
    first = {}
    for n in STEPS["T"]:
        for c in chunks_of(n):
            first.setdefault(c, COUNT["T"][n])
    held, places, before = [None] * RING, [], []
    for i, c in enumerate(chunks):
        until = [0 if h is None else COUNT["T"][last[chunks[h]]] for h in held]
        p = until.index(min(until))
        assert until[p] < first[c], c
        places.append(p)
        before.append(held[p])
        held[p] = i
    return [(c, last[c]) for c in chunks], places, before


CHUNKS, PLACE, BEFORE = plan_ring()
CHUNK_AT = {name: i for i, (name, _) in enumerate(CHUNKS)}


def loads_before(i):
    return sum(NE if CHUNKS[j][0][0] in ("w1", "w3", "w2") else 1 for j in range(i) if PLACE[j] == PLACE[i])


def readers(name):
    kind, l, rest = name[0], name[1], name[2:]
    one = {"mod": ("S", "modrow"), "modT": ("V", "modcol"), "modB": ("V", "modgate"),
           "zB": ("S", "zBout"), "hf": ("V", "hfarg"), "hf4": ("V", "hfwin"), "fnorm": ("V", "fnorms"),
           "fdft": ("S", "fdftout"), "lnmean": ("V", "xc"), "lnvar": ("V", "lnv"), "vxT": ("S", "vxTout"),
           "dft": ("S", "dftout"), "idft": ("V", "hyout"), "gate": ("S", "gtanh"), "br": ("V", "gmul"),
           "zAq": ("S", "zAqout"), "zAk": ("S", "zAkout"), "zC": ("S", "zCout"),
           "qkTA": ("S", "qkToutA"), "qkTC": ("S", "qkToutC"), "pTA": ("S", "pToutA"), "pTC": ("S", "pToutC"),
           "yA": ("V", "ynA"), "yC": ("S", "yToutC"), "yTA": ("S", "yToutA"),
           "wo": ("V", "xup"), "lg": ("S", "lgrow"), "lgT": ("V", "lgout"), "hb": ("S", "hbout"), "rank": ("V", "slots")}
    if kind in one:
        e, k = one[kind]
        return [(e, (k, l, *rest))]
    if kind == "hT":
        return [("V" if rest[1] % 2 else "S", ("hTout", l, *rest))]
    if kind == "zD":
        return [("S" if rest[0] >= 2 else "V", ("zDout", l, *rest))]
    if kind in ("sA", "sC"):
        return [("S", ("ex" + kind[1], l, *rest[:2]))]
    if kind == "experts":
        return [("V", ("experts", l)), ("S", ("experts", l))]
    raise KeyError(kind)


def bank_of(name):
    return (COUNT["T"][name] - 1) % BANKS


def check_order():
    at = {s: i for i, s in enumerate(ORDER)}
    for i in range(BANKS, len(STEPS["T"])):
        for s in readers(STEPS["T"][i - BANKS]):
            assert at[s] < at[("T", STEPS["T"][i])], (STEPS["T"][i], s)


check_order()


def build_trunk(nc, xin, ccol, const, cols, rows, hfw, wr, fdft, wmod, win, wbr, wout, w1, w3, w2, out):
    with ExitStack() as ctx:
        def sb(name, shape, dt=F32):
            return ctx.enter_context(nc.sbuf_tensor(name, shape, dt))

        def sem(name):
            return ctx.enter_context(nc.semaphore(name))

        x = sb("x", [P, TILES, D])
        hT = sb("hT", [P, KD, 512])
        con = sb("con", [P, NCONST])
        col = sb("col", [P, DEPTH, NC])
        row = sb("row", [P, NR * DEPTH])
        hw = sb("hw", [64, HF_COLS])
        wrt = sb("wrt", [P, DEPTH, KD, 32])
        cc = sb("cc", [P, KD * 32])
        ring = sb("ring", [P, RING, WCH])
        wide = sb("wide", [P, 4 * D])
        yT = sb("yT", [P, 2, 2, 512])
        gth = sb("gth", [P, 2, 512])
        gtmp = sb("gtmp", [P, 2, 512])
        ct = gtmp[:, 0, 0:KD * 32]
        mr = sb("mr", [P, 2, 512])
        mod = sb("mod", [P, DEPTH, 6, KD, 2])
        modt = sb("modt", [P, 4, 2])
        amp = sb("amp", [P, KD, 2])
        hbg = sb("hbg", [P, 32])
        ss = sb("ss", [P, 4])
        small = sb("small", [P, 3, 64])
        lamt = sb("lamt", [P, 72])
        nlam = sb("nlam", [P, 4])
        mx = sb("mx", [P, 2, 2])
        nm = sb("nm", [P, 2, 2])
        sums = sb("sums", [P, 2, 2])
        esk = sb("esk", [P, 2])
        rr = sb("rr", [P, 2])
        den = sb("den", [P, 4])
        rden = sb("rden", [P, 4])
        fn = sb("fn", [P, 2])
        ssa = sb("ssa", [P, TILES, 16])
        ssc = sb("ssc", [P, TILES, 6])
        rsa = sb("rsa", [P, TILES, 16])
        rsc = sb("rsc", [P, TILES, 6])
        m = sb("m", [P, 9736])
        n_ = sb("n_", [P, 5240])

        def part(t, at, *shape):
            size = int(np.prod(shape))
            ap = t[:, at:at + size]
            if len(shape) == 2:
                return ap.rearrange("p (a b) -> p a b", a=shape[0])
            if len(shape) == 3:
                return ap.rearrange("p (a b c) -> p a b c", a=shape[0], b=shape[1])
            return ap
        zb = part(m, 0, 2, 2, 258)
        hu = part(m, 1032, 6, 2, 256)
        us = part(m, 4104, 4, 512)
        ysp = part(m, 6152, 4, 512)
        fs = part(m, 8200, 6, 256)
        hfarg = part(m, 6144, 256)
        hfk = part(m, 6400, 256)
        hfa = part(m, 6656, 2, 256)
        hf2 = part(m, 5120, 2, 512)
        hf = part(m, 4096, 2, 512)
        ut = part(m, 2056, 2, 512)
        za = part(m, 0, TILES, 768)
        zc = part(m, 3072, TILES, 512)
        qkta = part(m, 5120, 4, 512)
        qktc = part(m, 7168, 3, 512)
        sq = part(m, 8704, 2, 512)
        rt = part(n_, 4608, 2, 256)
        gbc = part(m, 0, 2, D)
        xg = part(m, 2048, D)
        xgT = part(m, 3072, KD, P)
        u = part(m, 4096, FE)
        uT = part(m, 4608, 4, P)
        eth = part(m, 5120, FE)
        es = part(m, 5632, FE)
        ysb = part(m, 6144, D)
        lg = part(m, 7168, TILES, 20)
        rtmp = part(m, 7296, 12, 16)
        rt16 = part(m, 7488, TILES, 16)
        pick = part(m, 7552, 2, TILES * NE)
        both = part(m, 7952, TILES + 2, NE)
        ranks = part(m, 7744, TILES, NE)
        picked = part(m, 7808, TILES, NE)
        pw = part(m, 7872, 2, TILES)
        choice = part(m, 7880, 4, TILES)
        slotf = part(m, 7896, 4, TILES)
        idx = part(m, 7912, 4 * TILES).bitcast(U32)
        tok = part(m, 7928, TILES).bitcast(U32)
        lst = part(m, 7932, NE).bitcast(U32)
        idx1 = part(m, 7948, 1).bitcast(U32)
        most = part(m, 7949, 1)
        flag = part(m, 7950, 1).bitcast(I32)
        ud = part(n_, 0, 2, 2, 286)
        cv = part(n_, 1144, 2, 512)
        thd = part(n_, 2168, 2, 512)
        sqd = part(n_, 3192, 2, 512)
        rsd = part(n_, 4216, 2, 512)
        ee = part(n_, 0, 2, 2, 512)
        pt = part(n_, 2048, 4, 512)
        yn = part(n_, 4096, 256)
        ynq = part(n_, 4352, 256)

        zero = sb("zero", [P, 64])
        y2 = hT[:, :, :].rearrange("p k n -> p (k n)").rearrange("p (t d) -> p t d", t=4)
        xn = wide[:, :].rearrange("p (t d) -> p t d", t=4)
        acc = wide[:, :].rearrange("p (k n) -> p k n", k=KD)
        ps = ctx.enter_context(nc.psum_tensor("ps", [P, BANKS, 512], F32))

        h2_dram = nc.dram_tensor("h2_scratch", (TILES * P, D), F32, kind="Internal").ap()
        y_dram = nc.dram_tensor("y_scratch", (TILES * NE * P, D), F32, kind="Internal").ap()
        list_dram = nc.dram_tensor("list_scratch", (TILES * P * NE, 1), U32, kind="Internal").ap()

        def c(name, cols_=None):
            at, n = CONST_AT[name]
            return con[:, at:at + n]
        ident = c("ident")
        dft_c = c("dft").rearrange("p (a b) -> p a b", a=2)
        idft_c = c("idft").rearrange("p (a b) -> p a b", a=4)
        win_c = c("win").rearrange("p (a b) -> p a b", a=2)
        mask_c = c("mask").rearrange("p (a b) -> p a b", a=2)

        def rowp(l, at, n):
            return row[:, l * NR + at:l * NR + at + n]

        def streams(l):
            return live(l) // 2

        def bank(name):
            return ps[:, bank_of(name), :]

        tensor_done, vector_done, scalar_done, pool_done = (
            sem("tensor_done"), sem("vector_done"), sem("scalar_done"), sem("pool_done"))
        vector_chain = sem("vector_chain")
        params_landed = sem("params_landed")
        x_landed = sem("x_landed")
        hfw_landed = sem("hfw_landed")
        const_landed = sem("const_landed")
        chunk_landed = [sem(f"chunk_landed{i}") for i in range(RING)]
        out_stored = sem("out_stored")
        list_cleared = sem("list_cleared")
        h2_stored = sem("h2_stored")
        list_scattered = sem("list_scattered")
        list_landed = sem("list_landed")
        index_ready = sem("index_ready")
        waited = sem("waited")
        tokens_gathered = sem("tokens_gathered")
        tokens_turned = sem("tokens_turned")
        turned_low = sem("turned_low")
        turned_high = sem("turned_high")
        gate_done = sem("gate_done")
        up_done = sem("up_done")
        tanh_ready = sem("tanh_ready")
        gate_ready = sem("gate_ready")
        u_ready = sem("u_ready")
        u_turned = sem("u_turned")
        uT_ready = sem("uT_ready")
        down_low = sem("down_low")
        down_high = sem("down_high")
        y_low = sem("y_low")
        y_high = sem("y_high")
        y_stored = sem("y_stored")
        y_gathered = [sem(f"y_gathered{t}") for t in range(TILES)]
        more_landed = [sem(f"more_landed{l}") for l in range(DEPTH)]
        more_list = [sem(f"more_list{l}") for l in range(DEPTH)]
        more_index = [sem(f"more_index{l}") for l in range(DEPTH)]
        more_gathered = [sem(f"more_gathered{l}") for l in range(DEPTH)]
        more_tensor = [sem(f"more_tensor{l}") for l in range(DEPTH)]
        more_vector = [sem(f"more_vector{l}") for l in range(DEPTH)]
        more_scalar = [sem(f"more_scalar{l}") for l in range(DEPTH)]
        more_stored = [sem(f"more_stored{l}") for l in range(DEPTH)]
        done_of = {"T": tensor_done, "V": vector_done, "S": scalar_done, "P": pool_done}

        def tensor(*name):
            return COUNT["T"][name]

        def vector(*name):
            return COUNT["V"][name]

        def scalar(*name):
            return COUNT["S"][name]

        def pool(*name):
            return COUNT["P"][name]

        def chunk(name):
            return ring[:, PLACE[CHUNK_AT[name]], :]

        def chunk3(name, n=KD):
            return chunk(name).rearrange("p (k n) -> p k n", k=n)

        def landed(name):
            return 16 * (loads_before(CHUNK_AT[name]) + 1)

        def assignments(eng, l):
            eng.wait_ge(vector_done, vector("slots", l))
            return eng.value_load(flag[0:1, 0:1], min_val=0, max_val=TILES * P)

        block = ctx.enter_context(nc.Block())

        @block.sync
        def _(sp):
            source = {"wmod": wmod, "win": win, "wbr": wbr, "wout": wout}
            experts_weights = {"w1": w1, "w3": w3, "w2": w2}
            sp.dma_start(cc[:], ccol).then_inc(params_landed, 16)
            for t_, a in ((col[:], cols), (row[:], rows), (wrt[:], wr)):
                sp.dma_start(t_, a).then_inc(params_landed, 16)
            sp.dma_start(con[:], const).then_inc(const_landed, 16)
            sp.dma_start(hw[:], hfw[0]).then_inc(hfw_landed, 16)
            for i, (name, _) in enumerate(CHUNKS):
                if BEFORE[i] is not None:
                    old, last = CHUNKS[BEFORE[i]]
                    if old[0] in experts_weights:
                        sp.wait_ge(y_gathered[live(old[1]) - 1], 32 * (old[1] + 1))
                    if old[0] == "w1":
                        sp.wait_ge(gate_done, (old[1] + 1) * NE)
                    elif old[0] == "w3":
                        sp.wait_ge(up_done, (old[1] + 1) * NE)
                    elif old[0] == "w2":
                        sp.wait_ge(down_high, (old[1] + 1) * NE)
                    else:
                        sp.wait_ge(tensor_done, tensor(*last))
                place = ring[:, PLACE[i], :]
                here = chunk_landed[PLACE[i]]
                if name[0] in experts_weights:
                    l = name[1]
                    sp.dma_start(place, experts_weights[name[0]][l, 0]).then_inc(here, 16)
                    if name[0] != "w2":
                        continue
                    at = {w: (chunk((w, l)), chunk_landed[PLACE[CHUNK_AT[(w, l)]]])
                          for w in experts_weights}
                    sp.wait_ge(gate_done, l * NE + 1)
                    sp.dma_start(at["w1"][0], w1[l, 1]).then_inc(at["w1"][1], 16)
                    sp.wait_ge(up_done, l * NE + 1)
                    sp.dma_start(at["w3"][0], w3[l, 1]).then_inc(at["w3"][1], 16)
                    with sp.Fori(2, NE) as e:
                        sp.wait_ge(gate_done, l * NE + e)
                        sp.dma_start(at["w1"][0], w1[l, e]).then_inc(at["w1"][1], 16)
                        sp.wait_ge(up_done, l * NE + e)
                        sp.dma_start(at["w3"][0], w3[l, e]).then_inc(at["w3"][1], 16)
                        sp.wait_ge(down_high, l * NE + e - 1)
                        sp.dma_start(at["w2"][0], w2[l, e - 1]).then_inc(at["w2"][1], 16)
                    sp.wait_ge(down_high, (l + 1) * NE - 1)
                    sp.dma_start(at["w2"][0], w2[l, NE - 1]).then_inc(at["w2"][1], 16)
                    count = assignments(sp, l)
                    with sp.If(count > P):
                        sp.wait_ge(down_high, (l + 1) * NE)
                        with sp.Fori(0, live(l) - 1) as b:
                            with sp.Fori(0, NE) as e:
                                sp.dma_start(at["w1"][0], w1[l, e]).then_inc(more_landed[l], 16)
                                sp.dma_start(at["w3"][0], w3[l, e]).then_inc(more_landed[l], 16)
                                sp.dma_start(at["w2"][0], w2[l, e]).then_inc(more_landed[l], 16)
                                sp.wait_ge(more_vector[l], b * (4 * NE) + e * 4 + 4)
                                rows_at = y_dram.rearrange("(b e p) d -> b e p d", e=NE, p=P)
                                sp.dma_start(rows_at[b + 1, e], ysb).then_inc(more_stored[l], 16)
                                sp.wait_ge(more_stored[l], b * (16 * NE) + e * 16 + 16)
                                sp.sem_inc(waited, 1)
                    continue
                src = fdft if name[0] == "fdft" else source[name[0]][name[1], name[2]]
                width = src.shape[1]
                if name[0] == "win" and name[2] in (2, 3):
                    width = WCH // 2
                sp.dma_start(place[:, 0:width], src[:, 0:width]).then_inc(here, 16)
                if i == 1:
                    sp.dma_start(x[:], xin).then_inc(x_landed, 16)
                if name == ("wbr", 0, 2):
                    sp.wait_ge(tensor_done, tensor("hf4", 0, 1))
                    sp.dma_start(hw[:], hfw[1]).then_inc(hfw_landed, 16)
            for t in range(2):
                sp.wait_ge(vector_done, vector("xup2", DEPTH - 1, t))
                sp.dma_start(out[t * P:(t + 1) * P, :], x[:, t, :]).then_inc(out_stored, 16)
            sp.wait_ge(out_stored, 32)

        @block.tensor
        def _(pe):
            seen = set()

            def use(name):
                if name not in seen:
                    seen.add(name)
                    i = CHUNK_AT[name]
                    pe.wait_ge(chunk_landed[PLACE[i]], landed(name))

            pe.wait_ge(const_landed, 16)
            pe.wait_ge(params_landed, 16 * 4)
            for n, name in enumerate(STEPS["T"]):
                kind, l, rest = name[0], name[1], name[2:]
                W = 128 * live(l)
                b = ps[:, n % BANKS, :]
                if n >= BANKS:
                    for e, r in readers(STEPS["T"][n - BANKS]):
                        pe.wait_ge(done_of[e], COUNT[e][r])
                if kind == "mod":
                    (ch,) = rest
                    use(("wmod", l, ch))
                    if n == 0:
                        pe.wait_ge(vector_done, COUNT["V"][("pads", 0)])
                    w = chunk3(("wmod", l, ch))
                    for k in range(KD):
                        g = 32 * (k % 4)
                        last = pe.matmul(b[g:g + 32, :], cc[:, 32 * k:32 * k + 32], w[:, k, :],
                                         start=(k < 4), stop=(k >= 4), skip_group_check=True)
                    last.then_inc(tensor_done, 1)
                elif kind == "modT":
                    pe.wait_ge(scalar_done, scalar("modrow", l, *rest))
                    for j in range(4):
                        last = pe.transpose(b[:, j * P:(j + 1) * P], mr[:, rest[0] % 2, j * P:(j + 1) * P], ident)
                    last.then_inc(tensor_done, 1)
                elif kind == "modB":
                    ch, v = rest
                    pe.wait_ge(vector_done, vector("modcol", l, ch))
                    for k in range(4):
                        gate = mod[:, l, ch // 2, ch % 2 * 4 + k, v:v + 1]
                        last = pe.matmul(b[:, k * P:(k + 1) * P], gate.broadcast_to([P, P]), ident, start=True, stop=True)
                    last.then_inc(tensor_done, 1)
                elif kind == "hT":
                    nn, k = rest
                    T = TILES if nn == 1 else live(l)
                    for t in range(T):
                        if t % 2:
                            pe.wait_ge(scalar_done, scalar("xn", l, nn, t))
                        else:
                            pe.wait_ge(vector_done, vector("xn", l, nn, t))
                    for t in range(T):
                        last = pe.transpose(b[:, t * P:(t + 1) * P], xn[:, t, k * P:(k + 1) * P], ident)
                    last.then_inc(tensor_done, 1)
                elif kind in ("zD", "zB", "gate"):
                    if kind == "gate":
                        bi, j = rest
                        cn = ("win", l, 6 + 2 * bi + j // 4)
                        jj = j % 4
                    elif kind == "zD":
                        cn, jj = ("win", l, 0), rest[0]
                    else:
                        cn, jj = ("win", l, 1 + rest[0] // 4), rest[0] % 4
                    use(cn)
                    cols_ = 256 if cn[2] == 2 else 512
                    w = chunk(cn)[:, 0:KD * cols_].rearrange("p (k n) -> p k n", k=KD)
                    pe.wait_ge(scalar_done, scalar("hTout", l, 1, KD - 2))
                    pe.wait_ge(vector_done, vector("hTout", l, 1, KD - 1))
                    for k in range(KD):
                        last = pe.matmul(b[:, 0:W], w[:, k, jj * P:(jj + 1) * P], hT[:, k, 0:W],
                                         start=(k == 0), stop=(k == KD - 1))
                    last.then_inc(tensor_done, 1)
                elif kind in ("zAq", "zAk", "zC"):
                    (t,) = rest
                    cn = ("win", l, {"zAq": 3, "zAk": 4, "zC": 5}[kind])
                    use(cn)
                    wid = 256 if kind == "zAq" or (kind == "zC" and t >= live(l)) else 512
                    w = chunk(cn)[:, 0:KD * (256 if kind == "zAq" else 512)].rearrange("p (k n) -> p k n", k=KD)
                    for k in range(KD):
                        last = pe.matmul(b[:, 0:wid], hT[:, k, t * P:(t + 1) * P], w[:, k, 0:wid],
                                         start=(k == 0), stop=(k == KD - 1))
                    last.then_inc(tensor_done, 1)
                elif kind == "hf":
                    (i,) = rest
                    pe.wait_ge(hfw_landed, 16 * (l + 1))
                    if i == 1:
                        last = pe.matmul(b[0:64, 0:256], hw[0:33, 0:64], c("feat")[0:33, :], start=True, stop=True)
                    else:
                        pe.wait_ge(scalar_done, scalar("hfsin", l, i - 1))
                        last = pe.matmul(b[0:64, 0:256], hw[0:64, 64 * (i - 1):64 * i], hfa[0:64, (i - 1) % 2, :],
                                         start=True, stop=True)
                    last.then_inc(tensor_done, 1)
                elif kind == "hf4":
                    pe.wait_ge(scalar_done, scalar("hfsin", l, 3))
                    last = pe.matmul(b, hfa[0:64, 1, rest[0] * P:(rest[0] + 1) * P], hw[0:64, 192:704],
                                     start=True, stop=True)
                    last.then_inc(tensor_done, 1)
                elif kind == "fnorm":
                    pe.wait_ge(scalar_done, scalar("hfsq", l, 1))
                    for cch in range(2):
                        for i in range(2):
                            for side in range(2):
                                at = side * 256 + cch * P
                                last = pe.matmul(b[:, cch:cch + 1], hf2[:, i, at:at + P], c("mean")[:, 0:1],
                                                 start=(i + side == 0), stop=(i + side == 2))
                    last.then_inc(tensor_done, 1)
                elif kind == "fdft":
                    (j,) = rest
                    use(("fdft", l))
                    pe.wait_ge(vector_done, vector("hfwin", l, 1))
                    fd = chunk(("fdft", l))
                    for side in range(2):
                        for i in range(2):
                            at = (side * 2 + i) * 768 + j * P
                            last = pe.matmul(b[:, 0:256], fd[:, at:at + P], hf[:, i, side * 256:(side + 1) * 256],
                                             start=(side + i == 0), stop=(side + i == 2))
                    last.then_inc(tensor_done, 1)
                elif kind in ("lnmean", "lnvar"):
                    if kind == "lnmean":
                        pe.wait_ge(vector_done, vector("cfconv", l, 1, 1))
                        src = cv
                    else:
                        pe.wait_ge(scalar_done, scalar("xcsq", l))
                        src = sqd
                    for j in range(2):
                        last = pe.matmul(b[:, 0:W], c("mean"), src[:, j, 0:W], start=(j == 0), stop=(j == 1))
                    last.then_inc(tensor_done, 1)
                elif kind == "vxT":
                    (i,) = rest
                    pe.wait_ge(vector_done, vector("vx", l))
                    for s in range(streams(l)):
                        for cch in range(2):
                            at = s * 256 + cch * P
                            last = pe.transpose(b[:, at:at + P], hu[:, 4 + cch, s, i * P:(i + 1) * P], ident)
                    last.then_inc(tensor_done, 1)
                elif kind == "dft":
                    (f,) = rest
                    pe.wait_ge(scalar_done, scalar("vxTout", l, 1))
                    for i in range(2):
                        last = pe.matmul(b[:, 0:W], dft_c[:, i, f * P:(f + 1) * P], ut[:, i, 0:W],
                                         start=(i == 0), stop=(i == 1))
                    last.then_inc(tensor_done, 1)
                elif kind == "idft":
                    (cch,) = rest
                    pe.wait_ge(vector_done, vector("spec", l))
                    for s in range(streams(l)):
                        for f in range(4):
                            at = s * 256 + cch * P
                            last = pe.matmul(b[:, s * 256:(s + 1) * 256], ysp[:, f, at:at + P], idft_c[:, f, :],
                                             start=(f == 0), stop=(f == 3))
                    last.then_inc(tensor_done, 1)
                elif kind == "br":
                    bi, j = rest
                    use(("wbr", l, bi))
                    if bi == 3:
                        pe.wait_ge(vector_done, vector("lnout", l))
                    elif bi == 1:
                        pe.wait_ge(vector_done, vector("hyout", l, 1))
                    else:
                        pe.wait_ge(scalar_done, scalar("yTout" + ("A" if bi == 0 else "C"), l, live(l) - 1))
                    w = chunk(("wbr", l, bi))[:, 0:2 * D].rearrange("p (k n) -> p k n", k=2)
                    for k in range(2):
                        last = pe.matmul(b[:, 0:W], w[:, k, j * P:(j + 1) * P], yT[:, bi in (1, 2), k, 0:W],
                                         start=(k == 0), stop=(k == 1))
                    last.then_inc(tensor_done, 1)
                elif kind == "qkTA":
                    (t,) = rest
                    pe.wait_ge(vector_done, vector("ropeA", l, t))
                    for j in range(0 if t < live(l) else 2, 4):
                        last = pe.transpose(b[:, j * P:(j + 1) * P], za[:, t, j * P:(j + 1) * P], ident)
                    last.then_inc(tensor_done, 1)
                elif kind == "qkTC":
                    (t,) = rest
                    pe.wait_ge(vector_done, vector("ropeC", l, t))
                    for j in range(3 if t < live(l) else 1):
                        at = 0 if j == 0 else 256 + (j - 1) * P
                        last = pe.transpose(b[:, j * P:(j + 1) * P], zc[:, t, at:at + P], ident)
                    last.then_inc(tensor_done, 1)
                elif kind == "sA":
                    t, h, i = rest
                    pe.wait_ge(scalar_done, scalar("qkToutA", l, TILES - 1))
                    k0 = 0 if t < 2 else 256
                    r = slice(32 * h, 32 * h + 32)
                    last = pe.matmul(b[:, 0:512 - k0], qkta[r, i, t * P:(t + 1) * P], qkta[r, 2 + i, k0:512],
                                     start=True, stop=True)
                    last.then_inc(tensor_done, 1)
                elif kind == "sC":
                    t, h, _ = rest
                    pe.wait_ge(scalar_done, scalar("qkToutC", l, TILES - 1))
                    k0 = 0 if t < 2 else 256
                    r = slice(64 * (h // 2), 64 * (h // 2) + 64)
                    last = pe.matmul(b[:, 0:512 - k0], qktc[r, 1 + h % 2, t * P:(t + 1) * P], qktc[r, 0, k0:512],
                                     start=True, stop=True)
                    last.then_inc(tensor_done, 1)
                elif kind in ("pTA", "pTC"):
                    t, h = rest
                    pe.wait_ge(vector_done, vector("p" + kind[2], l, t, h))
                    for k in range(4 if t < 2 else 2):
                        last = pe.transpose(b[:, k * P:(k + 1) * P], ee[:, (t * 4 + h) % 2, 0, k * P:(k + 1) * P], ident)
                    last.then_inc(tensor_done, 1)
                elif kind == "yA":
                    (t,) = rest
                    pe.wait_ge(scalar_done, scalar("pToutA", l, t, 3))
                    k0, nk = (0, 4) if t < 2 else (2, 2)
                    for h in range(4):
                        for k in range(nk):
                            last = pe.matmul(b[:, h * 64:(h + 1) * 64], pt[:, h, k * P:(k + 1) * P],
                                             za[:, k0 + k, 512 + h * 64:576 + h * 64], start=(k == 0), stop=(k == nk - 1))
                    last.then_inc(tensor_done, 1)
                elif kind == "yC":
                    (t,) = rest
                    pe.wait_ge(scalar_done, scalar("pToutC", l, t, 3))
                    k0, nk = (0, 4) if t < 2 else (2, 2)
                    for j in range(2):
                        for k in range(nk):
                            for half in range(2):
                                last = pe.matmul(b[half * 64:half * 64 + 64, j * P:(j + 1) * P],
                                                 zc[:, k0 + k, 128 + j * 64:192 + j * 64],
                                                 pt[:, 2 * j + half, k * P:(k + 1) * P],
                                                 start=(k == 0), stop=(k == nk - 1), skip_group_check=True)
                    last.then_inc(tensor_done, 1)
                elif kind == "yTA":
                    (t,) = rest
                    pe.wait_ge(vector_done, vector("ynA", l, t))
                    for j in range(2):
                        last = pe.transpose(b[:, j * P:(j + 1) * P], yn[:, j * P:(j + 1) * P], ident)
                    last.then_inc(tensor_done, 1)
                elif kind == "wo":
                    t, half = rest
                    use(("wout", l, half))
                    pe.wait_ge(pool_done, pool("gadd", l, 2, KD - 1))
                    w = chunk3(("wout", l, half))
                    for k in range(KD):
                        last = pe.matmul(b, acc[:, k, t * P:(t + 1) * P], w[:, k, :], start=(k == 0), stop=(k == KD - 1))
                    last.then_inc(tensor_done, 1)
                elif kind == "lg":
                    pe.wait_ge(scalar_done, scalar("hTout", l, 2, KD - 2))
                    pe.wait_ge(vector_done, vector("hTout", l, 2, KD - 1))
                    for k in range(KD):
                        g = 32 * (k % 4)
                        last = pe.matmul(b[g:g + 32, 0:W], wrt[:, l, k, :], hT[:, k, 0:W],
                                         start=(k < 4), stop=(k >= 4), skip_group_check=True)
                    last.then_inc(tensor_done, 1)
                elif kind == "lgT":
                    pe.wait_ge(scalar_done, scalar("lgrow", l))
                    for t in range(live(l)):
                        last = pe.transpose(b[:, t * P:(t + 1) * P], mr[:, 0, t * P:(t + 1) * P], ident)
                    last.then_inc(tensor_done, 1)
                elif kind == "hb":
                    t, half = rest
                    for j in range(4):
                        last = pe.transpose(b[:, j * P:(j + 1) * P], hT[:, 4 * half + j, t * P:(t + 1) * P], ident)
                    last.then_inc(tensor_done, 1)
                elif kind == "rank":
                    pe.wait_ge(vector_done, vector("route3", l))
                    T = live(l)
                    pe.matmul(b[:, 0:(T + 1) * NE], c("mean"), both[:, 0:T + 1, :], start=True, stop=False,
                              skip_group_check=True)
                    for q in range(2, T + 1):
                        pe.matmul(b[:, q * NE:(T + 1) * NE], c("mean"), both[:, 1:T + 2 - q, :], start=False, stop=False,
                                  skip_group_check=True)
                    last = pe.matmul(b[:, 0:(T + 1) * NE], c("before"), both[:, 1:T + 2, :], start=False, stop=True,
                                     skip_group_check=True)
                    last.then_inc(tensor_done, 1)
                elif kind == "experts":
                    for q in range(1, BANKS):
                        for e_, r in readers(STEPS["T"][n - q]):
                            pe.wait_ge(done_of[e_], COUNT[e_][r])
                    base = l * NE
                    wg, wu, wd = chunk3(("w1", l)), chunk3(("w3", l)), chunk3(("w2", l), 4)
                    place = {w: chunk_landed[PLACE[CHUNK_AT[(w, l)]]] for w in ("w1", "w3", "w2")}
                    first = {w: landed((w, l)) for w in ("w1", "w3", "w2")}

                    def turn_tokens():
                        for k in range(KD):
                            last = pe.transpose(ps[:, k // 4, (k % 4) * P:(k % 4 + 1) * P], xg[:, k * P:(k + 1) * P], ident)
                        last.then_inc(tokens_turned, 1)

                    def gate_and_up(e):
                        pe.wait_ge(turned_low, base + e + 1)
                        pe.wait_ge(turned_high, base + e + 1)
                        if l or not isinstance(e, int):
                            pe.wait_ge(u_ready, base + e)
                        pe.wait_ge(place["w1"], first["w1"] + e * 16)
                        for k in range(KD):
                            last = pe.matmul(ps[:, 2, :], xgT[:, k, :], wg[:, k, :], start=(k == 0), stop=(k == KD - 1))
                        last.then_inc(gate_done, 1)
                        pe.wait_ge(place["w3"], first["w3"] + e * 16)
                        for k in range(KD):
                            last = pe.matmul(ps[:, 3, :], xgT[:, k, :], wu[:, k, :], start=(k == 0), stop=(k == KD - 1))
                        last.then_inc(up_done, 1)

                    def turn_u(e):
                        pe.wait_ge(u_ready, base + e + 1)
                        for f in range(4):
                            last = pe.transpose(ps[:, 4, f * P:(f + 1) * P], u[:, f * P:(f + 1) * P], ident)
                        last.then_inc(u_turned, 1)

                    def down(e):
                        pe.wait_ge(uT_ready, base + e + 1)
                        pe.wait_ge(place["w2"], first["w2"] + e * 16)
                        if l or not isinstance(e, int) or e:
                            pe.wait_ge(y_low, base + e)
                        for f in range(4):
                            last = pe.matmul(ps[:, 5, :], uT[:, f, :], wd[:, f, 0:512], start=(f == 0), stop=(f == 3))
                        last.then_inc(down_low, 1)
                        if l or not isinstance(e, int) or e:
                            pe.wait_ge(y_high, base + e)
                        for f in range(4):
                            last = pe.matmul(ps[:, 6, :], uT[:, f, :], wd[:, f, 512:D], start=(f == 0), stop=(f == 3))
                        last.then_inc(down_high, 1)

                    pe.wait_ge(tokens_gathered, 16 * (base + 1))
                    turn_tokens()
                    gate_and_up(0)
                    pe.wait_ge(tokens_gathered, 16 * (base + 2))
                    turn_tokens()
                    turn_u(0)
                    gate_and_up(1)
                    pe.wait_ge(tokens_gathered, 16 * (base + 3))
                    turn_tokens()
                    down(0)
                    turn_u(1)
                    with pe.Fori(2, NE - 1) as e:
                        gate_and_up(e)
                        pe.wait_ge(tokens_gathered, e * 16 + 16 * (base + 2))
                        turn_tokens()
                        down(e - 1)
                        turn_u(e)
                    gate_and_up(NE - 1)
                    down(NE - 2)
                    turn_u(NE - 1)
                    down(NE - 1)
                    pe.wait_ge(y_low, base + NE)
                    pe.wait_ge(y_high, base + NE)
                    count = assignments(pe, l)
                    with pe.If(count > P):
                        with pe.Fori(0, (live(l) - 1) * NE) as n_block:
                            pe.wait_ge(more_gathered[l], n_block * 16 + 16)
                            for k in range(KD):
                                last = pe.transpose(ps[:, k // 4, (k % 4) * P:(k % 4 + 1) * P], xg[:, k * P:(k + 1) * P], ident)
                            last.then_inc(more_tensor[l], 1)
                            pe.wait_ge(more_vector[l], n_block * 4 + 1)
                            pe.wait_ge(more_landed[l], n_block * 48 + 48)
                            for w, bnk in ((wg, 2), (wu, 3)):
                                for k in range(KD):
                                    last = pe.matmul(ps[:, bnk, :], xgT[:, k, :], w[:, k, :], start=(k == 0), stop=(k == KD - 1))
                            last.then_inc(more_tensor[l], 1)
                            pe.wait_ge(more_vector[l], n_block * 4 + 2)
                            for f in range(4):
                                last = pe.transpose(ps[:, 4, f * P:(f + 1) * P], u[:, f * P:(f + 1) * P], ident)
                            last.then_inc(more_tensor[l], 1)
                            pe.wait_ge(more_vector[l], n_block * 4 + 3)
                            for half in range(2):
                                for f in range(4):
                                    last = pe.matmul(ps[:, 5 + half, :], uT[:, f, :], wd[:, f, half * 512:(half + 1) * 512],
                                                     start=(f == 0), stop=(f == 3))
                            last.then_inc(more_tensor[l], 1)
                        pe.wait_ge(more_vector[l], (live(l) - 1) * NE * 4)
                    pe.nop().then_inc(tensor_done, 1)
                else:
                    raise KeyError(kind)

        @block.scalar
        def _(act):
            act.wait_ge(params_landed, 16 * 4)
            for n, name in enumerate(STEPS["S"]):
                kind, l, rest = name[0], name[1], name[2:]
                W = 128 * live(l)
                if n:
                    act.wait_ge(scalar_done, n)
                if kind == "silu":
                    last = act.activation(ct, cc[:], ACT.Tanh, scale=0.5)
                    last.then_inc(scalar_done, 1)
                elif kind == "lamexp":
                    act.wait_ge(vector_done, vector("pads", l))
                    last = act.activation(lamt[:, 66:68], lamt[:, 64:66], ACT.Exp)
                    last.then_inc(scalar_done, 1)
                elif kind == "modrow":
                    act.wait_ge(tensor_done, tensor("mod", l, *rest))
                    last = act.activation(mr[:, rest[0] % 2, :], bank(("mod", l, *rest)), ACT.Copy)
                    last.then_inc(scalar_done, 1)
                elif kind == "lgrow":
                    act.wait_ge(tensor_done, tensor("lg", l))
                    last = act.activation(mr[:, 0, 0:W], bank(("lg", l))[:, 0:W], ACT.Copy)
                    last.then_inc(scalar_done, 1)
                elif kind == "sq":
                    nn, t = rest
                    squares = xn[:, t, :]
                    if nn == 2:
                        act.wait_ge(vector_done, vector("xup", l, t, 1))
                        squares = gth[:, :, :].rearrange("p a n -> p (a n)")
                    elif l:
                        act.wait_ge(vector_done, vector("xup2", l - 1, t))
                    else:
                        act.wait_ge(x_landed, 16)
                    last = act.activation(squares, x[:, t, :], ACT.Square, accum_out=ss[:, t:t + 1])
                    last.then_inc(scalar_done, 1)
                elif kind == "xn":
                    nn, t = rest
                    act.wait_ge(vector_done, vector("rstd", l, nn, *normed_with(l, nn, t)))
                    if nn == 2:
                        act.wait_ge(tensor_done, tensor("wo", l, live(l) - 1, 1))
                    last = act.activation(xn[:, t, :], x[:, t, :], ACT.Copy, scale=small[:, 0, t:t + 1])
                    last.then_inc(scalar_done, 1)
                elif kind == "hTout":
                    nn, k = rest
                    act.wait_ge(tensor_done, tensor("hT", l, *rest))
                    act.wait_ge(vector_done, vector("modfin", l, nn))
                    for s in range(2 if nn == 1 else streams(l)):
                        h = slice(256 * s, 256 * s + 256)
                        last = act.activation(hT[:, k, h], bank(("hT", l, *rest))[:, h], ACT.Identity,
                                              bias=mod[:, l, 3 * nn - 3, k, s:s + 1], scale=amp[:, k, s:s + 1])
                    last.then_inc(scalar_done, 1)
                elif kind == "zDout":
                    (j,) = rest
                    act.wait_ge(tensor_done, tensor("zD", l, j))
                    last = act.activation(thd[:, j - 2, 0:W], bank(("zD", l, j))[:, 0:W], ACT.Tanh, scale=0.5)
                    last.then_inc(scalar_done, 1)
                elif kind == "zBout":
                    (j,) = rest
                    act.wait_ge(tensor_done, tensor("zB", l, j))
                    act.wait_ge(vector_done, vector(*(("hyconv", l, j - 2) if j >= 2 else ("pads", l))))
                    last = act.activation(zb[:, j % 2, 0:streams(l), 1:257],
                                          bank(("zB", l, j))[:, 0:W].rearrange("p (s n) -> p s n", s=streams(l)),
                                          ACT.Copy)
                    last.then_inc(scalar_done, 1)
                elif kind == "hfsin":
                    (i,) = rest
                    act.wait_ge(vector_done, vector("hfarg", l, i))
                    last = act.activation(hfa[0:64, i % 2, :], hfarg[0:64, :], ACT.Sin)
                    last.then_inc(scalar_done, 1)
                elif kind == "hfsq":
                    (i,) = rest
                    act.wait_ge(vector_done, vector("hfwin", l, i))
                    last = act.activation(hf2[:, i, :], hf[:, i, :], ACT.Square)
                    last.then_inc(scalar_done, 1)
                elif kind == "fdftout":
                    (j,) = rest
                    act.wait_ge(tensor_done, tensor("fdft", l, j))
                    last = act.activation(fs[:, j, :], bank(("fdft", l, j))[:, 0:256], ACT.Copy)
                    last.then_inc(scalar_done, 1)
                elif kind == "xcsq":
                    act.wait_ge(vector_done, vector("xc", l))
                    last = act.activation(sqd[:, :, 0:W], cv[:, :, 0:W], ACT.Square)
                    last.then_inc(scalar_done, 1)
                elif kind == "lntanh":
                    act.wait_ge(vector_done, vector("lnv", l))
                    last = act.activation(thd[:, :, 0:W], cv[:, :, 0:W], ACT.Tanh, scale=0.5)
                    last.then_inc(scalar_done, 1)
                elif kind == "vxTout":
                    (i,) = rest
                    act.wait_ge(tensor_done, tensor("vxT", l, i))
                    last = act.activation(ut[:, i, 0:W], bank(("vxT", l, i))[:, 0:W], ACT.Copy)
                    last.then_inc(scalar_done, 1)
                elif kind == "dftout":
                    (f,) = rest
                    act.wait_ge(tensor_done, tensor("dft", l, f))
                    last = act.activation(us[:, f, 0:W], bank(("dft", l, f))[:, 0:W], ACT.Copy)
                    last.then_inc(scalar_done, 1)
                elif kind == "gtanh":
                    bi, j = rest
                    act.wait_ge(tensor_done, tensor("gate", l, bi, j))
                    i = COUNT["V"][("gmul", l, bi, j)]
                    g = [s for s in STEPS["V"] if s[0] == "gmul"].index(("gmul", l, bi, j))
                    if g >= 2:
                        act.wait_ge(vector_done, vector(*[s for s in STEPS["V"] if s[0] == "gmul"][g - 2]))
                    last = act.activation(gth[:, g % 2, 0:W], bank(("gate", l, bi, j))[:, 0:W], ACT.Tanh,
                                          bias=hbg[:, bi * 8 + j:bi * 8 + j + 1], scale=0.5)
                    last.then_inc(scalar_done, 1)
                elif kind in ("zAqout", "zAkout", "zCout"):
                    (t,) = rest
                    act.wait_ge(vector_done, vector("hyout", l, 1))
                    act.wait_ge(tensor_done, tensor(kind[:-3], l, t))
                    b = bank((kind[:-3], l, t))
                    if kind == "zAqout":
                        last = act.activation(za[:, t, 0:256], b[:, 0:256], ACT.Copy)
                    elif kind == "zAkout":
                        last = act.activation(za[:, t, 256:768], b, ACT.Copy)
                    else:
                        wid = 512 if t < live(l) else 256
                        last = act.activation(zc[:, t, 0:wid], b[:, 0:wid], ACT.Copy)
                    last.then_inc(scalar_done, 1)
                elif kind == "qkToutA":
                    (t,) = rest
                    act.wait_ge(tensor_done, tensor("qkTA", l, t))
                    j0 = 0 if t < live(l) else 2
                    last = act.activation(qkta[:, j0:4, t * P:(t + 1) * P],
                                          bank(("qkTA", l, t))[:, j0 * P:512].rearrange("p (j n) -> p j n", n=P), ACT.Copy)
                    last.then_inc(scalar_done, 1)
                elif kind == "qkToutC":
                    (t,) = rest
                    act.wait_ge(tensor_done, tensor("qkTC", l, t))
                    nj = 3 if t < live(l) else 1
                    last = act.activation(qktc[:, 0:nj, t * P:(t + 1) * P],
                                          bank(("qkTC", l, t))[:, 0:nj * P].rearrange("p (j n) -> p j n", n=P), ACT.Copy)
                    last.then_inc(scalar_done, 1)
                elif kind in ("exA", "exC"):
                    t, h = rest
                    act.wait_ge(vector_done, vector("mx" + kind[-1], l, t, h))
                    i = (t * 4 + h) % 2
                    nk = (4 if t < 2 else 2) * P
                    for q in range(2 if kind == "exA" else 1):
                        last = act.activation(ee[:, i, q, 0:nk], bank(("s" + kind[2], l, t, h, q))[:, 0:nk], ACT.Exp,
                                              bias=nm[:, i, q:q + 1], scale=(32 if kind == "exA" else 64) ** -0.5,
                                              accum_out=sums[:, i, q:q + 1])
                    if kind == "exC":
                        last = act.activation(esk[:, i:i + 1], rowp(l, R_SINK + h, 1), ACT.Exp, bias=nm[:, i, 0:1])
                    last.then_inc(scalar_done, 1)
                elif kind in ("pToutA", "pToutC"):
                    t, h = rest
                    act.wait_ge(tensor_done, tensor("pT" + kind[-1], l, t, h))
                    nk = (4 if t < 2 else 2) * P
                    last = act.activation(pt[:, h, 0:nk], bank(("pT" + kind[-1], l, t, h))[:, 0:nk], ACT.Copy)
                    last.then_inc(scalar_done, 1)
                elif kind in ("yToutA", "yToutC"):
                    (t,) = rest
                    done = ("yTA" if kind == "yToutA" else "yC", l, t)
                    act.wait_ge(tensor_done, tensor(*done))
                    last = act.activation(yT[:, kind == "yToutC", :, t * P:(t + 1) * P],
                                          bank(done)[:, 0:256].rearrange("p (j n) -> p j n", n=P), ACT.Copy)
                    last.then_inc(scalar_done, 1)
                elif kind in ("rexp1", "rexp2"):
                    tt = live(l)
                    act.wait_ge(vector_done, vector("route1" if kind == "rexp1" else "route2", l))
                    if kind == "rexp1":
                        last = act.activation(rtmp[:, 3, 0:4 * tt], rtmp[:, 0, 0:4 * tt], ACT.Exp)
                    else:
                        last = act.activation(rtmp[:, 9, 0:tt], rtmp[:, 8, 0:tt], ACT.Exp)
                    last.then_inc(scalar_done, 1)
                elif kind == "hbout":
                    t, half = rest
                    act.wait_ge(tensor_done, tensor("hb", l, t, half))
                    last = act.activation(xn[:, t, half * 512:(half + 1) * 512], bank(("hb", l, t, half)), ACT.Copy)
                    last.then_inc(scalar_done, 1)
                elif kind == "hstore":
                    (t,) = rest
                    if l:
                        act.wait_ge(tokens_gathered, 16 * l * NE)
                    act.dma_start(h2_dram[t * P:(t + 1) * P, :], xn[:, t, :]).then_inc(h2_stored, 16)
                    act.nop().then_inc(scalar_done, 1)
                elif kind == "experts":
                    base = l * NE

                    def turned(e):
                        act.wait_ge(tokens_turned, base + e + 1)
                        act.activation(xgT[:, 4:8, :], ps[:, 1, :].rearrange("p (k n) -> p k n", n=P), ACT.Copy)\
                           .then_inc(turned_high, 1)

                    def tanh(e):
                        act.wait_ge(gate_done, base + e + 1)
                        if l or not isinstance(e, int):
                            act.wait_ge(u_ready, base + e)
                        act.activation(eth, ps[:, 2, :], ACT.Tanh, scale=0.5).then_inc(tanh_ready, 1)

                    def result(e):
                        act.wait_ge(down_high, base + e + 1)
                        if l or not isinstance(e, int) or e:
                            act.wait_ge(y_stored, (base + e) * 16)
                        act.activation(ysb[:, 512:D], ps[:, 6, :], ACT.Copy).then_inc(y_high, 1)
                        act.wait_ge(y_high, base + e + 1)
                        act.wait_ge(y_low, base + e + 1)
                        rows_of = y_dram[0:NE * P, :].rearrange("(e p) d -> e p d", p=P)
                        act.dma_start(rows_of[e], ysb).then_inc(y_stored, 16)

                    def turned_u(e):
                        act.wait_ge(u_turned, base + e + 1)
                        act.activation(uT, ps[:, 4, :].rearrange("p (f n) -> p f n", n=P), ACT.Copy).then_inc(uT_ready, 1)

                    turned(0)
                    tanh(0)
                    turned(1)
                    turned_u(0)
                    with act.Fori(1, NE - 1) as e:
                        tanh(e)
                        turned(e + 1)
                        result(e - 1)
                        turned_u(e)
                    tanh(NE - 1)
                    result(NE - 2)
                    turned_u(NE - 1)
                    result(NE - 1)
                    act.wait_ge(y_stored, (base + NE) * 16)
                    count = assignments(act, l)
                    with act.If(count > P):
                        with act.Fori(0, (live(l) - 1) * NE) as n_block:
                            act.wait_ge(more_tensor[l], n_block * 4 + 2)
                            act.activation(eth, ps[:, 2, :], ACT.Tanh, scale=0.5).then_inc(more_scalar[l], 1)
                    act.nop().then_inc(scalar_done, 1)
                elif kind == "weigh":
                    (t,) = rest
                    act.wait_ge(y_gathered[t], 32 * (l + 1))
                    act.activation(xn[:, t, :], xn[:, t, :], ACT.Copy, scale=pw[:, 0, t:t + 1]).then_inc(scalar_done, 1)
                else:
                    raise KeyError(kind)

        @block.gpsimd
        def _(gp):
            gm = [s for s in STEPS["V"] if s[0] == "gmul"]
            gp.wait_ge(vector_done, vector("pads", 0))
            gp.dma_start(list_dram.rearrange("(p n) o -> p (n o)", p=P), zero[:].bitcast(U32)).then_inc(list_cleared, 16)
            for n, name in enumerate(STEPS["P"]):
                kind, l, rest = name[0], name[1], name[2:]
                W = 128 * live(l)
                if n:
                    gp.wait_ge(pool_done, n)
                if kind == "gadd":
                    bi, j = rest
                    gp.wait_ge(vector_done, vector("gmul", l, bi, j))
                    g = gm.index(("gmul", l, bi, j))
                    last = nc.gpsimd.tensor_tensor(acc[:, j, 0:W], acc[:, j, 0:W], gtmp[:, g % 2, 0:W], ALU.add)
                    last.then_inc(pool_done, 1)
                elif kind == "sqA":
                    (t,) = rest
                    gp.wait_ge(scalar_done, scalar("zAkout", l, t))
                    lo = 0 if t < live(l) else 256
                    if t >= 2:
                        gp.wait_ge(vector_done, vector("ssA", l, t - 2))
                    last = nc.gpsimd.tensor_tensor(sq[:, t % 2, lo:512], za[:, t, lo:512], za[:, t, lo:512], ALU.mult)
                    last.then_inc(pool_done, 1)
                elif kind == "sqC":
                    (t,) = rest
                    gp.wait_ge(scalar_done, scalar("zCout", l, t))
                    gp.wait_ge(vector_done, vector(*(("ssC", l, t - 2) if t >= 2 else ("ssA", l, t + 2))))
                    last = nc.gpsimd.tensor_tensor(sq[:, t % 2, 0:128], zc[:, t, 0:128], zc[:, t, 0:128], ALU.mult)
                    if t < live(l):
                        last = nc.gpsimd.tensor_tensor(sq[:, t % 2, 256:512], zc[:, t, 256:512], zc[:, t, 256:512], ALU.mult)
                    last.then_inc(pool_done, 1)
                elif kind == "list":
                    tt = live(l)
                    gp.wait_ge(vector_done, vector("slots", l))
                    gp.wait_ge(list_cleared, 16)
                    for q in range(2):
                        for t in range(tt):
                            gp.indirect_dma_start(
                                out=list_dram, out_offset=bass.IndirectOffsetOnAxis(ap=idx[:, q * TILES + t:q * TILES + t + 1], axis=0),
                                in_=tok[:, t:t + 1], in_offset=None).then_inc(list_scattered, 16)
                    gp.wait_ge(list_scattered, 16 * 2 * (tt + l * live(0)))
                    gp.dma_start(lst, list_dram[0:P * NE, :].rearrange("(p e) o -> p (e o)", e=NE)).then_inc(list_landed, 16)
                    gp.wait_ge(list_landed, 16 * (l + 1))
                    gp.nop().then_inc(pool_done, 1)
                elif kind == "experts":
                    tt = live(l)
                    base = l * NE
                    gp.wait_ge(h2_stored, 16 * (tt + l * live(0)))
                    gp.tensor_copy(idx1, lst[:, 0:1]).then_inc(index_ready, 1)
                    gp.wait_ge(index_ready, base + 1)
                    gp.indirect_dma_start(out=xg, out_offset=None, in_=h2_dram,
                                          in_offset=bass.IndirectOffsetOnAxis(ap=idx1[:, 0:1], axis=0))                      .then_inc(tokens_gathered, 16)
                    with gp.Fori(1, NE) as e:
                        gp.wait_ge(tokens_turned, base + e)
                        gp.tensor_copy(idx1, lst[:, bass.ds(e, 1)]).then_inc(index_ready, 1)
                        gp.wait_ge(index_ready, base + e + 1)
                        gp.sem_inc(waited, 1)
                        gp.indirect_dma_start(out=xg, out_offset=None, in_=h2_dram,
                                              in_offset=bass.IndirectOffsetOnAxis(ap=idx1[:, 0:1], axis=0))\
                          .then_inc(tokens_gathered, 16)
                    gp.wait_ge(y_stored, 16 * (base + NE))
                    gp.wait_ge(tokens_turned, base + NE)

                    def gather_y(rows_):
                        gp.wait_ge(scalar_done, scalar("experts", l))
                        gp.wait_ge(tensor_done, tensor("experts", l))
                        for t in range(tt):
                            for q, dst in enumerate((xn, y2)):
                                at = (2 + q) * TILES + t
                                gp.indirect_dma_start(out=dst[:, t, :], out_offset=None, in_=y_dram[0:rows_, :],
                                                      in_offset=bass.IndirectOffsetOnAxis(ap=idx[:, at:at + 1], axis=0))\
                                  .then_inc(y_gathered[t], 16)

                    count = assignments(gp, l)
                    with gp.If(count > P):
                        entries = list_dram.rearrange("(b p e) o -> b p (e o)", p=P, e=NE)
                        with gp.Fori(0, tt - 1) as b:
                            gp.dma_start(lst, entries[b + 1]).then_inc(more_list[l], 16)
                            gp.wait_ge(more_list[l], b * 16 + 16)
                            gp.sem_inc(waited, 1)
                            with gp.Fori(0, NE) as e:
                                gp.tensor_copy(idx1, lst[:, bass.ds(e, 1)]).then_inc(more_index[l], 1)
                                gp.wait_ge(more_index[l], b * NE + e + 1)
                                gp.sem_inc(waited, 1)
                                gp.indirect_dma_start(out=xg, out_offset=None, in_=h2_dram,
                                                      in_offset=bass.IndirectOffsetOnAxis(ap=idx1[:, 0:1], axis=0))\
                                  .then_inc(more_gathered[l], 16)
                                gp.wait_ge(more_vector[l], b * (4 * NE) + e * 4 + 1)
                                gp.sem_inc(waited, 1)
                        gp.wait_ge(more_stored[l], 16 * NE * (tt - 1))
                        gather_y(tt * NE * P)
                    with gp.Else():
                        gather_y(NE * P)
                    gp.nop().then_inc(pool_done, 1)

        @block.vector
        def _(v):
            links = [0]

            def link(ins):
                links[0] += 1
                ins.then_inc(vector_chain, 1)
                v.wait_ge(vector_chain, links[0])

            def rsqrt(y, a, t, last=False):
                link(v.tensor_scalar(y.bitcast(I32), a.bitcast(I32), 1, None, ALU.logical_shift_right))
                link(v.tensor_scalar(y.bitcast(I32), y.bitcast(I32), -1.0, float(0x5f3759df), ALU.mult, ALU.add))
                for i in range(3):
                    link(v.scalar_tensor_tensor(out=t, in0=y, scalar=-0.5, in1=y, op0=ALU.mult, op1=ALU.mult))
                    link(v.tensor_tensor(t, t, a, ALU.mult))
                    ins = v.scalar_tensor_tensor(out=y, in0=t, scalar=1.5, in1=y, op0=ALU.add, op1=ALU.mult)
                    if last and i == 2:
                        return ins
                    link(ins)

            def rope(zt, rs, l, t, parts, d, cosn, sinn):
                for k, (lo, hi, g0, gain) in enumerate(parts):
                    G = (hi - lo) // d
                    X = zt[:, t, lo:hi].rearrange("p (g d) -> p g d", d=d)
                    ins = v.tensor_tensor(X, X, rs[:, t, g0:g0 + G].unsqueeze(2).broadcast_to([P, G, d]), ALU.mult)
                    link(ins)
                    ins = v.tensor_tensor(X, X, rowp(l, gain, d).unsqueeze(1).broadcast_to([P, G, d]), ALU.mult)
                    if t >= 2:
                        if k == len(parts) - 1:
                            return ins
                        link(ins)
                        continue
                    link(ins)
                    q = d // 4
                    cs = c(cosn).rearrange("p (t d) -> p t d", t=2)[:, t, :]
                    sn = c(sinn).rearrange("p (t a h q) -> p t a h q", t=2, a=2, h=2)[:, t]
                    R = rt[:, 0, 0:hi - lo].rearrange("p (g d) -> p g d", d=d)
                    link(v.tensor_tensor(R, X, cs.unsqueeze(1).broadcast_to([P, G, d]), ALU.mult))
                    X4 = zt[:, t, lo:hi].rearrange("p (g a h q) -> p g a h q", a=2, h=2, q=q)
                    T4 = rt[:, 1, 0:hi - lo].rearrange("p (g a h q) -> p g a h q", a=2, h=2, q=q)
                    for h in range(2):
                        ins = v.tensor_tensor(T4[:, :, :, h, :], X4[:, :, :, 1 - h, :],
                                              sn[:, :, h, :].unsqueeze(1).broadcast_to([P, G, 2, q]), ALU.mult)
                        link(ins)
                    ins = v.tensor_tensor(zt[:, t, lo:hi], rt[:, 0, 0:hi - lo], rt[:, 1, 0:hi - lo], ALU.add)
                    if k == len(parts) - 1:
                        return ins
                    link(ins)

            def first_max(one_hot, a, top, r, tt):
                A3 = lambda s: s.rearrange("p (t g) -> p t g", g=4)
                link(v.tensor_tensor(A3(r), A3(a), top.unsqueeze(2).broadcast_to([P, tt, 4]), ALU.is_equal))
                link(v.tensor_tensor(A3(r), A3(r), c("rank").unsqueeze(1).broadcast_to([P, tt, 4]), ALU.mult))
                link(v.tensor_reduce(top, A3(r), AX.X, ALU.max))
                link(v.tensor_tensor(A3(one_hot), A3(r), top.unsqueeze(2).broadcast_to([P, tt, 4]), ALU.is_equal))

            gm = [s for s in STEPS["V"] if s[0] == "gmul"]
            v.wait_ge(params_landed, 16 * 4)
            v.wait_ge(const_landed, 16)
            for n, name in enumerate(STEPS["V"]):
                kind, l, rest = name[0], name[1], name[2:]
                tt = live(l)
                W = 128 * tt
                if n:
                    v.wait_ge(vector_done, n)
                if kind == "pads":
                    if l:
                        v.wait_ge(tensor_done, tensor("experts", l - 1))
                        v.wait_ge(pool_done, pool("experts", l - 1))
                    else:
                        v.wait_ge(scalar_done, scalar("silu", 0))
                        link(v.scalar_tensor_tensor(out=ct, in0=ct, scalar=1.0, in1=cc[:], op0=ALU.add, op1=ALU.mult))
                        link(v.tensor_scalar(cc[:], ct, 0.5, None, ALU.mult))
                        link(v.memset(zero[:], 0.0))
                    link(v.memset(m[:, 0:1032], 0.0))
                    link(v.memset(n_[:, 0:1144], 0.0))
                    link(v.tensor_scalar(hbg[:], col[:, l, C_BGATE:C_BGATE + 32], 0.5, None, ALU.mult))
                    lam = rowp(l, R_LAM, 128).rearrange("p (a b n) -> p a b n", a=2, b=2)
                    prod = lamt[:, 0:64].rearrange("p (a n) -> p a n", a=2)
                    link(v.tensor_tensor(prod, lam[:, :, 0, :], lam[:, :, 1, :], ALU.mult))
                    last = v.tensor_reduce(lamt[:, 64:66], prod, AX.X, ALU.add)
                    last.then_inc(vector_done, 1)
                elif kind == "lam":
                    v.wait_ge(scalar_done, scalar("lamexp", l))
                    lam0 = 0.8 - 0.6 * math.exp(-0.3 * l)
                    link(v.tensor_tensor(nlam[:, 0:1], lamt[:, 67:68], lamt[:, 66:67], ALU.subtract))
                    last = v.tensor_scalar(nlam[:, 1:2], nlam[:, 0:1], -lam0, None, ALU.add)
                    last.then_inc(vector_done, 1)
                elif kind == "modcol":
                    (ch,) = rest
                    v.wait_ge(tensor_done, tensor("modT", l, ch))
                    k0 = (ch % 2) * 4
                    src = bank(("modT", l, ch)).rearrange("p (j g r) -> p j r g", g=4, r=32)[:, :, 0:2, :]
                    link(v.tensor_reduce(modt[:], src, AX.X, ALU.add))
                    bm = col[:, l, C_BMOD + ch * 4:C_BMOD + ch * 4 + 4].unsqueeze(2).broadcast_to([P, 4, 2])
                    last = v.tensor_tensor(mod[:, l, ch // 2, k0:k0 + 4, :], modt[:], bm, ALU.add)
                    last.then_inc(vector_done, 1)
                elif kind == "modgate":
                    ch, s = rest
                    v.wait_ge(tensor_done, tensor("modB", l, ch, s))
                    last = v.tensor_copy(gbc[:, s, (ch % 2) * 512:(ch % 2 + 1) * 512], bank(("modB", l, ch, s)))
                    last.then_inc(vector_done, 1)
                elif kind == "modfin":
                    (nn,) = rest
                    g = col[:, l, (C_N1, C_N2)[nn - 1]:(C_N1, C_N2)[nn - 1] + KD].unsqueeze(2).broadcast_to([P, KD, 2])
                    last = v.scalar_tensor_tensor(out=amp[:], in0=mod[:, l, 3 * nn - 2], scalar=1.0, in1=g,
                                                  op0=ALU.add, op1=ALU.mult)
                    last.then_inc(vector_done, 1)
                elif kind == "rstd":
                    nn, t0, t1 = rest
                    v.wait_ge(scalar_done, scalar("sq", l, nn, t1 - 1))
                    link(v.tensor_scalar(small[:, 1, t0:t1], ss[:, t0:t1], 1.0 / D, EPS, ALU.mult, ALU.add))
                    last = rsqrt(small[:, 0, t0:t1], small[:, 1, t0:t1], small[:, 2, t0:t1], True)
                    last.then_inc(vector_done, 1)
                elif kind == "xn":
                    nn, t = rest
                    if nn == 2:
                        v.wait_ge(tensor_done, tensor("wo", l, tt - 1, 1))
                    last = v.tensor_scalar(xn[:, t, :], x[:, t, :], small[:, 0, t:t + 1], None, ALU.mult)
                    last.then_inc(vector_done, 1)
                elif kind == "hTout":
                    nn, k = rest
                    v.wait_ge(tensor_done, tensor("hT", l, *rest))
                    for s in range(2 if nn == 1 else streams(l)):
                        h = slice(256 * s, 256 * s + 256)
                        last = v.tensor_scalar(hT[:, k, h], bank(("hT", l, *rest))[:, h], amp[:, k, s:s + 1],
                                               mod[:, l, 3 * nn - 3, k, s:s + 1], ALU.mult, ALU.add)
                    last.then_inc(vector_done, 1)
                elif kind == "zDout":
                    (j,) = rest
                    v.wait_ge(scalar_done, scalar("zDout", l, j + 2))
                    link(v.tensor_scalar(sqd[:, j, 0:W], thd[:, j, 0:W], 0.5, 0.5, ALU.mult, ALU.add))
                    v.wait_ge(tensor_done, tensor("zD", l, j))
                    s3 = lambda a: a[:, 0:W].rearrange("p (s n) -> p s n", n=256)
                    last = v.tensor_tensor(ud[:, j, 0:streams(l), PAD:PAD + 256], s3(sqd[:, j, :]),
                                           s3(bank(("zD", l, j))), ALU.mult)
                    last.then_inc(vector_done, 1)
                elif kind == "hyconv":
                    (j,) = rest
                    v.wait_ge(scalar_done, scalar("zBout", l, j))
                    ns = streams(l)
                    o = hu[:, j, 0:ns, :]
                    w = lambda k: col[:, l, C_HYW + k * 6 + j:C_HYW + k * 6 + j + 1]
                    link(v.tensor_scalar(o, zb[:, j % 2, 0:ns, 0:256], w(0), col[:, l, C_HYB + j:C_HYB + j + 1],
                                         ALU.mult, ALU.add))
                    link(v.scalar_tensor_tensor(out=o, in0=zb[:, j % 2, 0:ns, 1:257], scalar=w(1), in1=o,
                                                op0=ALU.mult, op1=ALU.add))
                    last = v.scalar_tensor_tensor(out=o, in0=zb[:, j % 2, 0:ns, 2:258], scalar=w(2), in1=o,
                                                  op0=ALU.mult, op1=ALU.add)
                    last.then_inc(vector_done, 1)
                elif kind == "vx":
                    ns = streams(l)
                    for j in range(2):
                        last = v.tensor_tensor(hu[:, 4 + j, 0:ns, :], hu[:, 4 + j, 0:ns, :], hu[:, 2 + j, 0:ns, :], ALU.mult)
                    last.then_inc(vector_done, 1)
                elif kind == "cfconv":
                    j, half = rest
                    ns = streams(l)
                    o = cv[:, j, 0:W].rearrange("p (s n) -> p s n", n=256)
                    w = lambda k: col[:, l, C_CFW + k * 2 + j:C_CFW + k * 2 + j + 1]
                    if half == 0:
                        link(v.tensor_scalar(o, ud[:, j, 0:ns, 0:256], w(0), col[:, l, C_CFB + j:C_CFB + j + 1],
                                             ALU.mult, ALU.add))
                    taps = range(1, TAPS // 2) if half == 0 else range(TAPS // 2, TAPS)
                    for k in taps:
                        last = v.scalar_tensor_tensor(out=o, in0=ud[:, j, 0:ns, k:k + 256], scalar=w(k), in1=o,
                                                      op0=ALU.mult, op1=ALU.add)
                        if k < taps[-1]:
                            link(last)
                    last.then_inc(vector_done, 1)
                elif kind == "hfarg":
                    (i,) = rest
                    v.wait_ge(tensor_done, tensor("hf", l, i))
                    a, kk = hfarg[0:64, :], hfk[0:64, :]
                    link(v.tensor_scalar(a, bank(("hf", l, i))[0:64, 0:256], col[0:64, l, C_HF + i - 1:C_HF + i],
                                         col[0:64, l, C_HF + 3:C_HF + 4], ALU.add, ALU.mult))
                    link(v.tensor_scalar(kk, a, 1.0 / TWO_PI, MAGIC, ALU.mult, ALU.add))
                    link(v.tensor_scalar(kk, kk, MAGIC, None, ALU.subtract))
                    link(v.scalar_tensor_tensor(out=a, in0=kk, scalar=-PI_HI, in1=a, op0=ALU.mult, op1=ALU.add))
                    link(v.scalar_tensor_tensor(out=a, in0=kk, scalar=-PI_LO, in1=a, op0=ALU.mult, op1=ALU.add))
                    last = v.tensor_scalar(a, a, SIN_MAX, -SIN_MAX, ALU.min, ALU.max)
                    last.then_inc(vector_done, 1)
                elif kind == "hfwin":
                    (i,) = rest
                    v.wait_ge(tensor_done, tensor("hf4", l, i))
                    last = v.tensor_tensor(hf[:, i, :], bank(("hf4", l, i)), win_c[:, i, :], ALU.mult)
                    last.then_inc(vector_done, 1)
                elif kind == "fnorms":
                    v.wait_ge(tensor_done, tensor("fnorm", l))
                    link(v.tensor_scalar(small[:, 1, 0:2], bank(("fnorm", l))[:, 0:2], 256.0, EPS, ALU.mult, ALU.add))
                    last = rsqrt(fn[:], small[:, 1, 0:2], small[:, 2, 0:2], True)
                    last.then_inc(vector_done, 1)
                elif kind == "xc":
                    v.wait_ge(tensor_done, tensor("lnmean", l))
                    for j in range(2):
                        last = v.tensor_tensor(cv[:, j, 0:W], cv[:, j, 0:W], bank(("lnmean", l))[:, 0:W], ALU.subtract)
                    last.then_inc(vector_done, 1)
                elif kind == "lnv":
                    v.wait_ge(tensor_done, tensor("lnvar", l))
                    a = sqd[:, 0, 0:W]
                    link(v.tensor_scalar(a, bank(("lnvar", l))[:, 0:W], EPS, None, ALU.add))
                    rsqrt(rsd[:, 0, 0:W], a, rsd[:, 1, 0:W])
                    for j in range(2):
                        link(v.tensor_tensor(cv[:, j, 0:W], cv[:, j, 0:W], rsd[:, 0, 0:W], ALU.mult))
                        last = v.tensor_scalar(cv[:, j, 0:W], cv[:, j, 0:W], col[:, l, C_LNG + j:C_LNG + j + 1],
                                               col[:, l, C_LNB + j:C_LNB + j + 1], ALU.mult, ALU.add)
                    last.then_inc(vector_done, 1)
                elif kind == "lnout":
                    v.wait_ge(scalar_done, scalar("lntanh", l))
                    link(v.tensor_scalar(sqd[:, :, 0:W], thd[:, :, 0:W], 0.5, 0.5, ALU.mult, ALU.add))
                    last = v.tensor_tensor(yT[:, 0, :, 0:W], cv[:, :, 0:W], sqd[:, :, 0:W], ALU.mult)
                    last.then_inc(vector_done, 1)
                elif kind == "spec":
                    v.wait_ge(scalar_done, scalar("dftout", l, 3))
                    v.wait_ge(scalar_done, scalar("fdftout", l, 5))
                    ns = streams(l)
                    S3 = lambda a: a[:, 0:W].rearrange("p (s n) -> p s n", n=256)
                    tmp = hu[:, 2, 0:ns, :]
                    for f in range(2):
                        A, B, C = (fs[:, f + 2 * q, :].unsqueeze(1).broadcast_to([P, ns, 256]) for q in range(3))
                        uc, us_, yc, ys = S3(us[:, f, :]), S3(us[:, 2 + f, :]), S3(ysp[:, f, :]), S3(ysp[:, 2 + f, :])
                        link(v.tensor_tensor(tmp, us_, B, ALU.mult))
                        link(v.tensor_tensor(yc, uc, A, ALU.mult))
                        link(v.tensor_tensor(yc, yc, tmp, ALU.subtract))
                        link(v.tensor_tensor(tmp, uc, B, ALU.mult))
                        link(v.tensor_tensor(ys, us_, C, ALU.mult))
                        last = v.tensor_tensor(ys, ys, tmp, ALU.add)
                        if f == 0:
                            link(last)
                    last.then_inc(vector_done, 1)
                elif kind == "hyout":
                    (j,) = rest
                    v.wait_ge(tensor_done, tensor("idft", l, j))
                    o = yT[:, 1, j, 0:W]
                    S3 = lambda a: a.rearrange("p (s n) -> p s n", n=256)
                    link(v.tensor_scalar(o, bank(("idft", l, j))[:, 0:W], fn[:, j:j + 1], None, ALU.mult))
                    ns = streams(l)
                    link(v.scalar_tensor_tensor(out=S3(o), in0=hu[:, 4 + j, 0:ns, :],
                                                scalar=col[:, l, C_HYBIAS + j:C_HYBIAS + j + 1], in1=S3(o),
                                                op0=ALU.mult, op1=ALU.add))
                    last = v.tensor_tensor(S3(o), S3(o), hu[:, j, 0:ns, :], ALU.mult)
                    last.then_inc(vector_done, 1)
                elif kind == "gmul":
                    bi, j = rest
                    g = gm.index(name)
                    v.wait_ge(scalar_done, scalar("gtanh", l, bi, j))
                    v.wait_ge(tensor_done, tensor("br", l, bi, j))
                    dst = acc[:, j, 0:W] if bi == BRANCHES[0] else gtmp[:, g % 2, 0:W]
                    if g >= 2 and ("gadd", *gm[g - 2][1:]) in COUNT["P"]:
                        v.wait_ge(pool_done, pool("gadd", *gm[g - 2][1:]))
                    last = v.scalar_tensor_tensor(out=dst, in0=gth[:, g % 2, 0:W], scalar=1.0,
                                                  in1=bank(("br", l, bi, j))[:, 0:W], op0=ALU.add, op1=ALU.mult)
                    last.then_inc(vector_done, 1)
                elif kind == "ssA":
                    (t,) = rest
                    v.wait_ge(pool_done, pool("sqA", l, t))
                    lo = 0 if t < tt else 256
                    last = v.tensor_reduce(ssa[:, t, lo // 32:16], sq[:, t % 2, lo:512].rearrange("p (g d) -> p g d", d=32),
                                           AX.X, ALU.add)
                    last.then_inc(vector_done, 1)
                elif kind == "ssC":
                    (t,) = rest
                    v.wait_ge(pool_done, pool("sqC", l, t))
                    last = v.tensor_reduce(ssc[:, t, 0:2], sq[:, t % 2, 0:128].rearrange("p (g d) -> p g d", d=64), AX.X, ALU.add)
                    if t < tt:
                        last = v.tensor_reduce(ssc[:, t, 2:6], sq[:, t % 2, 256:512].rearrange("p (g d) -> p g d", d=64),
                                               AX.X, ALU.add)
                    last.then_inc(vector_done, 1)
                elif kind in ("rsA", "rsC"):
                    s_, r_, k = (ssa, rsa, 64) if kind == "rsA" else (ssc, rsc, 24)
                    f = lambda a: a[:].rearrange("p t g -> p (t g)")
                    link(v.tensor_scalar(small[:, 1, 0:k], f(s_), 1.0 / (32 if kind == "rsA" else 64), EPS, ALU.mult, ALU.add))
                    last = rsqrt(f(r_), small[:, 1, 0:k], small[:, 2, 0:k], True)
                    last.then_inc(vector_done, 1)
                elif kind == "ropeA":
                    (t,) = rest
                    ps_ = ([(0, 256, 0, R_QN)] if t < tt else []) + [(256, 512, 8, R_KN)]
                    last = rope(za, rsa, l, t, ps_, 32, "cosa", "sina")
                    last.then_inc(vector_done, 1)
                elif kind == "ropeC":
                    (t,) = rest
                    ps_ = [(0, 128, 0, R_WK)] + ([(256, 512, 2, R_WQ)] if t < tt else [])
                    last = rope(zc, rsc, l, t, ps_, 64, "cosc", "sinc")
                    last.then_inc(vector_done, 1)
                elif kind == "mxA":
                    t, h = rest
                    i = (t * 4 + h) % 2
                    nk = (4 if t < 2 else 2) * P
                    v.wait_ge(tensor_done, tensor("sA", l, t, h, 1))
                    for q in range(2):
                        link(v.reduce_max(mx[:, i, q:q + 1], bank(("sA", l, t, h, q))[:, 0:nk], AX.X))
                    last = v.tensor_scalar(nm[:, i, :], mx[:, i, :], -(32 ** -0.5), None, ALU.mult)
                    last.then_inc(vector_done, 1)
                elif kind == "mxC":
                    t, h = rest
                    i = (t * 4 + h) % 2
                    nk = (4 if t < 2 else 2) * P
                    v.wait_ge(tensor_done, tensor("sC", l, t, h, 0))
                    b = bank(("sC", l, t, h, 0))
                    if t < 2:
                        other = b[:, (1 - t) * P:(2 - t) * P]
                        link(v.tensor_tensor(other, other, mask_c[:, t, :], ALU.add))
                    link(v.reduce_max(mx[:, i, 0:1], b[:, 0:nk], AX.X))
                    link(v.tensor_scalar(mx[:, i, 1:2], mx[:, i, 0:1], 64 ** -0.5, rowp(l, R_SINK + h, 1), ALU.mult, ALU.max))
                    last = v.tensor_scalar(nm[:, i, 0:1], mx[:, i, 1:2], -1.0, None, ALU.mult)
                    last.then_inc(vector_done, 1)
                elif kind == "pA":
                    t, h = rest
                    i = (t * 4 + h) % 2
                    nk = (4 if t < 2 else 2) * P
                    v.wait_ge(scalar_done, scalar("exA", l, t, h))
                    link(v.reciprocal(rr[:], sums[:, i, :]))
                    link(v.tensor_tensor(nlam[:, 2:3], rr[:, 1:2], nlam[:, 1:2], ALU.mult))
                    link(v.tensor_scalar(ee[:, i, 0, 0:nk], ee[:, i, 0, 0:nk], rr[:, 0:1], None, ALU.mult))
                    last = v.scalar_tensor_tensor(out=ee[:, i, 0, 0:nk], in0=ee[:, i, 1, 0:nk], scalar=nlam[:, 2:3],
                                                  in1=ee[:, i, 0, 0:nk], op0=ALU.mult, op1=ALU.add)
                    last.then_inc(vector_done, 1)
                elif kind == "pC":
                    t, h = rest
                    i = (t * 4 + h) % 2
                    v.wait_ge(scalar_done, scalar("exC", l, t, h))
                    E = ee[:, i, 0, 0:(4 if t < 2 else 2) * P]
                    link(v.tensor_tensor(den[:, h:h + 1], sums[:, i, 0:1], esk[:, i:i + 1], ALU.add))
                    link(v.reciprocal(rden[:, h:h + 1], den[:, h:h + 1]))
                    last = v.tensor_scalar(E, E, rden[:, h:h + 1], None, ALU.mult)
                    last.then_inc(vector_done, 1)
                elif kind == "ynA":
                    (t,) = rest
                    v.wait_ge(tensor_done, tensor("yA", l, t))
                    H = lambda a: a.rearrange("p (h d) -> p h d", h=4)
                    lam0 = 0.8 - 0.6 * math.exp(-0.3 * l)
                    link(v.tensor_copy(yn, bank(("yA", l, t))[:, 0:256]))
                    link(v.tensor_tensor(ynq, yn, yn, ALU.mult))
                    link(v.tensor_reduce(small[:, 1, 0:4], H(ynq), AX.X, ALU.add))
                    link(v.tensor_scalar(small[:, 1, 0:4], small[:, 1, 0:4], 1.0 / 64, EPS, ALU.mult, ALU.add))
                    rsqrt(small[:, 0, 8:12], small[:, 1, 0:4], small[:, 2, 0:4])
                    link(v.tensor_tensor(H(yn), H(yn), small[:, 0, 8:12].unsqueeze(2).broadcast_to([P, 4, 64]), ALU.mult))
                    last = v.scalar_tensor_tensor(out=H(yn), in0=H(yn), scalar=1.0 - lam0,
                                                  in1=rowp(l, R_SUB, 64).unsqueeze(1).broadcast_to([P, 4, 64]),
                                                  op0=ALU.mult, op1=ALU.mult)
                    last.then_inc(vector_done, 1)
                elif kind == "xup":
                    t, half = rest
                    v.wait_ge(tensor_done, tensor("wo", l, t, half))
                    xs = x[:, t, half * 512:(half + 1) * 512]
                    link(v.scalar_tensor_tensor(out=gtmp[:, half, :], in0=bank(("wo", l, t, half)), scalar=0.5,
                                                in1=gbc[:, t // 2, half * 512:(half + 1) * 512], op0=ALU.mult, op1=ALU.mult))
                    last = v.tensor_tensor(xs, xs, gtmp[:, half, :], ALU.add)
                    last.then_inc(vector_done, 1)
                elif kind == "lgout":
                    v.wait_ge(tensor_done, tensor("lgT", l))
                    src = bank(("lgT", l))[:, 0:W].rearrange("p (t g r) -> p t r g", g=4, r=32)[:, :, 0:20, :]
                    link(v.tensor_reduce(lg[:, 0:tt, :], src, AX.X, ALU.add))
                    last = v.tensor_tensor(lg[:, 0:tt, :], lg[:, 0:tt, :],
                                           rowp(l, R_BR, 20).unsqueeze(1).broadcast_to([P, tt, 20]), ALU.add)
                    last.then_inc(vector_done, 1)
                elif kind == "route1":
                    d0 = rtmp[:, 0, 0:4 * tt].rearrange("p (t g) -> p t g", g=4)
                    link(v.tensor_reduce(rtmp[:, 2, 0:tt], lg[:, 0:tt, 0:4], AX.X, ALU.max))
                    last = v.tensor_tensor(d0, lg[:, 0:tt, 0:4], rtmp[:, 2, 0:tt].unsqueeze(2).broadcast_to([P, tt, 4]),
                                           ALU.subtract)
                    last.then_inc(vector_done, 1)
                elif kind == "route2":
                    d0, oh = rtmp[:, 0, 0:4 * tt], rtmp[:, 1, 0:4 * tt]
                    v.wait_ge(scalar_done, scalar("rexp1", l))
                    T4 = lambda a: a.rearrange("p (t g) -> p t g", g=4)
                    link(v.tensor_reduce(rtmp[:, 2, 0:tt], T4(rtmp[:, 3, 0:4 * tt]), AX.X, ALU.add))
                    link(v.reciprocal(rtmp[:, 4, 0:tt], rtmp[:, 2, 0:tt]))
                    link(v.tensor_reduce(rtmp[:, 2, 0:tt], T4(d0), AX.X, ALU.max))
                    first_max(oh, d0, rtmp[:, 2, 0:tt], rtmp[:, 5, 0:4 * tt], tt)
                    for t in range(tt):
                        link(v.tensor_tensor(rt16[:, t, :].rearrange("p (g j) -> p g j", j=4),
                                             lg[:, t, 4:20].rearrange("p (g j) -> p g j", j=4),
                                             oh[:, 4 * t:4 * t + 4].unsqueeze(2).broadcast_to([P, 4, 4]), ALU.mult))
                    le = rtmp[:, 6, 0:4 * tt]
                    link(v.tensor_reduce(T4(le), rt16[:, 0:tt, :].rearrange("p t (g j) -> p t j g", j=4), AX.X, ALU.add))
                    link(v.tensor_reduce(rtmp[:, 2, 0:tt], T4(le), AX.X, ALU.max))
                    link(v.tensor_copy(rtmp[:, 2, 4:4 + tt], rtmp[:, 2, 0:tt]))
                    first_max(rtmp[:, 7, 0:4 * tt], le, rtmp[:, 2, 0:tt], rtmp[:, 5, 0:4 * tt], tt)
                    link(v.tensor_tensor(T4(le), T4(le), rtmp[:, 2, 4:4 + tt].unsqueeze(2).broadcast_to([P, tt, 4]),
                                         ALU.subtract))
                    link(v.scalar_tensor_tensor(out=le, in0=rtmp[:, 7, 0:4 * tt], scalar=NEG, in1=le,
                                                op0=ALU.mult, op1=ALU.add))
                    link(v.tensor_reduce(rtmp[:, 8, 0:tt], T4(le), AX.X, ALU.max))
                    link(v.tensor_copy(rtmp[:, 2, 0:tt], rtmp[:, 8, 0:tt]))
                    first_max(rtmp[:, 10, 0:4 * tt], le, rtmp[:, 2, 0:tt], rtmp[:, 5, 0:4 * tt], tt)
                    last = v.tensor_copy(rtmp[:, 11, 0:tt], rtmp[:, 8, 0:tt])
                    last.then_inc(vector_done, 1)
                elif kind == "route3":
                    v.wait_ge(scalar_done, scalar("rexp2", l))
                    T4 = lambda a: a.rearrange("p (t g) -> p t g", g=4)
                    p1, p2 = rtmp[:, 11, 0:tt], rtmp[:, 11, 4:4 + tt]
                    link(v.tensor_scalar(p1, rtmp[:, 9, 0:tt], 1.0, None, ALU.add))
                    link(v.reciprocal(p2, p1))
                    link(v.scalar_tensor_tensor(out=p1, in0=p2, scalar=0.5, in1=rtmp[:, 4, 0:tt], op0=ALU.mult, op1=ALU.mult))
                    link(v.tensor_tensor(p2, p1, rtmp[:, 9, 0:tt], ALU.mult))
                    link(v.tensor_copy(pw[:, 0, 0:tt], p1))
                    link(v.tensor_copy(pw[:, 1, 0:tt], p2))
                    for q in range(2):
                        for t in range(tt):
                            link(v.tensor_tensor(pick[:, q, t * NE:(t + 1) * NE].rearrange("p (g j) -> p g j", j=4),
                                                 rtmp[:, 1, 4 * t:4 * t + 4].unsqueeze(2).broadcast_to([P, 4, 4]),
                                                 rtmp[:, 7 + 3 * q, 4 * t:4 * t + 4].unsqueeze(1).broadcast_to([P, 4, 4]), ALU.mult))
                    link(v.memset(both[:, 0, :], 0.0))
                    link(v.memset(both[:, tt + 1, :], 0.0))
                    last = v.tensor_tensor(both[:, 1:tt + 1, :], pick[:, 0, 0:tt * NE].rearrange("p (t e) -> p t e", e=NE),
                                           pick[:, 1, 0:tt * NE].rearrange("p (t e) -> p t e", e=NE), ALU.add)
                    last.then_inc(vector_done, 1)
                elif kind == "slots":
                    v.wait_ge(tensor_done, tensor("rank", l))
                    b = bank(("rank", l))
                    link(v.tensor_copy(tok, c("token")))
                    link(v.tensor_scalar(ranks[:, 0:tt, :].rearrange("p t e -> p (t e)"), b[:, 0:tt * NE], 256.0, None, ALU.mult))
                    link(v.tensor_reduce(most, b[:, tt * NE:(tt + 1) * NE], AX.X, ALU.max))
                    link(v.tensor_scalar(most, most, 256.0, None, ALU.mult))
                    link(v.tensor_copy(flag, most))
                    for q in range(2):
                        pk = pick[:, q, 0:tt * NE].rearrange("p (t e) -> p t e", e=NE)
                        rk, ex = choice[:, 2 * q, 0:tt], choice[:, 2 * q + 1, 0:tt]
                        link(v.tensor_tensor(picked[:, 0:tt, :], pk, ranks[:, 0:tt, :], ALU.mult))
                        link(v.tensor_reduce(rk, picked[:, 0:tt, :], AX.X, ALU.add))
                        link(v.tensor_tensor(picked[:, 0:tt, :], pk, c("expert").unsqueeze(1).broadcast_to([P, tt, NE]), ALU.mult))
                        link(v.tensor_reduce(ex, picked[:, 0:tt, :], AX.X, ALU.add))
                        link(v.scalar_tensor_tensor(out=slotf[:, q, 0:tt], in0=rk, scalar=float(NE), in1=ex, op0=ALU.mult, op1=ALU.add))
                        ry = slotf[:, 2 + q, 0:tt]
                        link(v.scalar_tensor_tensor(out=ry, in0=ex, scalar=float(P), in1=rk, op0=ALU.mult, op1=ALU.add))
                        for k in range(1, tt):
                            link(v.tensor_scalar(picked[:, 0, 0:tt], rk, float(P * k), float(NE * P - P), ALU.is_ge, ALU.mult))
                            link(v.tensor_tensor(ry, ry, picked[:, 0, 0:tt], ALU.add))
                    last = v.tensor_copy(idx.rearrange("p (a t) -> p a t", t=TILES)[:, :, 0:tt], slotf[:, :, 0:tt])
                    last.then_inc(vector_done, 1)
                elif kind == "experts":
                    base = l * NE

                    def turned(e):
                        v.wait_ge(tokens_turned, base + e + 1)
                        v.tensor_copy(xgT[:, 0:4, :], ps[:, 0, :].rearrange("p (k n) -> p k n", n=P)).then_inc(turned_low, 1)

                    def hidden(e):
                        v.wait_ge(tanh_ready, base + e + 1)
                        v.scalar_tensor_tensor(out=es, in0=eth, scalar=1.0, in1=ps[:, 2, :], op0=ALU.add, op1=ALU.mult)                         .then_inc(gate_ready, 1)
                        v.wait_ge(gate_ready, base + e + 1)
                        v.wait_ge(up_done, base + e + 1)
                        v.tensor_tensor(u, es, ps[:, 3, :], ALU.mult).then_inc(u_ready, 1)

                    def result(e):
                        v.wait_ge(down_low, base + e + 1)
                        if l or not isinstance(e, int) or e:
                            v.wait_ge(y_stored, (base + e) * 16)
                        v.tensor_copy(ysb[:, 0:512], ps[:, 5, :]).then_inc(y_low, 1)

                    turned(0)
                    hidden(0)
                    turned(1)
                    with v.Fori(1, NE - 1) as e:
                        hidden(e)
                        turned(e + 1)
                        result(e - 1)
                    hidden(NE - 1)
                    result(NE - 2)
                    result(NE - 1)
                    count = assignments(v, l)
                    with v.If(count > P):
                        v.wait_ge(y_stored, 16 * (base + NE))
                        with v.Fori(0, (tt - 1) * NE) as n_block:
                            v.wait_ge(more_tensor[l], n_block * 4 + 1)
                            v.tensor_copy(xgT, ps[:, 0:2, :].rearrange("p a (k n) -> p (a k) n", n=P)).then_inc(more_vector[l], 1)
                            v.wait_ge(more_scalar[l], n_block + 1)
                            v.scalar_tensor_tensor(out=es, in0=eth, scalar=1.0, in1=ps[:, 2, :], op0=ALU.add, op1=ALU.mult)
                            v.drain()
                            v.tensor_tensor(u, es, ps[:, 3, :], ALU.mult).then_inc(more_vector[l], 1)
                            v.wait_ge(more_tensor[l], n_block * 4 + 3)
                            v.tensor_copy(uT, ps[:, 4, :].rearrange("p (f n) -> p f n", n=P)).then_inc(more_vector[l], 1)
                            v.wait_ge(more_tensor[l], n_block * 4 + 4)
                            v.tensor_copy(ysb.rearrange("p (a n) -> p a n", a=2), ps[:, 5:7, :]).then_inc(more_vector[l], 1)
                    v.nop().then_inc(vector_done, 1)
                elif kind == "xup2":
                    (t,) = rest
                    v.wait_ge(scalar_done, scalar("weigh", l, t))
                    link(v.scalar_tensor_tensor(out=xn[:, t, :], in0=y2[:, t, :], scalar=pw[:, 1, t:t + 1], in1=xn[:, t, :],
                                                op0=ALU.mult, op1=ALU.add))
                    link(v.tensor_tensor(xn[:, t, :], xn[:, t, :], gbc[:, t // 2, :], ALU.mult))
                    last = v.tensor_tensor(x[:, t, :], x[:, t, :], xn[:, t, :], ALU.add)
                    last.then_inc(vector_done, 1)
                else:
                    raise KeyError(kind)


def kernel(**inputs):
    import numpy as _np
    import concourse.bacc as _bacc
    from concourse import mybir as _mybir
    from concourse.bass_utils import run_bass_kernel_spmd as _run

    I = {k: _np.asarray(v) for k, v in inputs.items()}

    def tiles(a):
        n = a.shape[0] // P
        return a.reshape(n, P, a.shape[1]).transpose(1, 0, 2).reshape(P, -1)

    def chan(v):
        return v.reshape(-1, P).T

    arrays = {}
    tok = _np.concatenate([I["x"][0], I["ctx"][0]], 0)
    arrays["xin"] = tok.reshape(TILES, P, D).transpose(1, 0, 2)
    cc = _np.zeros((P, KD, 32), _np.float32)
    cc[:, :, 0] = chan(I["c"][0])
    cc[:, :, 1] = chan(I["c_ctx"])
    arrays["ccol"] = cc.reshape(P, -1)
    const, fd, _ = constants()
    arrays["const"] = const
    cols = _np.zeros((P, DEPTH, NC), _np.float32)
    rows = _np.zeros((DEPTH, NR), _np.float32)
    hfw = _np.zeros((DEPTH, 64, HF_COLS), _np.float32)
    wr = _np.zeros((P, DEPTH, KD, 32), _np.float32)
    winc = _np.zeros((DEPTH, 14, P, WCH), _np.float32)
    wmod = _np.zeros((DEPTH, 12, P, WCH), _np.float32)
    wbr = _np.zeros((DEPTH, 4, P, 2 * D), _np.float32)
    wout = _np.zeros((DEPTH, 2, P, WCH), _np.float32)
    for l in range(DEPTH):
        q = cols[:, l]
        q[:, C_N1:C_N1 + 8] = chan(I["norm1_g"][l])
        q[:, C_N2:C_N2 + 8] = chan(I["norm2_g"][l])
        q[:, C_BMOD:C_BMOD + 48] = chan(I["b_mod"][l])
        q[:, C_BGATE:C_BGATE + 32] = chan(I["b_gate"][l])
        for k in range(3):
            q[:, C_HYW + 6 * k:C_HYW + 6 * k + 6] = chan(I["hy_conv_w"][l, k])
        q[:, C_HYB:C_HYB + 6] = chan(I["hy_conv_b"][l])
        q[:, C_HYBIAS:C_HYBIAS + 2] = chan(I["hy_bias"][l])
        for k in range(TAPS):
            q[:, C_CFW + 2 * k:C_CFW + 2 * k + 2] = chan(I["cf_dw_w"][l, k])
        q[:, C_CFB:C_CFB + 2] = chan(I["cf_dw_b"][l])
        q[:, C_LNG:C_LNG + 2] = chan(I["cf_ln_g"][l])
        q[:, C_LNB:C_LNB + 2] = chan(I["cf_ln_b"][l])
        for k, nme in enumerate(("hf_b1", "hf_b2", "hf_b3", "hf_freq")):
            q[0:64, C_HF + k] = I[nme][l]
        rows[l, R_QN:R_QN + 32] = I["da_qn"][l]
        rows[l, R_KN:R_KN + 32] = I["da_kn"][l]
        rows[l, R_WQ:R_WQ + 64] = I["wa_qn"][l]
        rows[l, R_WK:R_WK + 64] = I["wa_kn"][l]
        rows[l, R_SUB:R_SUB + 64] = I["da_subln"][l]
        rows[l, R_BR:R_BR + 4] = I["b_rg"][l]
        rows[l, R_BR + 4:R_BR + 20] = I["b_re"][l]
        rows[l, R_SINK:R_SINK + 4] = I["wa_sink"][l]
        rows[l, R_LAM:R_LAM + 128] = I["da_lam"][l].reshape(-1)
        hfw[l, 0:33, 0:64] = I["hf_w1"][l]
        hfw[l, :, 64:128] = I["hf_w2"][l]
        hfw[l, :, 128:192] = I["hf_w3"][l]
        hfw[l, :, 192:704] = I["hf_w4"][l]
        wr[:, l, :, 0:20] = _np.concatenate([I["w_rg"][l], I["w_re"][l]], 1).reshape(KD, P, 20).transpose(1, 0, 2)
        w = I["w_in"][l]
        wb, wc, wd, wg = w[:, 768:1536], w[:, 1536:2048], w[:, 2048:2560], w[:, 2560:]
        heads = [wc[:, 64 * h:64 * h + 64] for h in (0, 2, 1, 3)]
        wc = _np.concatenate([wc[:, 256:512]] + heads, 1)
        for i, piece in enumerate((wd, wb[:, 0:512], wb[:, 512:768], w[:, 0:256], w[:, 256:768], wc)):
            winc[l, i, :, 0:KD * piece.shape[1]] = tiles(piece)
        for i in range(8):
            winc[l, 6 + i] = tiles(wg[:, i * 512:(i + 1) * 512])
        for i in range(12):
            wmod[l, i] = tiles(I["w_mod"][l][:, i * 512:(i + 1) * 512])
        for i in range(4):
            wbr[l, i] = tiles(I["w_branch"][l, i])
        for i in range(2):
            wout[l, i] = tiles(I["w_out"][l][:, i * 512:(i + 1) * 512])
    arrays["cols"], arrays["hfw"] = cols, hfw
    arrays["rows"] = _np.broadcast_to(rows.reshape(1, -1), (P, DEPTH * NR))
    arrays["wr"], arrays["fdft"] = wr, fd
    arrays["wmod"], arrays["win"], arrays["wbr"], arrays["wout"] = wmod, winc, wbr, wout
    for nme in ("w1", "w3"):
        arrays[nme] = I[nme].reshape(DEPTH, NE, KD, P, FE).transpose(0, 1, 3, 2, 4).reshape(DEPTH, NE, P, WCH)
    arrays["w2"] = I["w2"].reshape(DEPTH, NE, 4, P, D).transpose(0, 1, 3, 2, 4).reshape(DEPTH, NE, P, WCH)
    arrays = {k: _np.ascontiguousarray(a) for k, a in arrays.items()}

    nc = _bacc.Bacc("TRN2", target_bir_lowering=False, num_devices=1)
    args = {k: nc.dram_tensor(k, a.shape, _mybir.dt.from_np(a.dtype), kind="ExternalInput").ap()
            for k, a in arrays.items()}
    args["out"] = nc.dram_tensor("out", (SEQ, D), F32, kind="ExternalOutput").ap()
    build_trunk(nc, **args)
    r = _run(nc, [arrays], core_ids=[0])
    return r.results[0]["out"].reshape(1, SEQ, D)
```
